# Optimizing a Trainium2 kernel written in Bass

```python
import math
import jax
import jax.numpy as jnp
from jax import lax
import numpy as np

D_MODEL = 1024
BATCH = 1
SEQ = 128
DEPTH = 2
DEC_BATCH = 1
DEC_SEQ = 1024
PAST_LEN = 128

GRID_W = 64
N_EVEN = (DEPTH + 1) // 2
N_ODD = DEPTH // 2
N_MOD = 6
RMS_EPS = 1e-6
HD_A = 64
H_A = D_MODEL // 2 // HD_A
D_A = H_A * HD_A
R_W = 64
R_A = 64
R_G = 128
RWKV_LN_EPS = 64e-5
HD_B = 128
H_B = D_MODEL // 2 // HD_B
D_B = H_B * HD_B
SHORT_CONV = 3
CHUNK = 64
SIZES_A = (D_A, D_A, D_A, 2 * R_W, 2 * R_A, R_G)
SIZES_B = (D_B, D_B, D_B, D_B, 2 * H_B, 2 * H_B)
P_A = sum(SIZES_A)
P_B = sum(SIZES_B)
DV_C = 128
DK_C = 64
H_C = D_MODEL // DV_C
D_CQK = H_C * DK_C
D_CV = H_C * DV_C
SIZES_C = (D_CQK, D_CQK, D_CV, D_CV, 4 * H_C)
P_C = sum(SIZES_C)
GATE_CAP = 15.0
D_FF = ((8 * D_MODEL // 3 + 127) // 128) * 128

kernel_name = 'bidir_rwkv7_gdn_mlstm_convffn_prefix_ctx'

F32 = jnp.float32

def rms_norm(x, g):
    xf = x.astype(F32)
    y = xf * lax.rsqrt(jnp.mean(xf * xf, axis=-1, keepdims=True) + RMS_EPS)
    return (y * g.astype(F32)).astype(x.dtype)

def l2norm(t, eps=1e-6):
    return t * lax.rsqrt(jnp.sum(t * t, axis=-1, keepdims=True) + eps)

def soft_cap(t):
    return GATE_CAP * jnp.tanh(t / GATE_CAP)

def split_cols(z, sizes):
    return jnp.split(z, np.cumsum(sizes)[:-1].tolist(), axis=-1)

def flip_time(ts):
    return tuple(jnp.flip(t, axis=1) for t in ts)

def centred_neighbour_mean(z):
    zp = jnp.pad(z, ((0, 0), (1, 1), (0, 0)))
    return 0.5 * (zp[:, :-2] + zp[:, 2:])

def dwconv_seq(z, w):
    half = w.shape[0] // 2
    return lax.conv_general_dilated(z, w[:, None, :], window_strides=(1,), padding=((half, half),),
                                    dimension_numbers=('NWC', 'WIO', 'NWC'),
                                    feature_group_count=z.shape[-1])

def dwconv_grid(z, w):
    b, n, ch = z.shape
    rows = n // GRID_W
    zi = z.reshape(b, rows, GRID_W, ch)
    out = lax.conv_general_dilated(zi, w[:, :, None, :], window_strides=(1, 1),
                                   padding=((1, 1), (1, 1)),
                                   dimension_numbers=('NHWC', 'HWIO', 'NHWC'),
                                   feature_group_count=ch)
    return out.reshape(b, n, ch)

def to_chunks(t):
    b, n, h = t.shape[:3]
    t = t.reshape(b, n // CHUNK, CHUNK, h, *t.shape[3:])
    return jnp.moveaxis(jnp.moveaxis(t, 3, 2), 1, 0)

def from_chunks(t):
    nc, b, h, l = t.shape[:4]
    t = jnp.moveaxis(jnp.moveaxis(t, 0, 1), 2, 3)
    return t.reshape(b, nc * l, h, *t.shape[4:])

def tri_solve(a, rhs):
    return lax.linalg.triangular_solve(a, rhs, left_side=True, lower=True, unit_diagonal=True)

def rwkv7_scan(r, w_log, k, v, kk, a, s0):
    def step(s, inp):
        r_t, wl_t, k_t, v_t, kk_t, a_t = inp
        s = (s * jnp.exp(wl_t)[:, :, None, :]
             - jnp.einsum('bhvk,bhk->bhv', s, kk_t)[..., None] * (kk_t * a_t)[:, :, None, :]
             + v_t[..., None] * k_t[:, :, None, :])
        return s, jnp.einsum('bhvk,bhk->bhv', s, r_t)
    xs = tuple(jnp.moveaxis(t, 1, 0) for t in (r, w_log, k, v, kk, a))
    s, y = lax.scan(step, s0, xs)
    return jnp.moveaxis(y, 0, 1), s

def gdn_chunked(q, k, v, beta, g, s0):
    qc, kc, vc, bc, gc = (to_chunks(t) for t in (q, k, v, beta, g))
    G = jnp.cumsum(gc, axis=-1)
    idx = jnp.arange(CHUNK)
    incl = idx[:, None] >= idx[None, :]
    strict = idx[:, None] > idx[None, :]
    decay = jnp.exp(jnp.where(incl, G[..., :, None] - G[..., None, :], -jnp.inf))
    beta_m = jnp.where(strict, decay * jnp.einsum('cbhtk,cbhik->cbhti', kc, kc), 0.0) * bc[..., None]
    lhs = jnp.eye(CHUNK, dtype=beta_m.dtype) + beta_m
    u = tri_solve(lhs, bc[..., None] * vc)
    w = tri_solve(lhs, (bc * jnp.exp(G))[..., None] * kc)
    a_qk = decay * jnp.einsum('cbhtk,cbhik->cbhti', qc, kc)
    q_dec = qc * jnp.exp(G)[..., None]
    k_dec = kc * jnp.exp(G[..., -1:] - G)[..., None]
    g_last = jnp.exp(G[..., -1])

    def step(s, inp):
        u_c, w_c, a_c, qd, kd, gl = inp
        delta = u_c - jnp.einsum('bhtk,bhvk->bhtv', w_c, s)
        o = jnp.einsum('bhtk,bhvk->bhtv', qd, s) + jnp.einsum('bhti,bhiv->bhtv', a_c, delta)
        s = gl[..., None, None] * s + jnp.einsum('bhtv,bhtk->bhvk', delta, kd)
        return s, o
    s, o = lax.scan(step, s0, (u, w, a_qk, q_dec, k_dec, g_last))
    return from_chunks(o), s

def mlstm_chunked(q, k, v, i_pre, log_f, c0, n0, m0):
    idx = jnp.arange(CHUNK)
    incl = idx[:, None] >= idx[None, :]

    def step(carry, inp):
        c, nv, m = carry
        qc, kc, vc, ic, fc = inp
        bcum = jnp.cumsum(fc, axis=-1)
        log_intra = jnp.where(incl, bcum[..., :, None] - bcum[..., None, :] + ic[..., None, :], -jnp.inf)
        log_inter = bcum + m[..., None]
        m_t = jnp.maximum(log_inter, jnp.max(log_intra, axis=-1))
        w_intra = jnp.exp(log_intra - m_t[..., None])
        w_inter = jnp.exp(log_inter - m_t)
        s = jnp.einsum('bhtk,bhik->bhti', qc, kc) * w_intra
        num = w_inter[..., None] * jnp.einsum('bhtk,bhvk->bhtv', qc, c) + jnp.einsum('bhti,bhiv->bhtv', s, vc)
        den = w_inter * jnp.einsum('bhtk,bhk->bht', qc, nv) + jnp.sum(s, axis=-1)
        h = num / jnp.maximum(jnp.abs(den), jnp.exp(-m_t))[..., None]
        w_end = w_intra[..., -1, :]
        c = w_inter[..., -1, None, None] * c + jnp.einsum('bhi,bhiv,bhik->bhvk', w_end, vc, kc)
        nv = w_inter[..., -1, None] * nv + jnp.einsum('bhi,bhik->bhk', w_end, kc)
        return (c, nv, m_t[..., -1]), h
    xs = tuple(to_chunks(t) for t in (q, k, v, i_pre, log_f))
    (c, nv, m), h = lax.scan(step, (c0, n0, m0), xs)
    return from_chunks(h), c, nv, m

def rwkv7_mixer(za, mu, w0, w_up, a0, a_up, g_up, k_k, k_a, r_k, ln_g, ln_b, s0):
    b, n, _ = za.shape
    heads = lambda t: t.astype(F32).reshape(b, n, H_A, HD_A)
    zs = za + mu * (centred_neighbour_mean(za) - za)
    r, k, v, wd, ad, gd = split_cols(zs, SIZES_A)
    r_h, v_h = heads(r), heads(v)
    kk = l2norm(heads(k * k_k), 1e-12)
    wd = wd.reshape(b, n, 2, R_W)
    ad = ad.reshape(b, n, 2, R_A)
    y, bonus, finals = 0.0, 0.0, []
    for d in range(2):
        w = -jax.nn.softplus(-(w0[d] + jnp.tanh(wd[:, :, d]) @ w_up[d])) - 0.5
        a = jax.nn.sigmoid(a0[d] + ad[:, :, d] @ a_up[d])
        k_d = heads(k * (1.0 + (a - 1.0) * k_a))
        seq = (r_h, -jnp.exp(heads(w)), k_d, v_h, kk, heads(a))
        if d == 1:
            seq = flip_time(seq)
        y_d, s_d = rwkv7_scan(*seq, s0[:, d].astype(F32))
        if d == 1:
            y_d = jnp.flip(y_d, axis=1)
        y = y + y_d
        bonus = bonus + jnp.sum(r_h * k_d * r_k, axis=-1, keepdims=True) * v_h
        finals.append(s_d)
    yc = y - jnp.mean(y, axis=-1, keepdims=True)
    y = (yc * lax.rsqrt(jnp.mean(yc * yc, axis=-1, keepdims=True) + RWKV_LN_EPS)).reshape(b, n, D_A)
    y = (y * ln_g + ln_b + bonus.reshape(b, n, D_A)) * (jax.nn.sigmoid(gd) @ g_up)
    return y.astype(za.dtype), jnp.stack(finals, axis=1)

def gdn_mixer(zb, conv_w, a_log, dt_bias, norm_g, s0):
    b, n, _ = zb.shape
    q, k, v, gate, alpha, beta = split_cols(zb, SIZES_B)
    qkv = jax.nn.silu(dwconv_seq(jnp.concatenate([q, k, v], axis=-1), conv_w)).astype(F32)
    q, k, v = jnp.split(qkv, 3, axis=-1)
    q = l2norm(q.reshape(b, n, H_B, HD_B)) * HD_B ** -0.5
    k = l2norm(k.reshape(b, n, H_B, HD_B))
    v = v.reshape(b, n, H_B, HD_B)
    alpha = alpha.astype(F32).reshape(b, n, 2, H_B)
    beta = beta.astype(F32).reshape(b, n, 2, H_B)
    o, finals = 0.0, []
    for d in range(2):
        g_d = -jnp.exp(a_log[d]) * jax.nn.softplus(alpha[:, :, d] + dt_bias[d])
        seq = (q, k, v, jax.nn.sigmoid(beta[:, :, d]), g_d)
        if d == 1:
            seq = flip_time(seq)
        o_d, s_d = gdn_chunked(*seq, s0[:, d].astype(F32))
        if d == 1:
            o_d = jnp.flip(o_d, axis=1)
        o = o + o_d
        finals.append(s_d)
    o = rms_norm(o, norm_g) * jax.nn.silu(gate.astype(F32)).reshape(b, n, H_B, HD_B)
    return o.reshape(b, n, D_B).astype(zb.dtype), jnp.stack(finals, axis=1)

def mlstm_mixer(zc, gate_b, norm_g, c0, n0, m0):
    b, n, _ = zc.shape
    q, k, v, o, gates = split_cols(zc, SIZES_C)
    q = q.astype(F32).reshape(b, n, H_C, DK_C)
    k = k.astype(F32).reshape(b, n, H_C, DK_C) * DK_C ** -0.5
    v = v.astype(F32).reshape(b, n, H_C, DV_C)
    gates = soft_cap(gates.astype(F32) + gate_b).reshape(b, n, 4, H_C)
    h, cs, ns, ms = 0.0, [], [], []
    for d in range(2):
        seq = (q, k, v, gates[:, :, d], jax.nn.log_sigmoid(gates[:, :, 2 + d]))
        if d == 1:
            seq = flip_time(seq)
        h_d, c_d, n_d, m_d = mlstm_chunked(*seq, c0[:, d].astype(F32), n0[:, d].astype(F32),
                                           m0[:, d].astype(F32))
        if d == 1:
            h_d = jnp.flip(h_d, axis=1)
        h = h + h_d
        cs.append(c_d)
        ns.append(n_d)
        ms.append(m_d)
    h = rms_norm(h, norm_g).reshape(b, n, D_CV) * jax.nn.sigmoid(o.astype(F32))
    return h.astype(zc.dtype), jnp.stack(cs, axis=1), jnp.stack(ns, axis=1), jnp.stack(ms, axis=1)

def conv_ffn(h, w_in, conv_w, conv_b, w_out, on_grid):
    u, gate = jnp.split(h @ w_in, 2, axis=-1)
    u = (dwconv_grid(u, conv_w) if on_grid else dwconv_seq(u, conv_w[1])) + conv_b
    return (jax.nn.silu(u) * gate) @ w_out

def adaln(cond, w, b):
    m = jax.nn.silu(cond) @ w + b
    return jnp.split(m[:, None, :], N_MOD, axis=-1)

def trunk(x, cond, states, on_grid, P):
    st_rk, st_gd, st_mc, st_mn, st_mm = states
    new_rk, new_gd, new_mc, new_mn, new_mm = [], [], [], [], []
    for layer in range(DEPTH):
        j = layer // 2
        sh1, sc1, g1, sh2, sc2, g2 = adaln(cond, P['ada_w'][layer], P['ada_b'][layer])
        h = rms_norm(x, P['norm1_g'][layer]) * (1.0 + sc1) + sh1
        if layer % 2 == 0:
            z = h @ P['ab_w_in'][j]
            ya, sa = rwkv7_mixer(z[..., :P_A], P['rk_mu'][j], P['rk_w0'][j], P['rk_w_up'][j],
                                 P['rk_a0'][j], P['rk_a_up'][j], P['rk_g_up'][j], P['rk_k_k'][j],
                                 P['rk_k_a'][j], P['rk_r_k'][j], P['rk_ln_g'][j], P['rk_ln_b'][j],
                                 st_rk[:, j])
            yb, sb = gdn_mixer(z[..., P_A:], P['gd_conv_w'][j], P['gd_a_log'][j], P['gd_dt_bias'][j],
                               P['gd_norm_g'][j], st_gd[:, j])
            y = jnp.concatenate([ya, yb], axis=-1) @ P['ab_w_out'][j]
            new_rk.append(sa)
            new_gd.append(sb)
        else:
            yc, c_f, n_f, m_f = mlstm_mixer(h @ P['ml_w_in'][j], P['ml_gate_b'][j], P['ml_norm_g'][j],
                                            st_mc[:, j], st_mn[:, j], st_mm[:, j])
            y = yc @ P['ml_w_out'][j]
            new_mc.append(c_f)
            new_mn.append(n_f)
            new_mm.append(m_f)
        x = x + g1 * y
        h = rms_norm(x, P['norm2_g'][layer]) * (1.0 + sc2) + sh2
        x = x + g2 * conv_ffn(h, P['ffn_w_in'][layer], P['ffn_conv_w'][layer], P['ffn_conv_b'][layer],
                              P['ffn_w_out'][layer], on_grid)
    new_states = tuple(jnp.stack(s, axis=1) for s in (new_rk, new_gd, new_mc, new_mn, new_mm))
    return rms_norm(x, P['final_g']), new_states

def setup_inputs(seed: int = 0) -> dict:
    key = jax.random.key(seed)
    keys = iter(jax.random.split(key, 48))
    nrm = lambda shape, scale: scale * jax.random.normal(next(keys), shape, F32)
    unif = lambda shape, lo, hi: jax.random.uniform(next(keys), shape, F32, lo, hi)
    D = D_MODEL
    dt = jnp.exp(unif((N_EVEN, 2, H_B), math.log(1e-3), math.log(1e-1)))
    return {
        'x_prompt': nrm((BATCH, SEQ, D), 1.0),
        'x_sample': nrm((DEC_BATCH, DEC_SEQ, D), 1.0),
        'state_rwkv': nrm((DEC_BATCH, N_EVEN, 2, H_A, HD_A, HD_A), 0.1),
        'state_gdn': nrm((DEC_BATCH, N_EVEN, 2, H_B, HD_B, HD_B), 0.1),
        'state_mlstm_c': nrm((DEC_BATCH, N_ODD, 2, H_C, DV_C, DK_C), 0.3),
        'state_mlstm_n': nrm((DEC_BATCH, N_ODD, 2, H_C, DK_C), 0.3),
        'state_mlstm_m': unif((DEC_BATCH, N_ODD, 2, H_C), 0.0, 3.0),
        'c': nrm((DEC_BATCH, D), 1.0),
        'c_ctx': nrm((D,), 1.0),
        'ada_w': nrm((DEPTH, D, N_MOD * D), 0.5 * D ** -0.5),
        'ada_b': nrm((DEPTH, N_MOD * D), 0.01),
        'norm1_g': 1.0 + nrm((DEPTH, D), 0.02),
        'norm2_g': 1.0 + nrm((DEPTH, D), 0.02),
        'ab_w_in': nrm((N_EVEN, D, P_A + P_B), D ** -0.5),
        'ab_w_out': nrm((N_EVEN, D_A + D_B, D), (D_A + D_B) ** -0.5),
        'rk_mu': unif((N_EVEN, P_A), 0.0, 1.0),
        'rk_w0': unif((N_EVEN, 2, D_A), -4.0, 2.0),
        'rk_w_up': nrm((N_EVEN, 2, R_W, D_A), 0.1 * R_W ** -0.5),
        'rk_a0': nrm((N_EVEN, 2, D_A), 0.1),
        'rk_a_up': nrm((N_EVEN, 2, R_A, D_A), 0.1 * R_A ** -0.5),
        'rk_g_up': nrm((N_EVEN, R_G, D_A), R_G ** -0.5),
        'rk_k_k': 0.85 + nrm((N_EVEN, D_A), 0.05),
        'rk_k_a': 1.0 + nrm((N_EVEN, D_A), 0.05),
        'rk_r_k': nrm((N_EVEN, H_A, HD_A), 0.1),
        'rk_ln_g': 1.0 + nrm((N_EVEN, D_A), 0.02),
        'rk_ln_b': nrm((N_EVEN, D_A), 0.01),
        'gd_conv_w': nrm((N_EVEN, SHORT_CONV, 3 * D_B), SHORT_CONV ** -0.5),
        'gd_a_log': jnp.log(unif((N_EVEN, 2, H_B), 1.0, 16.0)),
        'gd_dt_bias': dt + jnp.log(-jnp.expm1(-dt)),
        'gd_norm_g': 1.0 + nrm((N_EVEN, HD_B), 0.02),
        'ml_w_in': nrm((N_ODD, D, P_C), D ** -0.5),
        'ml_gate_b': jnp.concatenate([nrm((N_ODD, 2 * H_C), 0.1), unif((N_ODD, 2 * H_C), 3.0, 6.0)], axis=-1),
        'ml_norm_g': 1.0 + nrm((N_ODD, DV_C), 0.02),
        'ml_w_out': nrm((N_ODD, D_CV, D), D_CV ** -0.5),
        'ffn_w_in': nrm((DEPTH, D, 2 * D_FF), D ** -0.5),
        'ffn_conv_w': nrm((DEPTH, 3, 3, D_FF), 1.0 / 3.0),
        'ffn_conv_b': nrm((DEPTH, D_FF), 0.01),
        'ffn_w_out': nrm((DEPTH, D_FF, D), D_FF ** -0.5),
        'final_g': 1.0 + nrm((D,), 0.02),
    }

def reference(x_prompt, x_sample, state_rwkv, state_gdn, state_mlstm_c, state_mlstm_n, state_mlstm_m,
              c, c_ctx, ada_w, ada_b, norm1_g, norm2_g, ab_w_in, ab_w_out, rk_mu, rk_w0, rk_w_up,
              rk_a0, rk_a_up, rk_g_up, rk_k_k, rk_k_a, rk_r_k, rk_ln_g, rk_ln_b, gd_conv_w, gd_a_log,
              gd_dt_bias, gd_norm_g, ml_w_in, ml_gate_b, ml_norm_g, ml_w_out, ffn_w_in, ffn_conv_w,
              ffn_conv_b, ffn_w_out, final_g):
    P = dict(ada_w=ada_w, ada_b=ada_b, norm1_g=norm1_g, norm2_g=norm2_g, ab_w_in=ab_w_in,
             ab_w_out=ab_w_out, rk_mu=rk_mu, rk_w0=rk_w0, rk_w_up=rk_w_up, rk_a0=rk_a0,
             rk_a_up=rk_a_up, rk_g_up=rk_g_up, rk_k_k=rk_k_k, rk_k_a=rk_k_a, rk_r_k=rk_r_k,
             rk_ln_g=rk_ln_g, rk_ln_b=rk_ln_b, gd_conv_w=gd_conv_w, gd_a_log=gd_a_log,
             gd_dt_bias=gd_dt_bias, gd_norm_g=gd_norm_g, ml_w_in=ml_w_in, ml_gate_b=ml_gate_b,
             ml_norm_g=ml_norm_g, ml_w_out=ml_w_out, ffn_w_in=ffn_w_in, ffn_conv_w=ffn_conv_w,
             ffn_conv_b=ffn_conv_b, ffn_w_out=ffn_w_out, final_g=final_g)
    cache = (state_rwkv, state_gdn, state_mlstm_c, state_mlstm_n, state_mlstm_m)
    ctx_init = tuple(jnp.zeros((x_prompt.shape[0],) + s.shape[1:], F32) for s in cache)
    y_prompt, (rk, gd, mc, mn, mm) = trunk(x_prompt, c_ctx[None, :], ctx_init, False, P)
    y_sample, _ = trunk(x_sample, c, cache, True, P)
    return (y_prompt, y_sample, rk, gd, mc, mn, mm)


_drawn_inputs = setup_inputs


def setup_inputs(seed=0):
    import zlib

    import numpy as np

    out = dict(_drawn_inputs(seed))
    spreads = {}
    factors = {'state_rwkv': 8.0,
     'state_gdn': 4.976,
     'state_mlstm_n': 4.31,
     'state_mlstm_m': 4.941,
     'norm2_g': 6.982,
     'rk_w_up': 4.551,
     'rk_ln_g': 8.0,
     'rk_ln_b': 42.506,
     'gd_norm_g': 8.0,
     'ml_norm_g': 64.0,
     'ffn_conv_b': 8.0,
     'final_g': 7.451}
    for name, (base, spread) in spreads.items():
        noise = np.random.default_rng([zlib.crc32(name.encode()), seed]).standard_normal(out[name].shape)
        drawn = base * np.exp(spread * noise) if base else spread * noise
        out[name] = jnp.asarray(drawn.astype(out[name].dtype))
    for name, factor in factors.items():
        out[name] = (out[name] * factor).astype(out[name].dtype)
    return out
```

```python
from contextlib import ExitStack, contextmanager

import numpy as np
import concourse.bass as bass
import concourse.mybir as mybir

F32 = mybir.dt.float32
ACT = mybir.ActivationFunctionType
ALU = mybir.AluOpType
AX_X = mybir.AxisListType.X

P = 128
D = 1024
KD = D // P
CTX = 128
LAT = 1024
T = CTX + LAT
NCH = T // P
GRID = 64
ROWS = LAT // GRID
HD_A, H_A = 64, 8
HD_B, H_B = 128, 4
DK_C, DV_C, H_C = 64, 128, 8
PA_T = 15
PB_T = 16
QKV_T = 12
AB_T = PA_T + PB_T
ML_T = 24
DFF = 2816
FT = DFF // P
RMS_EPS = 1e-6
RWKV_LN_EPS = 64e-5
GATE_CAP = 15.0
LEVELS = [1, 2, 4, 8, 16, 32, 64]
EXP_HALF = float(np.exp(-0.5))

C_ADAB, C_N1, C_N2 = 0, 96, 112
C_FIN, C_MU, C_W0, C_A0, C_KK, C_KA, C_RK, C_LNG, C_LNB, C_CONV, C_GDN, C_MLN = (
    128, 136, 151, 159, 167, 171, 175, 179, 183, 187, 223, 224)
C_FFW, C_FFB = 256, 256 + 2 * 9 * FT
PT_COLS = 6 * P


@contextmanager
def phase(nc, *names):
    sems = {n: nc.alloc_semaphore(f"{n}_{nc.next_id()}") for n in names}
    yield sems
    nc.clear_and_free_semaphores(list(sems.values()))
    nc.all_engine_barrier()


def early(eng, *aps):
    for ap in aps:
        if not isinstance(ap.offset, int):
            eng.lower_val(ap.offset * 4)


def chain(eng, sem):
    n = [0]

    def link(ins):
        n[0] += 1
        ins.then_inc(sem, 1)
        eng.wait_ge(sem, n[0])
    return link


def sbuf(ctx, nc, name, shape):
    return ctx.enter_context(nc.sbuf_tensor(f"{name}_{nc.next_id()}", shape, F32))


def psum(ctx, nc, name, shape):
    return ctx.enter_context(nc.psum_tensor(f"{name}_{nc.next_id()}", shape, F32))


def setup_phase(nc, A, K):
    with ExitStack() as ctx:
        rows = sbuf(ctx, nc, "param_rows", [P, 6, P])
        crow = sbuf(ctx, nc, "cond_rows", [16, P])
        xt = sbuf(ctx, nc, "x_tokens", [P, 3, D])
        pp = psum(ctx, nc, "params_ps", [P, 2, 512])
        pc = psum(ctx, nc, "cond_ps", [P, 512])
        px = psum(ctx, nc, "x_ps", [P, 2, D])
        rowsum = [
            (0, 0, A["ada_b"].rearrange("l (n c) -> (l n) c", c=P)),
            (0, C_N1, A["norm1_g"].rearrange("l (n c) -> (l n) c", c=P)),
            (0, C_N2, A["norm2_g"].rearrange("l (n c) -> (l n) c", c=P)),
            (1, C_FIN, A["final_g"].rearrange("(n c) -> n c", c=P)),
            (1, C_MU, A["rk_mu"].rearrange("l (n c) -> (l n) c", c=P)),
            (1, C_W0, A["rk_w0"].rearrange("l d (n c) -> (l d n) c", c=P)),
            (1, C_A0, A["rk_a0"].rearrange("l d (n c) -> (l d n) c", c=P)),
            (1, C_KK, A["rk_k_k"].rearrange("l (n c) -> (l n) c", c=P)),
            (1, C_KA, A["rk_k_a"].rearrange("l (n c) -> (l n) c", c=P)),
            (1, C_RK, A["rk_r_k"].rearrange("l (n a) c -> (l n) (a c)", a=2)),
            (1, C_LNG, A["rk_ln_g"].rearrange("l (n c) -> (l n) c", c=P)),
            (1, C_LNB, A["rk_ln_b"].rearrange("l (n c) -> (l n) c", c=P)),
            (1, C_CONV, A["gd_conv_w"].rearrange("l t (n c) -> (l t n) c", c=P)),
            (1, C_GDN, A["gd_norm_g"]),
            (1, C_MLN, A["ml_norm_g"]),
        ]
        ffw = A["ffn_conv_w"].rearrange("l a b (n c) -> (l a b n) c", c=P)
        ffb = A["ffn_conv_b"].rearrange("l (n c) -> (l n) c", c=P)
        nw = ffw.shape[0]
        for g in range(4):
            a, b = g * P, min(g * P + P, nw)
            rowsum.append((2 + g, C_FFW + a, ffw[a:b, :]))
        rowsum.append((5, C_FFB, ffb))
        xs = A["x_sample"].rearrange("b (n p) c -> (b n) p c", p=P)
        xp = A["x_prompt"].rearrange("b p c -> (b p) c")
        with phase(nc, "rows_in", "cond_in", "x_in0", "x_in1", "x_in2", "consts", "pool_chain", "turned",
                   "table", "cond_turned", "cond_silu", "x_turned0", "x_turned1", "x_out0", "x_out1",
                   "dve_chain", "zeroed") as s:
            x_in = [s["x_in0"], s["x_in1"], s["x_in2"]]
            x_turned = [s["x_turned0"], s["x_turned1"]]
            x_out = [s["x_out0"], s["x_out1"]]
            with nc.Block() as block:
                @block.sync
                def _(sp):
                    sp.wait_ge(s["zeroed"], 1)
                    for g, col, src in rowsum:
                        r = col - g * P
                        sp.dma_start(rows[r:r + src.shape[0], g, :], src).then_inc(s["rows_in"], 16)
                    sp.dma_start(crow[0:8, :], A["c_ctx"].rearrange("(k c) -> k c", c=P)).then_inc(s["cond_in"], 16)
                    sp.dma_start(crow[8:16, :], A["c"].rearrange("b (k c) -> (b k) c", c=P)).then_inc(s["cond_in"], 16)
                    sp.dma_start(xt[:, 2, :], xp).then_inc(x_in[2], 16)
                    with sp.Fori(0, 4) as j:
                        early(sp, xs[2 * j], xs[2 * j + 1])
                        for k in range(2):
                            sp.wait_ge(x_turned[k], j)
                            sp.dma_start(xt[:, k, :], xs[2 * j + k]).then_inc(x_in[k], 16)

                @block.gpsimd
                def _(pool):
                    link = chain(pool, s["pool_chain"])
                    link(pool.memset(K["ident"][:], 0.0))
                    link(pool.affine_select(out=K["ident"][:], in_=K["ident"][:], compare_op=ALU.not_equal, fill=1.0,
                                            base=0, pattern=[[-1, P]], channel_multiplier=1))
                    pool.nop().then_inc(s["consts"], 1)
                    link(pool.memset(K["ones"][:], 1.0))
                    link(pool.memset(K["ones64"][:], 1.0))
                    for lo, hi, cm, step, base in ((0, 64, -1, 0, 63), (64, 128, 1, 0, -64)):
                        link(pool.affine_select(out=K["ones64"][:, lo:hi], in_=K["ones64"][:, lo:hi],
                                                compare_op=ALU.is_ge, fill=0.0, base=base, pattern=[[0, 64]],
                                                channel_multiplier=cm))
                    link(pool.memset(K["order"][:], 1.0))
                    for d in range(2):
                        sg = 1 - 2 * d
                        for q, op in ((0, ALU.is_gt), (1, ALU.is_ge)):
                            v = K["order"][:, d, q, :]
                            link(pool.affine_select(out=v, in_=v, compare_op=op, fill=0.0, base=0,
                                                    pattern=[[sg, P]], channel_multiplier=-sg))
                    link(pool.memset(K["pairs"][:], 1.0))
                    for n, b in enumerate(LEVELS):
                        nb = P // (2 * b)
                        for d in range(2):
                            v = K["pairs"][:, n, d, :].rearrange("p (x y) -> p x y", x=nb)
                            lo, hi = (0, b - 1) if d == 0 else (b, 2 * b - 1)
                            for base, pat, cm in ((-lo, [[-2 * b, nb], [0, 2 * b]], 1),
                                                  (hi, [[2 * b, nb], [0, 2 * b]], -1),
                                                  (-b, [[0, nb], [1, 2 * b]], 0) if d == 0 else
                                                  (b - 1, [[0, nb], [-1, 2 * b]], 0)):
                                link(pool.affine_select(out=v, in_=v, compare_op=ALU.is_ge, fill=0.0, base=base,
                                                        pattern=pat, channel_multiplier=cm))
                    link(pool.memset(K["sel"][:], 0.0))
                    link(pool.affine_select(out=K["sel"][:], in_=K["sel"][:], compare_op=ALU.not_equal, fill=1.0,
                                            base=0, pattern=[[-1, 8], [0, P]], channel_multiplier=1))
                    link(pool.memset(K["selpair"][:], 0.0))
                    v = K["selpair"][:].rearrange("p a (b c) -> p a b c", b=2)
                    link(pool.affine_select(out=v, in_=v, compare_op=ALU.not_equal, fill=1.0, base=0,
                                            pattern=[[-2, 4], [-1, 2], [0, 64]], channel_multiplier=1))

                @block.tensor
                def _(pe):
                    pe.wait_ge(s["consts"], 1)
                    pe.wait_ge(s["cond_in"], 32)
                    pe.transpose(pc[:, 0:16], crow[:, :], K["ident"][0:16, 0:16]).then_inc(s["cond_turned"], 1)
                    pe.wait_ge(s["rows_in"], 16 * len(rowsum))
                    for g in range(6):
                        pe.transpose(pp[:, g // 4, g % 4 * P:g % 4 * P + P], rows[:, g, :],
                                     K["ident"][:]).then_inc(s["turned"], 1)

                    def tile(k, slot, bank, first):
                        if not first:
                            pe.wait_ge(x_out[bank], k)
                        for c in range(KD):
                            mm = pe.transpose(px[:, bank, c * P:c * P + P], xt[:, slot, c * P:c * P + P], K["ident"][:])
                        mm.then_inc(x_turned[bank], 1)
                    with pe.Fori(0, 4) as j:
                        for k in range(2):
                            pe.wait_ge(x_in[k], j * 16 + 16)
                            tile(j, k, k, False)
                    pe.wait_ge(x_in[2], 16)
                    tile(4, 2, 0, False)

                @block.scalar
                def _(act):
                    act.wait_ge(s["cond_turned"], 1)
                    act.activation(K["cond"][:].rearrange("p k n -> p n k"),
                                   pc[:, 0:16].rearrange("p (n k) -> p n k", n=2), ACT.Silu).then_inc(s["cond_silu"], 1)
                    with act.Fori(0, 4) as j:
                        for k in range(2):
                            act.wait_ge(x_turned[k], j + 1)
                            act.activation(K["XT"][:, :, bass.ds((2 * j + (k + 1)) * P, P)],
                                           px[:, k, :].rearrange("p (c t) -> p c t", c=KD),
                                           ACT.Copy).then_inc(x_out[k], 1)
                    act.wait_ge(x_turned[0], 5)
                    act.activation(K["XT"][:, :, 0:P], px[:, 0, :].rearrange("p (c t) -> p c t", c=KD),
                                   ACT.Copy).then_inc(x_out[0], 1)

                @block.vector
                def _(dve):
                    link = chain(dve, s["dve_chain"])
                    dve.memset(rows[:], 0.0).then_inc(s["zeroed"], 1)
                    dve.wait_ge(s["turned"], 6)
                    PT = K["PT"]
                    link(dve.tensor_copy(PT[:, 0:512], pp[:, 0, :]))
                    link(dve.tensor_copy(PT[:, 512:768], pp[:, 1, 0:256]))
                    taps = K["taps"]
                    mu = PT[:, C_MU:C_MU + PA_T]
                    for t in (0, 2):
                        link(dve.tensor_scalar(taps[:, 0:PA_T, t], mu, 0.5, None, ALU.mult))
                    link(dve.tensor_scalar(taps[:, 0:PA_T, 1], mu, -1.0, 1.0, ALU.mult, ALU.add))
                    link(dve.tensor_copy(taps[:, PA_T:PA_T + QKV_T, :],
                                         PT[:, C_CONV:C_CONV + 36].rearrange("p (t n) -> p n t", t=3)))
                    link(dve.memset(taps[:, PA_T + QKV_T:AB_T, :], 0.0))
                    link(dve.memset(taps[:, PA_T + QKV_T:AB_T, 1:2], 1.0))


def adaln_phase(nc, A, K):
    with ExitStack() as ctx:
        W = sbuf(ctx, nc, "ada_w", [P, 2, KD, 4 * P])
        ps = psum(ctx, nc, "ada_ps", [P, 2, 512])
        w_src = A["ada_w"].rearrange("l (k p) (n c) -> l n p k c", p=P, c=4 * P)
        n12 = 12
        mod = K["mod"]
        flat = mod[:].rearrange("p l g k n -> p (l g k n)")
        bias = K["PT"][:, C_ADAB:C_ADAB + 96]
        with phase(nc, "w_in0", "w_in1", "mm0", "mm1", "out0", "out1", "dve_chain") as s:
            w_in, mm_done, out = [[s[n + "0"], s[n + "1"]] for n in ("w_in", "mm", "out")]
            with nc.Block() as block:
                @block.sync
                def _(sp):
                    for l in range(2):
                        with sp.Fori(0, n12 // 2) as j:
                            early(sp, w_src[l, 2 * j], w_src[l, 2 * j + 1])
                            sp.lower_val(j + l * (n12 // 2))
                            for k in range(2):
                                sp.wait_ge(mm_done[k], j + l * (n12 // 2))
                                sp.dma_start(W[:, k], w_src[l, 2 * j + k]).then_inc(w_in[k], 16)

                @block.tensor
                def _(pe):
                    with pe.Fori(0, n12) as j:
                        for k in range(2):
                            pe.wait_ge(w_in[k], j * 16 + 16)
                            pe.wait_ge(out[k], j)
                            for m in range(4):
                                for c in range(KD):
                                    mm = pe.matmul(ps[:, k, 2 * m:2 * m + 2], W[:, k, c, m * P:m * P + P],
                                                   K["cond"][:, c, :], start=(c == 0), stop=(c == KD - 1))
                            mm.then_inc(mm_done[k], 1)

                @block.vector
                def _(dve):
                    with dve.Fori(0, n12) as j:
                        for k in range(2):
                            dve.wait_ge(mm_done[k], j + 1)
                            dve.tensor_copy(flat[:, bass.ds(16 * j + 8 * k, 8)], ps[:, k, 0:8]).then_inc(out[k], 1)
                    link = chain(dve, s["dve_chain"])
                    dve.wait_ge(out[0], n12)
                    dve.wait_ge(out[1], n12)
                    for n in range(2):
                        v = mod[:, :, :, :, n].rearrange("p l g k -> p (l g k)")
                        link(dve.tensor_tensor(v, v, bias, ALU.add))
                    for l in range(2):
                        for w, (g, col) in enumerate(((1, C_N1), (4, C_N2))):
                            for n in range(2):
                                link(dve.tensor_scalar(K["gain"][:, l, w, :, n], mod[:, l, g, :, n], 1.0, None, ALU.add))
                                link(dve.tensor_tensor(K["gain"][:, l, w, :, n], K["gain"][:, l, w, :, n],
                                                       K["PT"][:, col + 8 * l:col + 8 * l + 8], ALU.mult))


def norm_phase(nc, K, dst, gain, shift):
    XT = K["XT"]
    with ExitStack() as ctx:
        sq = sbuf(ctx, nc, "squares", [P, 2, T])
        rstd = sbuf(ctx, nc, "rstd", [P, T])
        eps = sbuf(ctx, nc, "norm_eps", [P, 1])
        ps = psum(ctx, nc, "sum_ps", [P, 3, 512])
        with phase(nc, "squared", "summed", "root", "inv", "scaled", "eps_set", "done") as s:
            with nc.Block() as block:
                @block.scalar
                def _(act):
                    for k in range(KD):
                        if k >= 2:
                            act.wait_ge(s["summed"], k - 1)
                        act.activation(sq[:, k % 2, :], XT[:, k, :], ACT.Square).then_inc(s["squared"], 1)
                    act.wait_ge(s["summed"], KD)
                    act.wait_ge(s["eps_set"], 1)
                    act.activation(rstd[:, 0:CTX], ps[:, 0, 0:CTX], ACT.Sqrt, bias=eps[:], scale=1.0 / D).then_inc(s["root"], 1)
                    act.activation(rstd[:, CTX:T], ps[:, 1:3, :].rearrange("p a b -> p (a b)"), ACT.Sqrt,
                                   bias=eps[:], scale=1.0 / D).then_inc(s["root"], 1)
                    if shift is not None:
                        for k in range(KD):
                            for n, (a, b) in enumerate(((0, CTX), (CTX, T))):
                                act.wait_ge(s["scaled"], 2 * k + n + 1)
                                act.activation(dst[:, k, a:b], dst[:, k, a:b], ACT.Identity,
                                               bias=shift[:, k, n:n + 1]).then_inc(s["done"], 1)

                @block.tensor
                def _(pe):
                    for k in range(KD):
                        pe.wait_ge(s["squared"], k + 1)
                        for b, (x, y) in enumerate(((0, 128), (128, 640), (640, 1152))):
                            mm = pe.matmul(ps[:, b, 0:y - x], K["ones"][:], sq[:, k % 2, x:y],
                                           start=(k == 0), stop=(k == KD - 1))
                        mm.then_inc(s["summed"], 1)

                @block.vector
                def _(dve):
                    dve.memset(eps[:], RMS_EPS).then_inc(s["eps_set"], 1)
                    dve.wait_ge(s["root"], 2)
                    dve.reciprocal(rstd[:], rstd[:]).then_inc(s["inv"], 1)
                    dve.wait_ge(s["inv"], 1)
                    for k in range(KD):
                        for n, (a, b) in enumerate(((0, CTX), (CTX, T))):
                            dve.scalar_tensor_tensor(out=dst[:, k, a:b], in0=XT[:, k, a:b], scalar=gain[:, k, n:n + 1],
                                                     in1=rstd[:, a:b], op0=ALU.mult, op1=ALU.mult).then_inc(s["scaled"], 1)


def matmul_tile(pe, ps, W, rhs, kt):
    for k in range(kt):
        for b, (x, y) in enumerate(((0, 128), (128, 640), (640, 1152))):
            mm = pe.matmul(ps[:, b, 0:y - x], W[:, k, :], rhs[:, k, x:y], start=(k == 0), stop=(k == kt - 1))
    return mm


def lat(ps):
    return ps[:, 1:3, :].rearrange("p a b -> p (a b)")


def mixer_in_phase(nc, K, w, tiles, tail, zc, ztail, taps):
    HT = K["HT"]
    with ExitStack() as ctx:
        W = sbuf(ctx, nc, "in_w", [P, 2, KD, P])
        Wt = sbuf(ctx, nc, "tail_w", [P, KD, tail])
        z = sbuf(ctx, nc, "z_tile", [P, 2, T])
        tp = sbuf(ctx, nc, "tile_taps", [P, 2, 3])
        ps = psum(ctx, nc, "in_ps", [P, 2, 3, 512])
        w_src = w[:, 0:tiles * P].rearrange("(k p) (m c) -> m p k c", p=P, c=P)
        with phase(nc, "w_in0", "w_in1", "tail_in", "mm0", "mm1", "taps0", "taps1", "mid0", "mid1", "mid_ctx0", "mid_ctx1",
                   "part0", "part1", "z0", "z1", "stored0", "stored1", "tail_out", "tail_st") as s:
            w_in, mm_done, taps_ok, mid, part, z_ok, stored = [
                [s[n + "0"], s[n + "1"]] for n in ("w_in", "mm", "taps", "mid", "part", "z", "stored")]
            pairs, odd = tiles // 2, tiles % 2
            with nc.Block() as block:
                @block.sync
                def _(sp):
                    sp.dma_start(Wt[:], w[:, tiles * P:tiles * P + tail].rearrange("(k p) c -> p k c", p=P)).then_inc(s["tail_in"], 16)

                    def load(j, k):
                        sp.wait_ge(mm_done[k], j)
                        sp.dma_start(W[:, k], w_src[2 * j + k]).then_inc(w_in[k], 16)
                    with sp.Fori(0, pairs) as j:
                        early(sp, w_src[2 * j], w_src[2 * j + 1])
                        for k in range(2):
                            load(j, k)
                    if odd:
                        load(pairs, 0)

                @block.tensor
                def _(pe):
                    def tile(j, k):
                        pe.wait_ge(w_in[k], j * 16 + 16)
                        pe.wait_ge(z_ok[k], j)
                        matmul_tile(pe, ps[:, k], W[:, k], HT, KD).then_inc(mm_done[k], 1)
                    with pe.Fori(0, pairs) as j:
                        for k in range(2):
                            tile(j, k)
                    if odd:
                        tile(pairs, 0)
                    pe.wait_ge(s["tail_in"], 16)
                    pe.wait_ge(z_ok[odd], pairs)
                    matmul_tile(pe, ps[0:tail, odd], Wt[:], HT, KD).then_inc(mm_done[odd], 1)

                @block.scalar
                def _(act):
                    def tile(j, k):
                        act.wait_ge(mm_done[k], j + 1)
                        act.wait_ge(stored[k], j * 16)
                        if taps is not None:
                            act.wait_ge(taps_ok[k], j + 1)
                            act.activation(z[:, k, 0:CTX], ps[:, k, 0, 0:CTX], ACT.Copy,
                                           scale=tp[:, k, 1:2]).then_inc(s["mid_ctx%d" % k], 1)
                            act.activation(z[:, k, CTX:T], lat(ps[:, k]), ACT.Copy,
                                           scale=tp[:, k, 1:2]).then_inc(mid[k], 1)
                        else:
                            act.activation(z[:, k, 0:CTX], ps[:, k, 0, 0:CTX], ACT.Copy).then_inc(mid[k], 1)
                            act.activation(z[:, k, CTX:T], lat(ps[:, k]), ACT.Copy).then_inc(z_ok[k], 1)
                    with act.Fori(0, pairs) as j:
                        for k in range(2):
                            tile(j, k)
                    if odd:
                        tile(pairs, 0)
                    act.wait_ge(mm_done[odd], pairs + 1)
                    act.wait_ge(stored[odd], pairs * 16)
                    act.activation(z[0:tail, odd, 0:CTX], ps[0:tail, odd, 0, 0:CTX], ACT.Copy).then_inc(s["tail_out"], 1)
                    act.activation(z[0:tail, odd, CTX:T], lat(ps[0:tail, odd]), ACT.Copy).then_inc(s["tail_out"], 1)

                if taps is not None:
                    @block.vector
                    def _(dve):
                        def tile(j, k):
                            dve.wait_ge(z_ok[k], j)
                            dve.tensor_copy(tp[:, k, :], taps[:, 2 * j + k, :]).then_inc(taps_ok[k], 1)
                            c, l = ps[:, k, 0, 0:CTX], lat(ps[:, k])
                            dve.wait_ge(taps_ok[k], j + 1)
                            dve.wait_ge(s["mid_ctx%d" % k], j + 1)
                            dve.wait_ge(mid[k], j + 1)

                            def add(o, i, t):
                                return dve.scalar_tensor_tensor(out=o, in0=i, scalar=tp[:, k, t:t + 1], in1=o,
                                                                op0=ALU.mult, op1=ALU.add)
                            add(z[:, k, 1:CTX], c[:, 0:CTX - 1], 0).then_inc(part[k], 1)
                            add(z[:, k, CTX + 1:T], l[:, 0:LAT - 1], 0).then_inc(part[k], 1)
                            dve.wait_ge(part[k], j * 3 + 1)
                            add(z[:, k, 0:CTX - 1], c[:, 1:CTX], 2).then_inc(part[k], 1)
                            dve.wait_ge(part[k], j * 3 + 3)
                            add(z[:, k, CTX:T - 1], l[:, 1:LAT], 2).then_inc(z_ok[k], 1)
                        with dve.Fori(0, pairs) as j:
                            for k in range(2):
                                tile(j, k)
                        if odd:
                            tile(pairs, 0)

                @block.gpsimd
                def _(pool):
                    def store(j, k):
                        pool.wait_ge(z_ok[k], j + 1)
                        if taps is None:
                            pool.wait_ge(mid[k], j + 1)
                        pool.dma_start(zc[2 * j + k], z[:, k, :]).then_inc(stored[k], 16)
                    with pool.Fori(0, pairs) as j:
                        for k in range(2):
                            store(j, k)
                    if odd:
                        store(pairs, 0)
                    pool.wait_ge(s["tail_out"], 2)
                    pool.dma_start(ztail, z[0:tail, odd, :]).then_inc(s["tail_st"], 16)
                    pool.wait_ge(s["tail_st"], 16)
                    pool.wait_ge(stored[0], (pairs + odd) * 16)
                    pool.wait_ge(stored[1], pairs * 16)


def add_out_phase(nc, K, w, src, kt, gate):
    XT = K["XT"]
    with ExitStack() as ctx:
        W = sbuf(ctx, nc, "out_w", [P, 2, kt, P])
        g = sbuf(ctx, nc, "tile_gate", [P, 2, 2])
        ps = psum(ctx, nc, "out_ps", [P, 2, 3, 512])
        w_src = w.rearrange("(k p) (m c) -> m p k c", p=P, c=P)
        with phase(nc, "w_in0", "w_in1", "mm0", "mm1", "gate0", "gate1", "added0", "added1") as s:
            w_in, mm_done, gate_ok, added = [[s[n + "0"], s[n + "1"]] for n in ("w_in", "mm", "gate", "added")]
            with nc.Block() as block:
                @block.sync
                def _(sp):
                    with sp.Fori(0, KD // 2) as j:
                        early(sp, w_src[2 * j], w_src[2 * j + 1])
                        for k in range(2):
                            sp.wait_ge(mm_done[k], j)
                            sp.dma_start(W[:, k], w_src[2 * j + k]).then_inc(w_in[k], 16)

                @block.tensor
                def _(pe):
                    with pe.Fori(0, KD // 2) as j:
                        for k in range(2):
                            pe.wait_ge(w_in[k], j * 16 + 16)
                            pe.wait_ge(added[k], j * 2)
                            matmul_tile(pe, ps[:, k], W[:, k], src, kt).then_inc(mm_done[k], 1)

                @block.vector
                def _(dve):
                    with dve.Fori(0, KD // 2) as j:
                        for k in range(2):
                            dve.wait_ge(added[k], j * 2)
                            dve.tensor_copy(g[:, k, :], gate[:, 2 * j + k, :]).then_inc(gate_ok[k], 1)
                            dve.wait_ge(gate_ok[k], j + 1)
                            dve.wait_ge(mm_done[k], j + 1)
                            for n, (a, b, p) in enumerate(((0, CTX, ps[:, k, 0, 0:CTX]), (CTX, T, lat(ps[:, k])))):
                                x = XT[:, 2 * j + k, a:b]
                                dve.scalar_tensor_tensor(out=x, in0=p, scalar=g[:, k, n:n + 1], in1=x,
                                                         op0=ALU.mult, op1=ALU.add).then_inc(added[k], 1)


def ffn_in_phase(nc, A, K, layer):
    HT, PT, G = K["HT"], K["PT"], K["G"]
    ffw = PT[:, C_FFW + layer * 9 * FT:C_FFW + (layer + 1) * 9 * FT].rearrange("p (t m) -> p t m", t=9)
    ffb = PT[:, C_FFB + layer * FT:C_FFB + (layer + 1) * FT]
    w_src = A["ffn_w_in"][layer].rearrange("(k p) (h m c) -> h m p k c", p=P, h=2, c=P)
    with ExitStack() as ctx:
        W = sbuf(ctx, nc, "ffn_w", [P, 2, KD, P])
        u = sbuf(ctx, nc, "u_tile", [P, T])
        acc = sbuf(ctx, nc, "conv_acc", [P, T])
        tp = sbuf(ctx, nc, "ffn_taps", [P, 10])
        ps = psum(ctx, nc, "ffn_ps", [P, 2, 3, 512])
        with phase(nc, "w_in0", "w_in1", "mm0", "mm1", "taps_ok", "taps_b", "u_ok", "centre", "conv", "conv_sum",
                   "silu", "g_free", "u_free") as s:
            w_in, mm_done = [s["w_in0"], s["w_in1"]], [s["mm0"], s["mm1"]]
            SH = [(dy, dx) for dy in (-1, 0, 1) for dx in (-1, 0, 1) if (dy, dx) != (0, 0)]
            NCONV = len(SH) + 2
            with nc.Block() as block:
                @block.sync
                def _(sp):
                    with sp.Fori(0, FT) as m:
                        early(sp, w_src[0, m], w_src[1, m])
                        for h in range(2):
                            sp.wait_ge(mm_done[h], m)
                            sp.dma_start(W[:, h], w_src[h, m]).then_inc(w_in[h], 16)

                @block.tensor
                def _(pe):
                    with pe.Fori(0, FT) as m:
                        pe.wait_ge(w_in[0], m * 16 + 16)
                        pe.wait_ge(s["u_ok"], m * 2)
                        matmul_tile(pe, ps[:, 0], W[:, 0], HT, KD).then_inc(mm_done[0], 1)
                        pe.wait_ge(w_in[1], m * 16 + 16)
                        pe.wait_ge(s["g_free"], m * 2)
                        matmul_tile(pe, ps[:, 1], W[:, 1], HT, KD).then_inc(mm_done[1], 1)

                @block.scalar
                def _(act):
                    with act.Fori(0, FT) as m:
                        act.wait_ge(mm_done[0], m + 1)
                        act.wait_ge(s["conv_sum"], m)
                        act.activation(u[:, 0:CTX], ps[:, 0, 0, 0:CTX], ACT.Copy).then_inc(s["u_ok"], 1)
                        act.activation(u[:, CTX:T], lat(ps[:, 0]), ACT.Copy).then_inc(s["u_ok"], 1)
                        act.wait_ge(s["u_ok"], m * 2 + 2)
                        act.wait_ge(s["taps_ok"], m * 2 + 2)
                        act.wait_ge(s["g_free"], m * 2)
                        act.activation(acc[:], u[:], ACT.Identity, bias=tp[:, 9:10],
                                       scale=tp[:, 4:5]).then_inc(s["centre"], 1)
                        act.wait_ge(s["conv_sum"], m + 1)
                        act.activation(acc[:], acc[:], ACT.Silu).then_inc(s["silu"], 1)

                @block.vector
                def _(dve):
                    with dve.Fori(0, FT) as m:
                        dve.wait_ge(s["g_free"], m * 2)
                        dve.tensor_copy(tp[:, 0:9], ffw[:, :, bass.ds(m, 1)].rearrange("p t m -> p (t m)")).then_inc(s["taps_ok"], 1)
                        dve.tensor_copy(tp[:, 9:10], ffb[:, bass.ds(m, 1)]).then_inc(s["taps_ok"], 1)
                        dve.wait_ge(s["centre"], m + 1)
                        dve.wait_ge(s["taps_ok"], m * 2 + 2)
                        ug = u[:, CTX:T].rearrange("p (r c) -> p r c", c=GRID)
                        ag = acc[:, CTX:T].rearrange("p (r c) -> p r c", c=GRID)
                        n = 0
                        for dy, dx in SH:
                            r0, r1 = max(0, -dy), ROWS - max(0, dy)
                            c0, c1 = max(0, -dx), GRID - max(0, dx)
                            t = 3 * (dy + 1) + dx + 1
                            steps = [(ag[:, r0:r1, c0:c1], ug[:, r0 + dy:r1 + dy, c0 + dx:c1 + dx])]
                            if dy == 0:
                                a, b = max(0, -dx), CTX - max(0, dx)
                                steps.append((acc[:, a:b], u[:, a + dx:b + dx]))
                            for o, i in steps:
                                if n:
                                    dve.wait_ge(s["conv"], m * (NCONV - 1) + n)
                                n += 1
                                dve.scalar_tensor_tensor(out=o, in0=i, scalar=tp[:, t:t + 1], in1=o,
                                                         op0=ALU.mult, op1=ALU.add).then_inc(
                                    s["conv"] if n < NCONV else s["conv_sum"], 1)
                        dve.wait_ge(s["silu"], m + 1)
                        dve.wait_ge(mm_done[1], m + 1)
                        dve.tensor_tensor(G[:, m, 0:CTX], acc[:, 0:CTX], ps[:, 1, 0, 0:CTX], ALU.mult).then_inc(s["g_free"], 1)
                        dve.tensor_tensor(G[:, m, CTX:T], acc[:, CTX:T], lat(ps[:, 1]), ALU.mult).then_inc(s["g_free"], 1)


def store_out_phase(nc, K, y_prompt, y_sample):
    HT = K["HT"]
    yp = y_prompt.rearrange("b p c -> (b p) c")
    ys = y_sample.rearrange("b (n p) c -> (b n) p c", p=P)
    with ExitStack() as ctx:
        y = sbuf(ctx, nc, "y_tokens", [P, 2, D])
        col = sbuf(ctx, nc, "h_cols", [P, 2, KD, P])
        ps = psum(ctx, nc, "y_ps", [P, 2, D])
        with phase(nc, "cols0", "cols1", "turned0", "turned1", "y0", "y1", "stored0", "stored1") as s:
            cols, turned, y_ok, stored = [[s[n + "0"], s[n + "1"]] for n in ("cols", "turned", "y", "stored")]
            with nc.Block() as block:
                @block.vector
                def _(dve):
                    def take(j, k, t):
                        dve.wait_ge(turned[k], j)
                        dve.tensor_copy(col[:, k], HT[:, :, bass.ds(t * P, P)]).then_inc(cols[k], 1)
                    with dve.Fori(0, 4) as j:
                        for k in range(2):
                            take(j, k, 2 * j + k)
                    take(4, 0, 8)

                @block.tensor
                def _(pe):
                    def turn(j, k):
                        pe.wait_ge(cols[k], j + 1)
                        pe.wait_ge(y_ok[k], j)
                        for c in range(KD):
                            mm = pe.transpose(ps[:, k, c * P:c * P + P], col[:, k, c, :], K["ident"][:])
                        mm.then_inc(turned[k], 1)
                    with pe.Fori(0, 4) as j:
                        for k in range(2):
                            turn(j, k)
                    turn(4, 0)

                @block.scalar
                def _(act):
                    def out(j, k):
                        act.wait_ge(turned[k], j + 1)
                        act.wait_ge(stored[k], j * 16)
                        act.activation(y[:, k, :], ps[:, k, :], ACT.Copy).then_inc(y_ok[k], 1)
                    with act.Fori(0, 4) as j:
                        for k in range(2):
                            out(j, k)
                    out(4, 0)

                @block.gpsimd
                def _(pool):
                    pool.wait_ge(y_ok[0], 1)
                    pool.dma_start(yp, y[:, 0, :]).then_inc(stored[0], 16)
                    with pool.Fori(0, 4) as j:
                        for k in (1, 0):
                            pool.wait_ge(y_ok[k], j + (2 - k))
                            pool.dma_start(ys[2 * j + (1 - k)], y[:, k, :]).then_inc(stored[k], 16)
                    pool.wait_ge(stored[0], 5 * 16)
                    pool.wait_ge(stored[1], 4 * 16)


class Steps:

    def __init__(self, sem, names):
        self.sem, self.names, self.n = sem, names, 0

    def did(self, ins, name):
        assert self.names[self.n % len(self.names)] == name, (self.names[self.n % len(self.names)], name)
        self.n += 1
        ins.then_inc(self.sem, 1)

    def value(self, name, it):
        return it * len(self.names) + (self.names.index(name) + 1)

    def wait(self, eng, name, it=0):
        eng.wait_ge(self.sem, self.value(name, it))

    def wait_before(self, eng, it):
        eng.wait_ge(self.sem, it * len(self.names))


def chunked(ap):
    return ap.rearrange("p (c t) -> p c t", t=P)


def banks(T0=((0, 128), (128, 640), (640, 1152))):
    return list(enumerate(T0))


RW_DVE = (["pv", "ka1", "kkraw", "rinv", "kk"]
          + [f"{n}{d}" for d in range(2) for n in ("kd_a", "kd", "ks", "b", "G", "M", "Gm", "Gex", "kkd", "rd", "kt", "bt")]
          + ["rk", "bonus_c", "bonus_l"])
RW_ACT = (["sq", "root_c", "root_l"]
          + [f"{n}{d}" for d in range(2) for n in ("sg_c", "sg_l", "a_c", "a_l", "em", "e_in", "e_ex", "e_inv")])
RW_PE = ["norm"] + [f"{n}{d}" for d in range(2) for n in ("w", "a")] + ["bonus"]


def rwkv_prep_phase(nc, A, K, zc, units, bonus):
    HT = K["HT"]
    kkt, at, kdt, bt, sgt, gt, gx, ks = [HT[:, i, :] for i in range(8)]
    with ExitStack() as ctx:
        wd = sbuf(ctx, nc, "wd", [P, T])
        ad = sbuf(ctx, nc, "ad", [P, T])
        rkv = sbuf(ctx, nc, "rkv", [P, 2, 3, T])
        up = sbuf(ctx, nc, "w_a_up", [P, 2, 2, P])
        un = sbuf(ctx, nc, "unit_rows", [P, 2, NCH, 4, P])
        reset = sbuf(ctx, nc, "resets", [P, 2, T])
        pv = sbuf(ctx, nc, "pair_params", [P, 8])
        m9 = sbuf(ctx, nc, "half_end", [P, 2, NCH])
        tiny = sbuf(ctx, nc, "kk_eps", [P, 1])
        ps = psum(ctx, nc, "prep_ps", [P, 2, 3, 512])
        w_up = A["rk_w_up"][0].rearrange("d r (q c) -> q (d r) c", c=P)
        a_up = A["rk_a_up"][0].rearrange("d r (q c) -> q (d r) c", c=P)
        par = K["PT"][:, C_W0:C_W0 + 28].rearrange("p (g q) -> p g q", q=4)
        with phase(nc, "loras_in", "in0", "in1", "dve", "act", "pe", "tanh", "ready", "st_un0", "st_un1", "st_bonus") as s:
            dv, ac, pe_ = Steps(s["dve"], RW_DVE), Steps(s["act"], RW_ACT), Steps(s["pe"], RW_PE)
            loaded = [s["in0"], s["in1"]]
            st_un = [s["st_un0"], s["st_un1"]]
            with nc.Block() as block:
                @block.sync
                def _(sp):
                    sp.dma_start(wd[:], zc[12]).then_inc(s["loras_in"], 16)
                    sp.dma_start(ad[:], zc[13]).then_inc(s["loras_in"], 16)

                    def load(q, k):
                        for i in range(3):
                            sp.dma_start(rkv[:, k, i, :], zc[4 * i + q]).then_inc(loaded[k], 16)
                        sp.dma_start(up[:, k, 0, :], w_up[q]).then_inc(loaded[k], 16)
                        sp.dma_start(up[:, k, 1, :], a_up[q]).then_inc(loaded[k], 16)
                    load(0, 0)
                    load(1, 1)
                    for k in range(2):
                        dv.wait(sp, "bonus_l", k)
                        load(2 + k, k)

                @block.tensor
                def _(pe):
                    with pe.Fori(0, 2) as j:
                        for k in range(2):
                            it = 2 * j + k
                            ac.wait(pe, "sq", it)
                            dv.wait_before(pe, it)
                            for b, (x, y) in banks():
                                mm = pe.matmul(ps[:, 0, b, 0:y - x], K["ones64"][:], at[:, x:y], start=True, stop=True)
                            pe_.did(mm, "norm")
                            for d in range(2):
                                pe.wait_ge(s["tanh"], 1)
                                pe.wait_ge(loaded[k], j * 80 + 80)
                                ac.wait(pe, "root_l" if d == 0 else "sg_l0", it)
                                for b, (x, y) in banks():
                                    mm = pe.matmul(ps[:, 0, b, 0:y - x], up[64 * d:64 * d + 64, k, 0, :],
                                                   wd[64 * d:64 * d + 64, x:y], start=True, stop=True)
                                pe_.did(mm, f"w{d}")
                                if d == 1:
                                    ac.wait(pe, "a_l0", it)
                                for b, (x, y) in banks():
                                    mm = pe.matmul(ps[:, 1, b, 0:y - x], up[64 * d:64 * d + 64, k, 1, :],
                                                   ad[64 * d:64 * d + 64, x:y], start=True, stop=True)
                                pe_.did(mm, f"a{d}")
                            dv.wait(pe, "rk", it)
                            ac.wait(pe, "sg_l1", it)
                            for b, (x, y) in banks():
                                mm = pe.matmul(ps[:, 0, b, 0:y - x], K["ones64"][:], ks[:, x:y], start=True, stop=True)
                            pe_.did(mm, "bonus")

                @block.scalar
                def _(act):
                    act.wait_ge(s["loras_in"], 32)
                    act.activation(wd[:], wd[:], ACT.Tanh).then_inc(s["tanh"], 1)
                    act.wait_ge(s["ready"], 3)
                    with act.Fori(0, 2) as j:
                        for k in range(2):
                            it = 2 * j + k
                            dv.wait(act, "kkraw", it)
                            ac.did(act.activation(at, kkt, ACT.Square), "sq")
                            pe_.wait(act, "norm", it)
                            for n, q, v in (("c", slice(0, CTX), ps[:, 0, 0, 0:CTX]), ("l", slice(CTX, T), lat(ps[:, 0]))):
                                ac.did(act.activation(kdt[:, q], v, ACT.Sqrt, bias=tiny[:]), f"root_{n}")
                            for d in range(2):
                                for nm, sl, dst, off in (("sg", 0, sgt, d), ("a", 1, at, 2 + d)):
                                    pe_.wait(act, f"{'w' if sl == 0 else 'a'}{d}", it)
                                    if d == 1:
                                        dv.wait(act, "bt0", it)
                                    for n, q, v in (("c", slice(0, CTX), ps[:, sl, 0, 0:CTX]),
                                                    ("l", slice(CTX, T), lat(ps[:, sl]))):
                                        ac.did(act.activation(dst[:, q], v, ACT.Sigmoid, bias=pv[:, off:off + 1]),
                                               f"{nm}_{n}{d}")
                                act.wait_ge(st_un[d], it * 16)
                                dv.wait(act, f"Gex{d}", it)
                                em = K["EM"][:, d, :, bass.ds(it, 1)].rearrange("p c o -> p (c o)")
                                ac.did(act.activation(em, m9[:, d, :], ACT.Exp, scale=-EXP_HALF), f"em{d}")
                                g, x = chunked(gt), chunked(gx)
                                ac.did(act.activation(un[:, d, :, 1, :], g, ACT.Exp, scale=-EXP_HALF), f"e_in{d}")
                                ac.did(act.activation(un[:, d, :, 0, :], x, ACT.Exp, scale=-EXP_HALF), f"e_ex{d}")
                                ac.did(act.activation(un[:, d, :, 2, :], g, ACT.Exp, scale=EXP_HALF), f"e_inv{d}")

                @block.vector
                def _(dve):
                    dve.memset(reset[:], 1.0).then_inc(s["ready"], 1)
                    dve.memset(tiny[:], 1e-12).then_inc(s["ready"], 1)
                    dve.wait_ge(s["ready"], 2)
                    for d in range(2):
                        ins = dve.memset(chunked(reset[:, d, :])[:, :, d * (P - 1):d * (P - 1) + 1], 0.0)
                    ins.then_inc(s["ready"], 1)
                    dve.wait_ge(s["ready"], 3)
                    with dve.Fori(0, 2) as j:
                        for k in range(2):
                            it = 2 * j + k
                            r, kr, v = [rkv[:, k, i, :] for i in range(3)]
                            ac.wait_before(dve, it)
                            dve.wait_ge(s["st_bonus"], it * 16)
                            dv.did(dve.tensor_copy(pv[:, 0:7], par[:, :, bass.ds(it, 1)].rearrange("p g o -> p (g o)")), "pv")
                            dv.wait(dve, "pv", it)
                            dv.did(dve.tensor_scalar(pv[:, 7:8], pv[:, 5:6], -1.0, 1.0, ALU.mult, ALU.add), "ka1")
                            dve.wait_ge(loaded[k], j * 80 + 80)
                            dv.did(dve.tensor_scalar(kkt, kr, pv[:, 4:5], None, ALU.mult), "kkraw")
                            ac.wait(dve, "root_l", it)
                            dv.did(dve.reciprocal(kdt, kdt), "rinv")
                            dv.wait(dve, "rinv", it)
                            dv.did(dve.tensor_tensor(kkt, kkt, kdt, ALU.mult), "kk")
                            for d in range(2):
                                ac.wait(dve, f"a_l{d}", it)
                                dv.wait(dve, "kk" if d == 0 else "bt0", it)
                                dv.did(dve.tensor_scalar(kdt, at, pv[:, 5:6], pv[:, 7:8], ALU.mult, ALU.add), f"kd_a{d}")
                                dv.wait(dve, f"kd_a{d}", it)
                                dv.did(dve.tensor_tensor(kdt, kdt, kr, ALU.mult), f"kd{d}")
                                dv.wait(dve, f"kd{d}", it)
                                if d == 0:
                                    dv.did(dve.tensor_copy(ks, kdt), "ks0")
                                else:
                                    dv.did(dve.tensor_tensor(ks, ks, kdt, ALU.add), "ks1")
                                dv.did(dve.tensor_tensor(bt, kkt, at, ALU.mult), f"b{d}")
                                sd = -1 if d else 1
                                if d == 1:
                                    ac.wait(dve, "e_inv0", it)
                                dv.did(dve.tensor_tensor_scan(gt[:, ::sd], reset[:, d, ::sd], sgt[:, ::sd], 0.0,
                                                              ALU.mult, ALU.add), f"G{d}")
                                dv.wait(dve, f"G{d}", it)
                                end = chunked(gt)[:, :, (0 if d else P - 1):(1 if d else P)]
                                dv.did(dve.tensor_scalar(m9[:, d, :], end.rearrange("p c o -> p (c o)"), 0.5, None,
                                                         ALU.mult), f"M{d}")
                                dv.wait(dve, f"M{d}", it)
                                dv.did(dve.tensor_tensor(chunked(gt), chunked(gt),
                                                         m9[:, d, :, None].to_broadcast([P, NCH, P]), ALU.subtract), f"Gm{d}")
                                dv.wait(dve, f"Gm{d}", it)
                                dv.did(dve.tensor_tensor(gx, gt, sgt, ALU.subtract), f"Gex{d}")
                                u = un[:, d]
                                ac.wait(dve, f"e_ex{d}", it)
                                dv.did(dve.tensor_tensor(u[:, :, 0, :], u[:, :, 0, :], chunked(kkt), ALU.mult), f"kkd{d}")
                                dv.did(dve.tensor_tensor(u[:, :, 1, :], u[:, :, 1, :], chunked(r), ALU.mult), f"rd{d}")
                                ac.wait(dve, f"e_inv{d}", it)
                                dv.did(dve.tensor_tensor(u[:, :, 3, :], u[:, :, 2, :], chunked(kdt), ALU.mult), f"kt{d}")
                                dv.wait(dve, f"kt{d}", it)
                                dv.did(dve.tensor_tensor(u[:, :, 2, :], u[:, :, 2, :], chunked(bt), ALU.mult), f"bt{d}")
                            dv.did(dve.scalar_tensor_tensor(out=ks, in0=ks, scalar=pv[:, 6:7], in1=r, op0=ALU.mult,
                                                            op1=ALU.mult), "rk")
                            pe_.wait(dve, "bonus", it)
                            dv.did(dve.tensor_tensor(ks[:, 0:CTX], v[:, 0:CTX], ps[:, 0, 0, 0:CTX], ALU.mult), "bonus_c")
                            dv.did(dve.tensor_tensor(ks[:, CTX:T], v[:, CTX:T], lat(ps[:, 0]), ALU.mult), "bonus_l")

                @block.gpsimd
                def _(pool):
                    with pool.Fori(0, 4) as it:
                        for d in range(2):
                            dv.wait(pool, f"bt{d}", it)
                            pool.dma_start(units[it, d].rearrange("p c u t -> p (c u t)"),
                                           un[:, d].rearrange("p c u t -> p (c u t)")).then_inc(st_un[d], 16)
                        dv.wait(pool, "bonus_l", it)
                        pool.dma_start(bonus[it], ks).then_inc(s["st_bonus"], 16)
                    for n in ("st_un0", "st_un1", "st_bonus"):
                        pool.wait_ge(s[n], 64)


class ItSteps:

    def __init__(self, steps, it):
        self.steps, self.it = steps, it

    def did(self, ins, name):
        self.steps.did(ins, name)

    def wait(self, eng, name):
        self.steps.wait(eng, name, self.it)


NL = len(LEVELS)
INV_PE = ["y0"] + [f"{n}{l}" for l in range(1, NL - 1) for n in ("w", "dy", "dx")] + [f"w{NL - 1}", f"dx{NL - 1}"]


def inverse_pe(pe, ps, st, K, B, q, g, level):
    dv, ac, po, pe_ = st
    X, Y, W, NM = B["X"][:, g], B["Y"][:, g], B["W"][:, g], B["NM"][:, g]
    lanes = [(h, d) for h in range(2) for d in range(2)]

    def bank(n, i):
        return ps[:, g, n, i * P:i * P + P]
    if level == 0:
        po.wait(pe, f"{q}m0")
        for i, (h, d) in enumerate(lanes):
            mm = pe.transpose(bank(0, i), NM[:, 0, h, d, :], K["ident"][:])
        pe_.did(mm, f"{q}y0")
        return
    po.wait(pe, f"{q}m{level}")
    dv.wait(pe, f"{q}Y{level - 1}")
    if level > 1:
        dv.wait(pe, f"{q}X{level - 1}")
    else:
        po.wait(pe, f"{q}X0")
    for i, (h, d) in enumerate(lanes):
        mm = pe.matmul(bank(1, i), NM[:, level, h, d, :], Y[:, h, d, :], start=True, stop=True)
    pe_.did(mm, f"{q}w{level}")


def inverse_pe2(pe, ps, st, K, B, q, g, level):
    dv, ac, po, pe_ = st
    X, Y, W = B["X"][:, g], B["Y"][:, g], B["W"][:, g]
    lanes = [(h, d) for h in range(2) for d in range(2)]
    ac.wait(pe, f"{q}W{level}")
    if level < NL - 1:
        for i, (h, d) in enumerate(lanes):
            mm = pe.matmul(ps[:, g, 2, i * P:i * P + P], X[:, h, d, :], W[:, h, d, :], start=True, stop=True)
        pe_.did(mm, f"{q}dy{level}")
    for i, (h, d) in enumerate(lanes):
        mm = pe.matmul(ps[:, g, 3, i * P:i * P + P], W[:, h, d, :], X[:, h, d, :], start=True, stop=True)
    pe_.did(mm, f"{q}dx{level}")


INV_DVE = ["Y0"] + [f"{n}{l}" for l in range(1, NL - 1) for n in ("Y", "X")] + [f"X{NL - 1}"]


def four(ap):
    return ap.rearrange("p h d t -> p (h d t)")


def inverse_dve(dve, ps, st, K, B, q, g, level):
    dv, ac, po, pe_ = st
    X, Y = four(B["X"][:, g]), four(B["Y"][:, g])
    if level == 0:
        pe_.wait(dve, f"{q}y0")
        dv.did(dve.tensor_tensor(Y.rearrange("p (l t) -> p l t", t=P), K["ident"][:, None, :].to_broadcast([P, 4, P]),
                                 ps[:, g, 0, :].rearrange("p (l t) -> p l t", t=P), ALU.subtract), f"{q}Y0")
        return
    if level < NL - 1:
        pe_.wait(dve, f"{q}dx{level}")
        dv.did(dve.tensor_tensor(Y, Y, ps[:, g, 2, :], ALU.subtract), f"{q}Y{level}")
    pe_.wait(dve, f"{q}dx{level}")
    dv.did(dve.tensor_tensor(X, X, ps[:, g, 3, :], ALU.subtract), f"{q}X{level}")


INV_POOL = ["m0", "X0"] + [f"m{l}" for l in range(1, NL)]


def inverse_pool(pool, st, K, B, q, g):
    dv, ac, po, pe_ = st
    N, NM, X = B["N"][:, g], B["NM"][:, g], B["X"][:, g]
    for level in range(NL):
        po.did(pool.tensor_tensor(NM[:, level], N[:, :, :, 0, :],
                                  K["pairs"][:, level, None, :, :].to_broadcast([P, 2, 2, P]), ALU.mult), f"{q}m{level}")
        if level == 0:
            po.wait(pool, f"{q}m0")
            po.did(pool.tensor_tensor(four(X).rearrange("p (l t) -> p l t", t=P),
                                      K["ident"][:, None, :].to_broadcast([P, 4, P]),
                                      four(NM[:, 0]).rearrange("p (l t) -> p l t", t=P), ALU.subtract), f"{q}X0")


def scan_steps(s, groups, pe_pre, pe_post, dve_pre, dve_post, act_pre, act_post, dve_head=(), inverse=True):
    pe, dve, act, pool = [], list(dve_head), [], []
    for a in range(0, groups, 2):
        prs = (a, a + 1)
        for lst, names in ((pe, pe_pre), (dve, dve_pre), (act, act_pre)):
            for q in prs:
                lst += [f"{q}{n}" for n in names]
        if inverse:
            for q in prs:
                pool += [f"{q}{n}" for n in INV_POOL]
            for l in range(NL):
                for q in prs:
                    pe += [f"{q}y0"] if l == 0 else [f"{q}w{l}"]
                    if l:
                        act += [f"{q}W{l}"]
                if l:
                    for q in prs:
                        pe += [f"{q}dy{l}", f"{q}dx{l}"] if l < NL - 1 else [f"{q}dx{l}"]
                for q in prs:
                    dve += [f"{q}Y0"] if l == 0 else ([f"{q}Y{l}", f"{q}X{l}"] if l < NL - 1 else [f"{q}X{l}"])
        for names, lst in ((pe_post, pe), (dve_post, dve), (act_post, act)):
            for part in names:
                for q in prs:
                    lst += [f"{q}{n}" for n in part]
    return Steps(s["dve"], dve), Steps(s["act"], act), Steps(s["pool"], pool), Steps(s["pe"], pe)


def scan_iterations(eng, steps, body):
    if steps == 1:
        body(0, 0, 0)
    else:
        with eng.Fori(0, steps) as it:
            body(it, it + 1, steps - it)


def rwkv_scan_phase(nc, K, units, zc, yscan, steps, state):
    with ExitStack() as ctx:
        B = {n: sbuf(ctx, nc, n, [P, 2, 2, 2, P]) for n in ("X", "Y", "W")}
        B["N"] = sbuf(ctx, nc, "N", [P, 2, 2, 2, 2, P])
        B["NM"] = sbuf(ctx, nc, "NM", [P, 2, NL, 2, 2, P])
        AK = sbuf(ctx, nc, "AK", [P, 2, 2, 2, 2, P])
        un = sbuf(ctx, nc, "un", [P, 4, 2, 4, P])
        vv = sbuf(ctx, nc, "vv", [P, 4, 2, P])
        tok = sbuf(ctx, nc, "tok", [P, 2, 3, 2, P])
        em = sbuf(ctx, nc, "em", [P, 2, 4])
        S1 = sbuf(ctx, nc, "S_scaled", [P, 4, 2, 64])
        Rb = sbuf(ctx, nc, "Rb", [P, 2, 2, 2, 64])
        Ub = sbuf(ctx, nc, "Ub", [P, 2, 2, 2, 64])
        yt = sbuf(ctx, nc, "yt", [P, 4, 2, P])
        ps = psum(ctx, nc, "scan_ps", [P, 2, 4, 512])
        with phase(nc, "dve", "act", "pool", "pe", *[f"in{q}" for q in range(4)], *[f"out{q}" for q in range(4)]) as s:
            st = scan_steps(s, 4, ["tok", "a1", "a2"], [["r"], ["u"], ["y", "s"]],
                            ["S1", "n0", "n1", "k0", "k1"], [["s_tmp", "S"]],
                            ["tok_a", "tok_b"], [["R0", "R1"], ["U"], ["yt0", "yt1"]], dve_head=["em0", "em1"])
            dv, ac, po, pe_ = st
            loaded = [s[f"in{q}"] for q in range(4)]
            stored = [s[f"out{q}"] for q in range(4)]
            u_src = units.rearrange("q d p c u t -> q d c p (u t)")
            v_src = zc.rearrange("m p (c t) -> m c p t", t=P)
            y_dst = yscan.rearrange("d q p (c t) -> d q c p t", t=P)
            with nc.Block() as block:
                @block.sync
                def _(sp):
                    def load(q, d, c):
                        sp.dma_start(un[:, q, d], u_src[q, d, c].rearrange("p (u t) -> p u t", u=4)).then_inc(loaded[q], 16)
                        sp.dma_start(vv[:, q, d], v_src[8 + q, c]).then_inc(loaded[q], 16)

                    def body(it, cs, wait):
                        for q in range(4):
                            for d in range(2):
                                early(sp, u_src[q, d, cs[d]], v_src[8 + q, cs[d]])
                        for q in range(4):
                            if wait:
                                pe_.wait(sp, f"{q}s", it - 1)
                            for d in range(2):
                                load(q, d, cs[d])
                    if steps == 1:
                        body(0, (0, 0), False)
                    else:
                        body(0, (1, steps), False)
                        with sp.Fori(1, steps) as it:
                            body(it, (it + 1, steps - it), True)

                @block.tensor
                def _(pe):
                    def body(it, c0, c1):
                        for a in (0, 2):
                            for q in (a, a + 1):
                                g = q - a
                                pe.wait_ge(loaded[q], it * 64 + 64)
                                if a == 0:
                                    dv.wait_before(pe, it)
                                    ac.wait_before(pe, it)
                                else:
                                    dv.wait(pe, f"{g}S", it)
                                    ac.wait(pe, f"{g}yt1", it)
                                for i, (w, d) in enumerate(((2, 0), (2, 1), (3, 0), (3, 1))):
                                    pe.transpose(ps[:, g, 2, i * P:i * P + P], un[:, q, d, w, :], K["ident"][:])
                                for d in range(2):
                                    mm = pe.transpose(ps[:, g, 3, d * P:d * P + P], vv[:, q, d, :], K["ident"][:])
                                pe_.did(mm, f"{q}tok")
                                for w, nm in ((2, "a1"), (3, "a2")):
                                    if nm == "a2":
                                        ac.wait(pe, f"{q}tok_b", it)
                                    for d in range(2):
                                        for h in range(2):
                                            x = slice(64 * h, 64 * h + 64)
                                            mm = pe.matmul(ps[:, g, (w - 2) * 2 + h, d * 256:d * 256 + 256],
                                                           un[x, q, d, w, :], un[x, q, d, 0:2, :].rearrange("p u t -> p (u t)"),
                                                           start=True, stop=True)
                                    pe_.did(mm, f"{q}{nm}")
                            st_it = [ItSteps(x, it) for x in st]
                            for l in range(NL):
                                for q in (a, a + 1):
                                    if l == 0:
                                        dv.wait(pe, f"{q}n1", it)
                                    if l == 1:
                                        dv.wait(pe, f"{q}k1", it)
                                    inverse_pe(pe, ps, st_it, K, B, q, q - a, l)
                                if l:
                                    for q in (a, a + 1):
                                        inverse_pe2(pe, ps, st_it, K, B, q, q - a, l)
                            for q in (a, a + 1):
                                g = q - a
                                dv.wait(pe, f"{q}S1", it)
                                ac.wait(pe, f"{q}W{NL - 1}", it)
                                for h in range(2):
                                    x = slice(64 * h, 64 * h + 64)
                                    for d in range(2):
                                        o = ps[:, g, h, d * 64:d * 64 + 64]
                                        pe.matmul(o, un[x, q, d, 0, :], S1[x, q, d, :], start=True, stop=False)
                                        mm = pe.matmul(o, AK[:, g, h, d, 0, :], tok[:, g, 2, d, x], start=False, stop=True)
                                pe_.did(mm, f"{q}r")
                            for q in (a, a + 1):
                                g = q - a
                                dv.wait(pe, f"{q}X{NL - 1}", it)
                                ac.wait(pe, f"{q}R1", it)
                                for h in range(2):
                                    for d in range(2):
                                        i = 2 * h + d
                                        mm = pe.matmul(ps[:, g, 2, i * 64:i * 64 + 64], B["X"][:, g, h, d, :], Rb[:, g, h, d, :],
                                                       start=True, stop=True)
                                pe_.did(mm, f"{q}u")
                            for q in (a, a + 1):
                                g = q - a
                                ac.wait(pe, f"{q}U", it)
                                for h in range(2):
                                    x = slice(64 * h, 64 * h + 64)
                                    for d in range(2):
                                        o = ps[x, g, h, d * P:d * P + P]
                                        pe.matmul(o, Ub[:, g, h, d, :], B["N"][:, g, h, d, 1, :], start=True, stop=False)
                                        pe.matmul(o, tok[:, g, 2, d, x], AK[:, g, h, d, 1, :], start=False, stop=False)
                                        mm = pe.matmul(o, S1[x, q, d, :], un[x, q, d, 1, :], start=False, stop=True)
                                pe_.did(mm, f"{q}y")
                                for h in range(2):
                                    x = slice(64 * h, 64 * h + 64)
                                    for d in range(2):
                                        o = ps[x, g, 3, d * 64:d * 64 + 64]
                                        pe.matmul(o, tok[:, g, 0, d, x], Ub[:, g, h, d, :], start=True, stop=False)
                                        mm = pe.matmul(o, tok[:, g, 1, d, x], tok[:, g, 2, d, x], start=False, stop=True)
                                pe_.did(mm, f"{q}s")
                    scan_iterations(pe, steps, body)

                @block.scalar
                def _(act):
                    def body(it, c0, c1):
                        for a in (0, 2):
                            for q in (a, a + 1):
                                g = q - a
                                pe_.wait(act, f"{q}tok", it)
                                ac.did(act.activation(tok[:, g, 0:2].rearrange("p w d c -> p (w d c)"), ps[:, g, 2, :],
                                                      ACT.Copy), f"{q}tok_a")
                                ac.did(act.activation(tok[:, g, 2].rearrange("p d c -> p (d c)"), ps[:, g, 3, 0:256],
                                                      ACT.Copy), f"{q}tok_b")
                            for l in range(1, NL):
                                for q in (a, a + 1):
                                    pe_.wait(act, f"{q}w{l}", it)
                                    ac.did(act.activation(four(B["W"][:, q - a]), ps[:, q - a, 1, :], ACT.Copy), f"{q}W{l}")
                            for q in (a, a + 1):
                                pe_.wait(act, f"{q}r", it)
                                for h in range(2):
                                    ac.did(act.activation(Rb[:, q - a, h].rearrange("p d v -> p (d v)"),
                                                          ps[:, q - a, h, 0:P], ACT.Copy, scale=-1.0), f"{q}R{h}")
                            for q in (a, a + 1):
                                pe_.wait(act, f"{q}u", it)
                                ac.did(act.activation(Ub[:, q - a].rearrange("p h d v -> p (h d v)"),
                                                      ps[:, q - a, 2, 0:256], ACT.Copy), f"{q}U")
                            for q in (a, a + 1):
                                pe_.wait(act, f"{q}y", it)
                                act.wait_ge(stored[q], it * 32)
                                for h in range(2):
                                    x = slice(64 * h, 64 * h + 64)
                                    ac.did(act.activation(yt[x, q].rearrange("p d t -> p (d t)"), ps[x, q - a, h, 0:256],
                                                          ACT.Copy), f"{q}yt{h}")
                            for q in (a, a + 1):
                                ac.wait(act, f"{q}yt1", it)
                                for d in range(2):
                                    act.dma_start(y_dst[d, q, (c0, c1)[d]], yt[:, q, d, :]).then_inc(stored[q], 16)
                    scan_iterations(act, steps, body)
                    for q in range(4):
                        act.wait_ge(stored[q], steps * 32)

                @block.vector
                def _(dve):
                    def body(it, c0, c1):
                        dv.wait_before(dve, it)
                        for d, c in enumerate((c0, c1)):
                            dv.did(dve.tensor_copy(em[:, d, :], K["EM"][:, d, bass.ds(c, 1), :].rearrange("p o q -> p (o q)")),
                                   f"em{d}")
                        for a in (0, 2):
                            for q in (a, a + 1):
                                g = q - a
                                dv.wait(dve, "em1", it)
                                dv.did(dve.tensor_tensor(S1[:, q], state[:, q], em[:, :, q:q + 1].to_broadcast([P, 2, 64]),
                                                         ALU.mult), f"{q}S1")
                                for w, (nm, mt, dst) in enumerate((("n", "a1", B["N"]), ("k", "a2", AK))):
                                    pe_.wait(dve, f"{q}{mt}", it)
                                    for h in range(2):
                                        dv.did(dve.tensor_tensor(dst[:, g, h].rearrange("p d w t -> p (d w t)"), ps[:, g, 2 * w + h, :],
                                                                 K["order"][:].rearrange("p d w t -> p (d w t)"), ALU.mult),
                                               f"{q}{nm}{h}")
                            st_it = [ItSteps(x, it) for x in st]
                            for l in range(NL):
                                for q in (a, a + 1):
                                    inverse_dve(dve, ps, st_it, K, B, q, q - a, l)
                            for q in (a, a + 1):
                                pe_.wait(dve, f"{q}s", it)
                                dv.did(dve.tensor_tensor(S1[:, q].rearrange("p d v -> p (d v)"), S1[:, q].rearrange("p d v -> p (d v)"),
                                                         ps[:, q - a, 3, 0:P], ALU.add), f"{q}s_tmp")
                                dv.wait(dve, f"{q}s_tmp", it)
                                dv.did(dve.tensor_tensor(state[:, q], S1[:, q], em[:, :, q:q + 1].to_broadcast([P, 2, 64]),
                                                         ALU.mult), f"{q}S")
                    scan_iterations(dve, steps, body)

                @block.gpsimd
                def _(pool):
                    def body(it, c0, c1):
                        for a in (0, 2):
                            for q in (a, a + 1):
                                dv.wait(pool, f"{q}n1", it)
                                inverse_pool(pool, [ItSteps(x, it) for x in st], K, B, q, q - a)
                    scan_iterations(pool, steps, body)


GD_PREP_DVE = ["rk", "rq"]


def gdn_prep_phase(nc, A, K, zc, ztail, qkv):
    GR, GC = K["GR"], K["GC"]
    with ExitStack() as ctx:
        z3 = sbuf(ctx, nc, "kqv", [P, 2, 3, T])
        un = sbuf(ctx, nc, "gdn_rows", [P, 2, NCH, 3, P])
        sq = sbuf(ctx, nc, "gdn_sq", [P, 2, T])
        rn = sbuf(ctx, nc, "gdn_rnorm", [P, 2, T])
        eps = sbuf(ctx, nc, "gdn_eps", [P, 1])
        al, be, t0, reset = [K["HT"][0:4, 2 * i:2 * i + 2, :] for i in range(4)]
        prm = sbuf(ctx, nc, "gate_params", [4, 2, 2])
        ps = psum(ctx, nc, "gdn_ps", [P, 2, 3, 512])
        pc = psum(ctx, nc, "gdn_cols", [P, 512])
        with phase(nc, "rows_in", "params_in", "d_chain", "a_chain", "gates", "cols", "in0", "in1", "dve", "act", "pe",
                   "eps_set", "st0", "st1", "x_ready", "abs_done", "reset_ok") as s:
            dv = Steps(s["dve"], ["k", "q"])
            ac = Steps(s["act"], ["sk", "sq", "sv", "qk", "qq", "lk0", "lk1", "lq0", "lq1", "ek", "eq"])
            pe_ = Steps(s["pe"], ["nk", "nq"])
            loaded, stored = [s["in0"], s["in1"]], [s["st0"], s["st1"]]
            with nc.Block() as block:
                @block.sync
                def _(sp):
                    sp.dma_start(al, ztail[0:8, :].rearrange("(d h) t -> h d t", d=2)).then_inc(s["rows_in"], 16)
                    sp.dma_start(be, ztail[8:16, :].rearrange("(d h) t -> h d t", d=2)).then_inc(s["rows_in"], 16)
                    for i, n in enumerate(("gd_a_log", "gd_dt_bias")):
                        sp.dma_start(prm[:, i, :], A[n].rearrange("l d h -> h (l d)"),
                                     allow_slow_non_contiguous=True).then_inc(s["params_in"], 16)

                    def load(h, k):
                        for i, base in enumerate((19, 15, 23)):
                            sp.dma_start(z3[:, k, i, :], zc[base + h]).then_inc(loaded[k], 16)
                    load(0, 0)
                    load(1, 1)
                    for k in range(2):
                        ac.wait(sp, "sv", k)
                        load(2 + k, k)

                @block.scalar
                def _(act):
                    link = chain(act, s["a_chain"])
                    act.wait_ge(s["rows_in"], 32)
                    act.wait_ge(s["params_in"], 32)
                    link(act.activation(prm[:, 0, :], prm[:, 0, :], ACT.Exp))
                    link(act.activation(be, be, ACT.Sigmoid))
                    act.wait_ge(s["x_ready"], 2)
                    link(act.activation(t0, al, ACT.Abs))
                    link(act.activation(t0, t0, ACT.Exp, scale=-1.0))
                    link(act.activation(t0, t0, ACT.Ln, bias=1.0))
                    act.nop().then_inc(s["abs_done"], 1)
                    act.wait_ge(s["cols"], 1)
                    cols = pc[:, 0:NCH * 16].rearrange("p (c w x) -> p c w x", c=NCH, w=2)
                    out = [GC[:, :, i].rearrange("p c d h -> p c (d h)") for i in range(3)]
                    link(act.activation(out[0], cols[:, :, 0, :], ACT.Copy))
                    link(act.activation(out[2], cols[:, :, 1, :], ACT.Copy))
                    link(act.activation(out[1], cols[:, :, 0, :], ACT.Exp))
                    link(act.activation(out[1], out[1], ACT.Copy, scale=-1.0))
                    act.wait_ge(s["eps_set"], 1)
                    with act.Fori(0, 2) as j:
                        for k in range(2):
                            it = 2 * j + k
                            act.wait_ge(loaded[k], j * 48 + 48)
                            act.wait_ge(stored[k], j * 16)
                            dv.wait_before(act, it)
                            for i, n in enumerate("kqv"):
                                ac.did(act.activation(un[:, k, :, i, :], chunked(z3[:, k, i, :]), ACT.Silu), f"s{n}")
                            for i, n in enumerate("kq"):
                                ac.wait(act, f"s{n}", it)
                                ac.did(act.activation(chunked(sq[:, i, :]), un[:, k, :, i, :], ACT.Square), f"q{n}")
                            for i, n in enumerate("kq"):
                                pe_.wait(act, f"n{n}", it)
                                ac.did(act.activation(rn[:, i, 0:CTX], ps[:, i, 0, 0:CTX], ACT.Ln, bias=eps[:]), f"l{n}0")
                                ac.did(act.activation(rn[:, i, CTX:T], lat(ps[:, i]), ACT.Ln, bias=eps[:]), f"l{n}1")
                            for i, n in enumerate("kq"):
                                ac.wait(act, f"l{n}1", it)
                                ac.did(act.activation(rn[:, i], rn[:, i], ACT.Exp, scale=-0.5), f"e{n}")

                @block.tensor
                def _(pe):
                    pe.wait_ge(s["gates"], 1)
                    for c in range(NCH):
                        for w, src in enumerate((GR, be)):
                            for d in range(2):
                                o = c * 16 + w * 8 + d * 4
                                mm = pe.transpose(pc[:, o:o + 4], src[:, d, c * P:c * P + P], K["ident"][0:4, 0:4])
                    mm.then_inc(s["cols"], 1)
                    with pe.Fori(0, 4) as it:
                        for i, n in enumerate("kq"):
                            ac.wait(pe, f"q{n}", it)
                            if i == 0:
                                ac.wait_before(pe, it)
                            for b, (x, y) in banks():
                                mm = pe.matmul(ps[:, i, b, 0:y - x], K["ones"][:], sq[:, i, x:y], start=True, stop=True)
                            pe_.did(mm, f"n{n}")

                @block.vector
                def _(dve):
                    link = chain(dve, s["d_chain"])
                    dve.memset(eps[:], 1e-6).then_inc(s["eps_set"], 1)
                    link(dve.memset(reset, 1.0))
                    for d in range(2):
                        link(dve.memset(chunked(reset[:, d, :])[:, :, d * (P - 1):d * (P - 1) + 1], 0.0))
                    dve.wait_ge(s["rows_in"], 32)
                    dve.wait_ge(s["params_in"], 32)
                    for d in range(2):
                        dve.tensor_scalar(al[:, d], al[:, d], prm[:, 1, d:d + 1], None, ALU.add).then_inc(s["x_ready"], 1)
                    dve.wait_ge(s["abs_done"], 1)
                    link(dve.tensor_scalar(prm[:, 0, :], prm[:, 0, :], -1.0, None, ALU.mult))
                    link(dve.scalar_tensor_tensor(out=al, in0=al, scalar=0.0, in1=t0, op0=ALU.max, op1=ALU.add))
                    for d in range(2):
                        link(dve.tensor_scalar(al[:, d], al[:, d], prm[:, 0, d:d + 1], None, ALU.mult))
                    for d in range(2):
                        sd = -1 if d else 1
                        link(dve.tensor_tensor_scan(GR[:, d, ::sd], reset[:, d, ::sd], al[:, d, ::sd], 0.0,
                                                    ALU.mult, ALU.add))
                    dve.nop().then_inc(s["gates"], 1)
                    with dve.Fori(0, 2) as j:
                        for k in range(2):
                            it = 2 * j + k
                            ac.wait(dve, "ek", it)
                            dv.did(dve.tensor_tensor(un[:, k, :, 0, :], un[:, k, :, 0, :], chunked(rn[:, 0]), ALU.mult), "k")
                            ac.wait(dve, "eq", it)
                            dv.did(dve.scalar_tensor_tensor(out=un[:, k, :, 1, :], in0=un[:, k, :, 1, :], scalar=HD_B ** -0.5,
                                                            in1=chunked(rn[:, 1]), op0=ALU.mult, op1=ALU.mult), "q")

                @block.gpsimd
                def _(pool):
                    with pool.Fori(0, 2) as j:
                        for k in range(2):
                            dv.wait(pool, "q", 2 * j + k)
                            pool.dma_start(qkv[2 * j + k].rearrange("p c u t -> p (c u t)"),
                                           un[:, k].rearrange("p c u t -> p (c u t)")).then_inc(stored[k], 16)
                    for k in range(2):
                        pool.wait_ge(stored[k], 32)


def gdn_scan_phase(nc, K, qkv, oscan, steps, state):
    GR, GC = K["GR"], K["GC"]
    with ExitStack() as ctx:
        B = {n: sbuf(ctx, nc, n, [P, 2, 2, 2, P]) for n in ("X", "Y", "W")}
        B["N"] = sbuf(ctx, nc, "N", [P, 2, 2, 2, 2, P])
        B["NM"] = sbuf(ctx, nc, "NM", [P, 2, NL, 2, 2, P])
        un = sbuf(ctx, nc, "gun", [P, 2, 2, 2, 3, P])
        idle = K["HT"][:].rearrange("p k t -> p (k t)")
        kt, vt, Dm, EG, QD, Rb, Ub, yt = [
            idle[:, n * 8 * P:(n + 1) * 8 * P].rearrange("p (g h d t) -> p g h d t", g=2, h=2, d=2) for n in range(8)]
        DM = sbuf(ctx, nc, "decay_masked", [P, 2, 2, 2, 2, P])
        cs = sbuf(ctx, nc, "chunk_cols", [P, 3, 2, 4])
        gr = sbuf(ctx, nc, "chunk_rows", [4, 2, P])
        ps = psum(ctx, nc, "gscan_ps", [P, 2, 4, 512])
        lanes = [(h, d) for h in range(2) for d in range(2)]
        with phase(nc, "dve", "act", "pool", "pe", "in0", "in1", "out0", "out1") as s:
            st = scan_steps(s, 2, ["gb", "tok", "a"], [["r"], ["u"], ["y", "s"]],
                            ["d0", "n", "qk"], [["R"], ["S"]],
                            ["D", "EG", "v", "k"], [["U"], ["yt"]], dve_head=["cs0", "cs1", "gr0", "gr1"])
            dv, ac, po, pe_ = st
            dv.names[4:10] = ["0d0", "1d0", "0n", "0qk", "1n", "1qk"]
            po.names[:] = [f"{q}{n}" for q in range(2) for n in ["dm0", "dm1", "qd"] + INV_POOL]
            loaded, stored = [s["in0"], s["in1"]], [s["out0"], s["out1"]]
            u_src = qkv.rearrange("h p c u t -> h c p (u t)")
            o_dst = oscan.rearrange("d h p (c t) -> d h c p t", t=P)
            with nc.Block() as block:
                @block.sync
                def _(sp):
                    def body(it, cs_, wait):
                        for q in range(2):
                            for h, d in lanes:
                                early(sp, u_src[2 * q + h, cs_[d]])
                            if wait:
                                sp.lower_val(pe_.value(f"{q}s", it - 1))
                                sp.lower_val(po.value(f"{q}qd", it - 1))
                        for q in range(2):
                            if wait:
                                pe_.wait(sp, f"{q}s", it - 1)
                                po.wait(sp, f"{q}qd", it - 1)
                            for h, d in lanes:
                                sp.dma_start(un[:, q, h, d].rearrange("p u t -> p (u t)"),
                                             u_src[2 * q + h, cs_[d]]).then_inc(loaded[q], 16)
                    if steps == 1:
                        body(0, (0, 0), False)
                    else:
                        body(0, (1, steps), False)
                        with sp.Fori(1, steps) as it:
                            body(it, (it + 1, steps - it), True)

                @block.tensor
                def _(pe):
                    def body(it, c0, c1):
                        dv.wait(pe, "gr1", it)
                        dv.wait_before(pe, it)
                        ac.wait_before(pe, it)
                        st_it = [ItSteps(x, it) for x in st]
                        for q in range(2):
                            for i, (h, d) in enumerate(lanes):
                                mm = pe.matmul(ps[:, q, 0, i * P:i * P + P], K["sel"][0:4, 2 * q + h, :], gr[:, d, :],
                                               start=True, stop=True)
                            pe_.did(mm, f"{q}gb")
                            pe.wait_ge(loaded[q], it * 64 + 64)
                            for w, b in ((0, 2), (2, 3)):
                                for i, (h, d) in enumerate(lanes):
                                    mm = pe.transpose(ps[:, q, b, i * P:i * P + P], un[:, q, h, d, w, :], K["ident"][:])
                            pe_.did(mm, f"{q}tok")
                            ac.wait(pe, f"{q}EG", it)
                            dv.wait(pe, f"{q}d0", it)
                            for i, (h, d) in enumerate(lanes):
                                mm = pe.matmul(ps[:, q, h, d * 256:d * 256 + 256], un[:, q, h, d, 0, :],
                                               un[:, q, h, d, 0:2, :].rearrange("p u t -> p (u t)"), start=True, stop=True)
                            pe_.did(mm, f"{q}a")
                        for l in range(NL):
                            for q in range(2):
                                if l == 0:
                                    dv.wait(pe, f"{q}qk", it)
                                    ac.wait(pe, f"{q}k", it)
                                inverse_pe(pe, ps, st_it, K, B, q, q, l)
                            if l:
                                for q in range(2):
                                    inverse_pe2(pe, ps, st_it, K, B, q, q, l)
                        for q in range(2):
                            for i, (h, d) in enumerate(lanes):
                                mm = pe.matmul(ps[:, q, 0, i * P:i * P + P], un[:, q, h, d, 0, :], state[:, q, h, d, :],
                                               start=True, stop=True)
                            pe_.did(mm, f"{q}r")
                        for q in range(2):
                            dv.wait(pe, f"{q}X{NL - 1}", it)
                            dv.wait(pe, f"{q}R", it)
                            for i, (h, d) in enumerate(lanes):
                                mm = pe.matmul(ps[:, q, 2, i * P:i * P + P], B["X"][:, q, h, d, :], Rb[:, q, h, d, :],
                                               start=True, stop=True)
                            pe_.did(mm, f"{q}u")
                        for q in range(2):
                            ac.wait(pe, f"{q}U", it)
                            for i, (h, d) in enumerate(lanes):
                                o = ps[:, q, 1, i * P:i * P + P]
                                pe.matmul(o, state[:, q, h, d, :], QD[:, q, h, d, :], start=True, stop=False)
                                mm = pe.matmul(o, Ub[:, q, h, d, :], B["N"][:, q, h, d, 1, :], start=False, stop=True)
                            pe_.did(mm, f"{q}y")
                            for i, (h, d) in enumerate(lanes):
                                mm = pe.matmul(ps[:, q, 3, i * P:i * P + P], kt[:, q, h, d, :], Ub[:, q, h, d, :],
                                               start=True, stop=True)
                            pe_.did(mm, f"{q}s")
                    scan_iterations(pe, steps, body)

                @block.scalar
                def _(act):
                    def body(it, c0, c1):
                        for q in range(2):
                            dv.wait(act, f"{q}d0", it)
                            ac.did(act.activation(four(Dm[:, q]), four(Dm[:, q]), ACT.Exp), f"{q}D")
                            ac.did(act.activation(four(EG[:, q]), ps[:, q, 0, :], ACT.Exp), f"{q}EG")
                            pe_.wait(act, f"{q}tok", it)
                            ac.did(act.activation(four(vt[:, q]), ps[:, q, 3, :], ACT.Copy), f"{q}v")
                            ac.wait(act, f"{q}D", it)
                            for i, (h, d) in enumerate(lanes):
                                e = 0 if d else P - 1
                                ins = act.activation(kt[:, q, h, d, :], ps[:, q, 2, i * P:i * P + P], ACT.Copy,
                                                     scale=Dm[:, q, h, d, e:e + 1])
                            ac.did(ins, f"{q}k")
                        for l in range(1, NL):
                            for q in range(2):
                                pe_.wait(act, f"{q}w{l}", it)
                                ac.did(act.activation(four(B["W"][:, q]), ps[:, q, 1, :], ACT.Copy), f"{q}W{l}")
                        for q in range(2):
                            pe_.wait(act, f"{q}u", it)
                            for i, (h, d) in enumerate(lanes):
                                ins = act.activation(Ub[:, q, h, d, :], ps[:, q, 2, i * P:i * P + P], ACT.Copy,
                                                     scale=cs[:, 2, d, 2 * q + h:2 * q + h + 1])
                            ac.did(ins, f"{q}U")
                        for q in range(2):
                            pe_.wait(act, f"{q}y", it)
                            act.wait_ge(stored[q], it * 64)
                            ac.did(act.activation(four(yt[:, q]), ps[:, q, 1, :], ACT.Copy), f"{q}yt")
                        for q in range(2):
                            ac.wait(act, f"{q}yt", it)
                            for h, d in lanes:
                                act.dma_start(o_dst[d, 2 * q + h, (c0, c1)[d]], yt[:, q, h, d, :]).then_inc(stored[q], 16)
                    scan_iterations(act, steps, body)
                    for q in range(2):
                        act.wait_ge(stored[q], steps * 64)

                @block.vector
                def _(dve):
                    def body(it, c0, c1):
                        dv.wait_before(dve, it)
                        ac.wait_before(dve, it)
                        pe_.wait_before(dve, it)
                        po.wait_before(dve, it)
                        for d, c in enumerate((c0, c1)):
                            dv.did(dve.tensor_copy(cs[:, :, d, :], GC[:, bass.ds(c, 1), :, d, :].rearrange("p o w h -> p (o w) h")),
                                   f"cs{d}")
                        for d, c in enumerate((c0, c1)):
                            dv.did(dve.tensor_copy(gr[:, d, :], GR[:, d, bass.ds(c * P, P)]), f"gr{d}")
                        dv.wait(dve, "cs1", it)
                        for q in range(2):
                            pe_.wait(dve, f"{q}gb", it)
                            for i, (h, d) in enumerate(lanes):
                                ins = dve.tensor_scalar(Dm[:, q, h, d, :], ps[:, q, 0, i * P:i * P + P],
                                                        cs[:, 0, d, 2 * q + h:2 * q + h + 1], 0.0, ALU.subtract, ALU.min)
                            dv.did(ins, f"{q}d0")
                        for q in range(2):
                            pe_.wait(dve, f"{q}a", it)
                            po.wait(dve, f"{q}dm1", it)
                            for i, (h, d) in enumerate(lanes):
                                ins = dve.scalar_tensor_tensor(out=B["N"][:, q, h, d, 0, :], in0=ps[:, q, h, d * 256:d * 256 + P],
                                                               scalar=cs[:, 2, d, 2 * q + h:2 * q + h + 1],
                                                               in1=DM[:, q, h, d, 0, :], op0=ALU.mult, op1=ALU.mult)
                            dv.did(ins, f"{q}n")
                            qk = ps[:, q, 0:2, :].rearrange("p h (d w t) -> p h d w t", d=2, w=2)[:, :, :, 1, :]
                            dv.did(dve.tensor_tensor(B["N"][:, q, :, :, 1, :], qk, DM[:, q, :, :, 1, :], ALU.mult), f"{q}qk")
                        st_it = [ItSteps(x, it) for x in st]
                        for l in range(NL):
                            for q in range(2):
                                inverse_dve(dve, ps, st_it, K, B, q, q, l)
                        for q in range(2):
                            pe_.wait(dve, f"{q}r", it)
                            ac.wait(dve, f"{q}v", it)
                            for i, (h, d) in enumerate(lanes):
                                ins = dve.scalar_tensor_tensor(out=Rb[:, q, h, d, :], in0=ps[:, q, 0, i * P:i * P + P],
                                                               scalar=cs[:, 1, d, 2 * q + h:2 * q + h + 1],
                                                               in1=vt[:, q, h, d, :], op0=ALU.mult, op1=ALU.add)
                            dv.did(ins, f"{q}R")
                        for q in range(2):
                            pe_.wait(dve, f"{q}s", it)
                            for i, (h, d) in enumerate(lanes):
                                e = 0 if d else P - 1
                                ins = dve.scalar_tensor_tensor(out=state[:, q, h, d, :], in0=state[:, q, h, d, :],
                                                               scalar=EG[:, q, h, d, e:e + 1], in1=ps[:, q, 3, i * P:i * P + P],
                                                               op0=ALU.mult, op1=ALU.add)
                            dv.did(ins, f"{q}S")
                    scan_iterations(dve, steps, body)

                @block.gpsimd
                def _(pool):
                    def body(it, c0, c1):
                        for q in range(2):
                            ac.wait(pool, f"{q}EG", it)
                            for h in range(2):
                                po.did(pool.tensor_tensor(DM[:, q, h], Dm[:, q, h, :, None, :].to_broadcast([P, 2, 2, P]),
                                                          K["order"][:], ALU.mult), f"{q}dm{h}")
                            pool.wait_ge(loaded[q], it * 64 + 64)
                            po.did(pool.tensor_tensor(QD[:, q], un[:, q, :, :, 1, :], EG[:, q], ALU.mult), f"{q}qd")
                            dv.wait(pool, f"{q}n", it)
                            inverse_pool(pool, [ItSteps(x, it) for x in st], K, B, q, q)
                    scan_iterations(pool, steps, body)


def zero_states_phase(nc, tiles):
    with phase(nc, "zeroed") as s:
        with nc.Block() as block:
            @block.vector
            def _(dve):
                for t in tiles:
                    dve.memset(t, 0.0).then_inc(s["zeroed"], 1)
                dve.wait_ge(s["zeroed"], len(tiles))


def turn_states_phase(nc, K, outs, ins):
    n_out, n_in = sum(len(x[2]) for x in outs), sum(len(x[2]) for x in ins)
    with ExitStack() as ctx:
        ps = psum(ctx, nc, "state_ps", [P, 8, 512])
        with phase(nc, "loaded", "out_t", "out_c", "in_t", "in_c", "stored") as s:
            jobs_out = [j for x in outs for j in x[2]]
            jobs_in = [j for x in ins for j in x[2]]
            with nc.Block() as block:
                @block.sync
                def _(sp):
                    n = 0
                    for dram, stage, _ in ins:
                        for d, t in zip(dram, stage):
                            sp.dma_start(t, d).then_inc(s["loaded"], 16)
                    sp.wait_ge(s["out_c"], n_out)
                    for dram, stage, _ in outs:
                        for d, t in zip(dram, stage):
                            sp.dma_start(d, t).then_inc(s["stored"], 16)
                            n += 16
                    sp.wait_ge(s["stored"], n)

                def out_ps(n, src):
                    return ps[0:src.shape[1], n % 8, 0:src.shape[0]]

                @block.tensor
                def _(pe):
                    for n, (state, stage) in enumerate(jobs_out):
                        if n >= 8:
                            pe.wait_ge(s["out_c"], n - 7)
                        pe.transpose(out_ps(n, state), state, K["ident"][:]).then_inc(s["out_t"], 1)
                    pe.wait_ge(s["loaded"], 16 * sum(len(x[0]) for x in ins))
                    pe.wait_ge(s["out_c"], n_out)
                    for n, (state, stage) in enumerate(jobs_in):
                        if n >= 8:
                            pe.wait_ge(s["in_c"], n - 7)
                        k = stage.shape[0]
                        pe.transpose(out_ps(n, stage), stage, K["ident"][0:k, 0:k]).then_inc(s["in_t"], 1)

                @block.vector
                def _(dve):
                    for n, (state, stage) in enumerate(jobs_out):
                        dve.wait_ge(s["out_t"], n + 1)
                        dve.tensor_copy(stage, out_ps(n, state)).then_inc(s["out_c"], 1)
                    for n, (state, stage) in enumerate(jobs_in):
                        dve.wait_ge(s["in_t"], n + 1)
                        dve.tensor_copy(state, out_ps(n, stage)).then_inc(s["in_c"], 1)


def even_states(nc, ctx, A, rk_out, gd_out, rk_state, gd_state):
    r_o = sbuf(ctx, nc, "rk_stage_out", [64, 2, 4, P])
    r_i = sbuf(ctx, nc, "rk_stage_in", [64, 2, 4, P])
    g_o = sbuf(ctx, nc, "gd_stage_out", [P, 2, 4, P])
    g_i = sbuf(ctx, nc, "gd_stage_in", [P, 2, 4, P])

    def entry(rk, gd, r, g, out):
        rd = [rk[0, 0, d].rearrange("h v k -> v h k") for d in range(2)]
        gdd = [gd[0, 0, d].rearrange("h v k -> v h k") for d in range(2)]
        return [
            (rd, [r[:, d].rearrange("v q (h k) -> v (q h) k", h=2) for d in range(2)],
             [(rk_state[:, q, d, :], r[:, d, q, :]) for d in range(2) for q in range(4)]),
            (gdd, [g[:, d] for d in range(2)],
             [(gd_state[:, h // 2, h % 2, d, :], g[:, d, h, :]) for d in range(2) for h in range(4)]),
        ]
    return entry(rk_out, gd_out, r_o, g_o, True), entry(A["state_rwkv"], A["state_gdn"], r_i, g_i, False)


def odd_states(nc, ctx, A, c_out, n_out, state):
    c_o = sbuf(ctx, nc, "c_stage_out", [P, 2, 4, P])
    c_i = sbuf(ctx, nc, "c_stage_in", [P, 2, 4, P])
    n_o = sbuf(ctx, nc, "n_stage_out", [4, 2, P])
    n_i = sbuf(ctx, nc, "n_stage_in", [4, 2, P])

    def entry(c, n, cs, ns):
        return [
            ([c[0, 0, d].rearrange("h v k -> v h k") for d in range(2)],
             [cs[:, d].rearrange("v q (h k) -> v (q h) k", h=2) for d in range(2)],
             [(state[:, q, d, 0:P], cs[:, d, q, :]) for d in range(2) for q in range(4)]),
            ([n[0, 0, d].rearrange("(q h) k -> q (h k)", h=2) for d in range(2)],
             [ns[:, d, :] for d in range(2)],
             [(state[:, :, d, P], ns[:, d, :]) for d in range(2)]),
        ]
    return entry(c_out, n_out, c_o, n_o), entry(A["state_mlstm_c"], A["state_mlstm_n"], c_i, n_i)


def rwkv_post_phase(nc, A, K, zc, yscan, bonus):
    HT, PT = K["HT"], K["PT"]
    with ExitStack() as ctx:
        gd = sbuf(ctx, nc, "gd", [P, T])
        y3 = sbuf(ctx, nc, "y_fwd_bwd_bonus", [P, 2, 3, T])
        gu = sbuf(ctx, nc, "g_up", [P, 2, P])
        sq = sbuf(ctx, nc, "y_sq", [P, T])
        rs = sbuf(ctx, nc, "y_rstd", [P, T])
        lnp = sbuf(ctx, nc, "ln_params", [P, 2])
        eps = sbuf(ctx, nc, "ln_eps", [P, 1])
        ps = psum(ctx, nc, "post_ps", [P, 2, 3, 512])
        par = PT[:, C_LNG:C_LNG + 8].rearrange("p (g q) -> p g q", q=4)
        with phase(nc, "gd_in", "gd_ok", "in0", "in1", "dve", "act", "pe", "eps_set") as s:
            dv = Steps(s["dve"], ["par", "y", "yc_c", "yc_l", "yn", "ya", "yb", "o_c", "o_l"])
            ac = Steps(s["act"], ["sq", "ln_c", "ln_l", "rs"])
            pe_ = Steps(s["pe"], ["sum", "var", "g"])
            loaded = [s["in0"], s["in1"]]
            g_src = A["rk_g_up"][0].rearrange("r (q c) -> q r c", c=P)
            with nc.Block() as block:
                @block.sync
                def _(sp):
                    sp.dma_start(gd[:], zc[14]).then_inc(s["gd_in"], 16)
                    for q in range(4):
                        if q >= 2:
                            dv.wait(sp, "o_l", q - 2)
                        for i, src in enumerate((yscan[0, q], yscan[1, q], bonus[q])):
                            sp.dma_start(y3[:, q % 2, i, :], src).then_inc(loaded[q % 2], 16)
                        sp.dma_start(gu[:, q % 2, :], g_src[q]).then_inc(loaded[q % 2], 16)

                @block.tensor
                def _(pe):
                    with pe.Fori(0, 2) as j:
                        for k in range(2):
                            it = 2 * j + k
                            dv.wait(pe, "y", it)
                            for b, (x, y) in banks():
                                mm = pe.matmul(ps[:, 0, b, 0:y - x], K["ones64"][:], y3[:, k, 0, x:y], start=True, stop=True)
                            pe_.did(mm, "sum")
                            ac.wait(pe, "sq", it)
                            for b, (x, y) in banks():
                                mm = pe.matmul(ps[:, 1, b, 0:y - x], K["ones64"][:], sq[:, x:y], start=True, stop=True)
                            pe_.did(mm, "var")
                            pe.wait_ge(s["gd_ok"], 1)
                            dv.wait(pe, "yc_l", it)
                            for b, (x, y) in banks():
                                mm = pe.matmul(ps[:, 0, b, 0:y - x], gu[:, k, :], gd[:, x:y], start=True, stop=True)
                            pe_.did(mm, "g")

                @block.scalar
                def _(act):
                    act.wait_ge(s["gd_in"], 16)
                    act.activation(gd[:], gd[:], ACT.Sigmoid).then_inc(s["gd_ok"], 1)
                    act.wait_ge(s["eps_set"], 1)
                    with act.Fori(0, 2) as j:
                        for k in range(2):
                            it = 2 * j + k
                            dv.wait(act, "yc_l", it)
                            ac.did(act.activation(sq[:], y3[:, k, 0, :], ACT.Square), "sq")
                            pe_.wait(act, "var", it)
                            ac.did(act.activation(rs[:, 0:CTX], ps[:, 1, 0, 0:CTX], ACT.Ln, scale=1.0 / HD_A, bias=eps[:]), "ln_c")
                            ac.did(act.activation(rs[:, CTX:T], lat(ps[:, 1]), ACT.Ln, scale=1.0 / HD_A, bias=eps[:]), "ln_l")
                            ac.wait(act, "ln_l", it)
                            ac.did(act.activation(rs[:], rs[:], ACT.Exp, scale=-0.5), "rs")

                @block.vector
                def _(dve):
                    dve.memset(eps[:], RWKV_LN_EPS).then_inc(s["eps_set"], 1)
                    with dve.Fori(0, 2) as j:
                        for k in range(2):
                            it = 2 * j + k
                            y, yb, bn = [y3[:, k, i, :] for i in range(3)]
                            dv.wait_before(dve, it)
                            dv.did(dve.tensor_copy(lnp[:], par[:, :, bass.ds(it, 1)].rearrange("p g o -> p (g o)")), "par")
                            dve.wait_ge(loaded[k], j * 64 + 64)
                            dv.did(dve.tensor_tensor(y, y, yb, ALU.add), "y")
                            pe_.wait(dve, "sum", it)
                            for n, (x, z), p in (("c", (0, CTX), ps[:, 0, 0, 0:CTX]), ("l", (CTX, T), lat(ps[:, 0]))):
                                dv.did(dve.scalar_tensor_tensor(out=y[:, x:z], in0=p, scalar=-1.0 / HD_A, in1=y[:, x:z],
                                                                op0=ALU.mult, op1=ALU.add), f"yc_{n}")
                            ac.wait(dve, "rs", it)
                            dv.did(dve.tensor_tensor(y, y, rs[:], ALU.mult), "yn")
                            dv.wait(dve, "yn", it)
                            dv.did(dve.tensor_scalar(y, y, lnp[:, 0:1], lnp[:, 1:2], ALU.mult, ALU.add), "ya")
                            dv.wait(dve, "ya", it)
                            dv.did(dve.tensor_tensor(y, y, bn, ALU.add), "yb")
                            dv.wait(dve, "yb", it)
                            pe_.wait(dve, "g", it)
                            for n, (x, z), p in (("c", (0, CTX), ps[:, 0, 0, 0:CTX]), ("l", (CTX, T), lat(ps[:, 0]))):
                                dv.did(dve.tensor_tensor(HT[:, it, x:z], y[:, x:z], p, ALU.mult), f"o_{n}")


def gdn_post_phase(nc, K, zc, oscan):
    HT, PT = K["HT"], K["PT"]
    with ExitStack() as ctx:
        o3 = sbuf(ctx, nc, "o_fwd_bwd_gate", [P, 2, 3, T])
        sq = sbuf(ctx, nc, "o_sq", [P, T])
        rs = sbuf(ctx, nc, "o_rstd", [P, T])
        eps = sbuf(ctx, nc, "o_eps", [P, 1])
        ps = psum(ctx, nc, "gpost_ps", [P, 3, 512])
        with phase(nc, "in0", "in1", "dve", "act", "pe", "eps_set") as s:
            dv = Steps(s["dve"], ["o", "on", "out"])
            ac = Steps(s["act"], ["silu", "sq", "ln_c", "ln_l", "rs"])
            pe_ = Steps(s["pe"], ["sum"])
            loaded = [s["in0"], s["in1"]]
            with nc.Block() as block:
                @block.sync
                def _(sp):
                    for h in range(4):
                        if h >= 2:
                            dv.wait(sp, "out", h - 2)
                        for i, src in enumerate((oscan[0, h], oscan[1, h], zc[27 + h])):
                            sp.dma_start(o3[:, h % 2, i, :], src).then_inc(loaded[h % 2], 16)

                @block.tensor
                def _(pe):
                    with pe.Fori(0, 4) as it:
                        ac.wait(pe, "sq", it)
                        for b, (x, y) in banks():
                            mm = pe.matmul(ps[:, b, 0:y - x], K["ones"][:], sq[:, x:y], start=True, stop=True)
                        pe_.did(mm, "sum")

                @block.scalar
                def _(act):
                    act.wait_ge(s["eps_set"], 1)
                    with act.Fori(0, 2) as j:
                        for k in range(2):
                            it = 2 * j + k
                            act.wait_ge(loaded[k], j * 48 + 48)
                            ac.did(act.activation(o3[:, k, 2, :], o3[:, k, 2, :], ACT.Silu), "silu")
                            dv.wait(act, "o", it)
                            ac.did(act.activation(sq[:], o3[:, k, 0, :], ACT.Square), "sq")
                            pe_.wait(act, "sum", it)
                            ac.did(act.activation(rs[:, 0:CTX], ps[:, 0, 0:CTX], ACT.Ln, scale=1.0 / HD_B, bias=eps[:]), "ln_c")
                            ac.did(act.activation(rs[:, CTX:T], lat(ps), ACT.Ln, scale=1.0 / HD_B, bias=eps[:]), "ln_l")
                            ac.wait(act, "ln_l", it)
                            ac.did(act.activation(rs[:], rs[:], ACT.Exp, scale=-0.5), "rs")

                @block.vector
                def _(dve):
                    dve.memset(eps[:], RMS_EPS).then_inc(s["eps_set"], 1)
                    with dve.Fori(0, 2) as j:
                        for k in range(2):
                            it = 2 * j + k
                            o, ob, gt = [o3[:, k, i, :] for i in range(3)]
                            dve.wait_ge(loaded[k], j * 48 + 48)
                            dv.did(dve.tensor_tensor(o, o, ob, ALU.add), "o")
                            ac.wait(dve, "rs", it)
                            dv.did(dve.tensor_tensor(o, o, rs[:], ALU.mult), "on")
                            dv.wait(dve, "on", it)
                            dv.did(dve.scalar_tensor_tensor(out=HT[:, 4 + it, :], in0=o, scalar=PT[:, C_GDN:C_GDN + 1], in1=gt,
                                                            op0=ALU.mult, op1=ALU.mult), "out")


def mlstm_prep_phase(nc, A, K, ztail, m_out):
    MN, MC, WE = K["MN"], K["MC"], K["WE"]
    with ExitStack() as ctx:
        g = sbuf(ctx, nc, "gates", [8, 4, T])
        t0 = sbuf(ctx, nc, "softplus", [8, 2, T])
        bs = sbuf(ctx, nc, "b_sum", [8, 2, T])
        en = sbuf(ctx, nc, "minus_m", [8, 2, T])
        wi = sbuf(ctx, nc, "m_minus_M", [8, 2, T])
        reset = sbuf(ctx, nc, "ml_reset", [8, 2, T])
        gb = sbuf(ctx, nc, "gate_bias", [8, 4])
        m0 = sbuf(ctx, nc, "m_latent", [8, 2])
        mp = sbuf(ctx, nc, "m_before", [8, 2, NCH + 1])
        me = sbuf(ctx, nc, "m_ctx_end", [8, 2])
        we = sbuf(ctx, nc, "w_end", [8, 2, NCH])
        pc = psum(ctx, nc, "ml_cols", [P, 512])
        pw = psum(ctx, nc, "ml_we", [P, 512])
        with phase(nc, "in", "bias_in", "bias_ok", "tanh", "abs_ready", "sp", "rows", "we_ok", "cols", "we_ps", "link_d",
                   "link_a", "m_stored", "ctx_m") as s:
            with nc.Block() as block:
                @block.sync
                def _(sp):
                    sp.dma_start(g[:], ztail.rearrange("(g h) t -> h g t", g=4)).then_inc(s["in"], 16)
                    sp.dma_start(gb[:], A["ml_gate_b"].rearrange("l (g h) -> h (l g)", g=4),
                                 allow_slow_non_contiguous=True).then_inc(s["bias_in"], 16)
                    sp.dma_start(m0[:], A["state_mlstm_m"].rearrange("a l d h -> h (a l d)"),
                                 allow_slow_non_contiguous=True).then_inc(s["bias_in"], 16)
                    sp.wait_ge(s["ctx_m"], 1)
                    sp.dma_start(m_out.rearrange("a l d h -> h (a l d)"), me[:],
                                 allow_slow_non_contiguous=True).then_inc(s["m_stored"], 16)
                    sp.wait_ge(s["m_stored"], 16)

                @block.scalar
                def _(act):
                    link = chain(act, s["link_a"])
                    act.wait_ge(s["bias_ok"], 1)
                    act.wait_ge(s["in"], 16)
                    for i in range(4):
                        act.activation(g[:, i], g[:, i], ACT.Tanh, scale=1.0 / GATE_CAP, bias=gb[:, i:i + 1]).then_inc(s["tanh"], 1)
                    act.wait_ge(s["abs_ready"], 1)
                    link(act.activation(t0[:], g[:, 2:4], ACT.Abs))
                    link(act.activation(t0[:], t0[:], ACT.Exp, scale=-1.0))
                    link(act.activation(t0[:], t0[:], ACT.Ln, bias=1.0))
                    act.nop().then_inc(s["sp"], 1)
                    act.wait_ge(s["rows"], 1)
                    link(act.activation(we[:], we[:], ACT.Exp))
                    act.nop().then_inc(s["we_ok"], 1)
                    act.wait_ge(s["cols"], 1)
                    cols = pc[:, 0:NCH * 48].rearrange("p (c w x) -> p c w x", c=NCH, w=3)
                    out = MC[:].rearrange("p c w d h -> p c w (d h)")
                    link(act.activation(out[:, :, 0, :], cols[:, :, 0, :], ACT.Copy))
                    link(act.activation(out[:, :, 1:3, :], cols[:, :, 1:3, :], ACT.Exp))
                    act.wait_ge(s["we_ps"], 1)
                    link(act.activation(WE[:].rearrange("p q d c -> p (q d c)"), pw[:, 0:8 * NCH], ACT.Copy))

                @block.vector
                def _(dve):
                    link = chain(dve, s["link_d"])
                    dve.wait_ge(s["bias_in"], 32)
                    link(dve.tensor_scalar(gb[:], gb[:], 1.0 / GATE_CAP, None, ALU.mult))
                    dve.nop().then_inc(s["bias_ok"], 1)
                    link(dve.memset(reset[:], 1.0))
                    for d in range(2):
                        link(dve.memset(chunked(reset[:, d, :])[:, :, d * (P - 1):d * (P - 1) + 1], 0.0))
                    link(dve.memset(mp[:], 0.0))
                    for d in range(2):
                        link(dve.tensor_copy(mp[:, d, 1:2], m0[:, d:d + 1]))
                    dve.wait_ge(s["tanh"], 4)
                    link(dve.tensor_scalar(g[:], g[:], GATE_CAP, None, ALU.mult))
                    dve.nop().then_inc(s["abs_ready"], 1)
                    dve.wait_ge(s["sp"], 1)
                    link(dve.scalar_tensor_tensor(out=g[:, 2:4], in0=g[:, 2:4], scalar=0.0, in1=t0[:], op0=ALU.min,
                                                  op1=ALU.subtract))
                    for d in range(2):
                        sd = -1 if d else 1
                        link(dve.tensor_tensor_scan(bs[:, d, ::sd], reset[:, d, ::sd], g[:, 2 + d, ::sd], 0.0,
                                                    ALU.mult, ALU.add))
                    link(dve.tensor_tensor(g[:, 0:2], g[:, 0:2], bs[:], ALU.subtract))
                    for n in range(NCH):
                        for d in range(2):
                            c = n if (n == 0 or d == 0) else NCH - n
                            x = slice(c * P, c * P + P)
                            sd = -1 if d else 1
                            e = c * P + (0 if d else P - 1)
                            a, M = g[:, d, x][:, ::sd], MN[:, d, x][:, ::sd]
                            link(dve.tensor_tensor_scan(M, a, a, mp[:, d, n:n + 1], ALU.max, ALU.max))
                            link(dve.tensor_scalar(wi[:, d, x], MN[:, d, x], -1.0, mp[:, d, n:n + 1], ALU.mult, ALU.add))
                            if n == 0:
                                link(dve.tensor_tensor(me[:, d:d + 1], bs[:, d, e:e + 1], MN[:, d, e:e + 1], ALU.add))
                            else:
                                link(dve.tensor_tensor(mp[:, d, n + 1:n + 2], bs[:, d, e:e + 1], MN[:, d, e:e + 1], ALU.add))\
                                    if n < NCH - 1 else None
                        if n == 0:
                            dve.nop().then_inc(s["ctx_m"], 1)
                    for d in range(2):
                        e = chunked(wi[:, d])[:, :, (0 if d else P - 1):(1 if d else P)]
                        link(dve.tensor_copy(we[:, d, :], e.rearrange("p c o -> p (c o)")))
                    link(dve.scalar_tensor_tensor(out=en[:], in0=MN[:], scalar=-1.0, in1=bs[:], op0=ALU.mult, op1=ALU.subtract))
                    link(dve.tensor_scalar(MN[:], MN[:], -1.0, None, ALU.mult))
                    dve.nop().then_inc(s["rows"], 1)

                @block.tensor
                def _(pe):
                    pe.wait_ge(s["rows"], 1)
                    for c in range(NCH):
                        for w, src in enumerate((g, wi, en)):
                            for d in range(2):
                                o = c * 48 + w * 16 + d * 8
                                mm = pe.transpose(pc[:, o:o + 8], src[:, d, c * P:c * P + P], K["ident"][0:8, 0:8])
                    mm.then_inc(s["cols"], 1)
                    pe.wait_ge(s["we_ok"], 1)
                    for q in range(4):
                        mm = pe.matmul(pw[:, q * 2 * NCH:(q + 1) * 2 * NCH], K["selpair"][:, q, :],
                                       we[:].rearrange("p d c -> p (d c)"), start=True, stop=True)
                    mm.then_inc(s["we_ps"], 1)


V1 = DV_C + 1


def mlstm_scan_phase(nc, K, zc, hscan, steps, state):
    MN, MC, WE = K["MN"], K["MC"], K["WE"]
    with ExitStack() as ctx:
        kq = sbuf(ctx, nc, "kq", [P, 4, 2, 2, P])
        vv = sbuf(ctx, nc, "mv", [P, 4, 2, 2, P])
        Wt, Wm, St = [sbuf(ctx, nc, n, [P, 2, 2, 2, P]) for n in ("w_raw", "w_intra", "s_intra")]
        Ht = sbuf(ctx, nc, "h_tok", [P, 4, 2, 2, P])
        kt = sbuf(ctx, nc, "mk_tok", [P, 2, 2, 2, 64])
        vt, NI = [sbuf(ctx, nc, n, [P, 2, 2, 2, V1]) for n in ("mv_tok", "num_inter")]
        den = sbuf(ctx, nc, "den", [P, 2, 2, 2])
        cs = sbuf(ctx, nc, "ml_cols", [P, 3, 2, 8])
        mn = sbuf(ctx, nc, "ml_rows", [8, 2, P])
        we = sbuf(ctx, nc, "ml_wend", [P, 2, 4])
        ps = psum(ctx, nc, "mscan_ps", [P, 2, 4, 512])
        lanes = [(h, d) for h in range(2) for d in range(2)]
        with phase(nc, "dve", "act", "pool", "pe", "ones_set", *[f"in{q}" for q in range(4)], *[f"out{q}" for q in range(4)]) as s:
            dv, ac, po, pe_ = scan_steps(s, 4, ["mb", "tok", "a"], [["num", "inter"], ["c"]],
                                         ["w0", "k", "s"], [["tot", "abs", "max", "rec", "h"], ["C"]],
                                         ["W", "v"], [["I"]],
                                         dve_head=["cs0", "cs1", "mn0", "mn1", "we0", "we1"], inverse=False)
            po.names[:] = [f"{q}wm" for q in range(4)]
            loaded = [s[f"in{q}"] for q in range(4)]
            stored = [s[f"out{q}"] for q in range(4)]
            z_src = zc.rearrange("m p (c t) -> m c p t", t=P)
            with nc.Block() as block:
                @block.sync
                def _(sp):
                    def body(it, cc, wait):
                        for q in range(4):
                            for d in range(2):
                                early(sp, z_src[4 + q, cc[d]], z_src[q, cc[d]], z_src[8 + 2 * q, cc[d]], z_src[9 + 2 * q, cc[d]])
                        for q in range(4):
                            if wait:
                                pe_.wait(sp, f"{q}inter", it - 1)
                            for d in range(2):
                                sp.dma_start(kq[:, q, d, 0, :], z_src[4 + q, cc[d]]).then_inc(loaded[q], 16)
                                sp.dma_start(kq[:, q, d, 1, :], z_src[q, cc[d]]).then_inc(loaded[q], 16)
                                for h in range(2):
                                    sp.dma_start(vv[:, q, h, d, :], z_src[8 + 2 * q + h, cc[d]]).then_inc(loaded[q], 16)
                    if steps == 1:
                        body(0, (0, 0), False)
                    else:
                        body(0, (1, steps), False)
                        with sp.Fori(1, steps) as it:
                            body(it, (it + 1, steps - it), True)

                @block.tensor
                def _(pe):
                    def body(it, c0, c1):
                        dv.wait(pe, "mn1", it)
                        for a in (0, 2):
                            for q in (a, a + 1):
                                g = q - a
                                if a == 0:
                                    dv.wait_before(pe, it)
                                    ac.wait_before(pe, it)
                                else:
                                    dv.wait(pe, f"{g}C", it)
                                for i, (h, d) in enumerate(lanes):
                                    mm = pe.matmul(ps[:, g, 0, i * P:i * P + P], K["sel"][:, 2 * q + h, :], mn[:, d, :],
                                                   start=True, stop=True)
                                pe_.did(mm, f"{q}mb")
                                pe.wait_ge(loaded[q], it * 128 + 128)
                                for d in range(2):
                                    pe.transpose(ps[:, g, 1, d * P:d * P + P], kq[:, q, d, 0, :], K["ident"][:])
                                for i, (h, d) in enumerate(lanes):
                                    mm = pe.transpose(ps[:, g, 2, i * P:i * P + P], vv[:, q, h, d, :], K["ident"][:])
                                pe_.did(mm, f"{q}tok")
                                for h, o in ((0, ps[:, g, 1, 256:512]), (1, ps[:, g, 3, 0:256])):
                                    x = slice(64 * h, 64 * h + 64)
                                    for d in range(2):
                                        mm = pe.matmul(o[:, d * P:d * P + P], kq[x, q, d, 0, :], kq[x, q, d, 1, :],
                                                       start=True, stop=True)
                                pe_.did(mm, f"{q}a")
                            for q in (a, a + 1):
                                g = q - a
                                dv.wait(pe, f"{q}s", it)
                                ac.wait(pe, f"{q}v", it)
                                for h in range(2):
                                    for d in range(2):
                                        mm = pe.matmul(ps[:, g, 2 + h, d * V1:d * V1 + V1], St[:, g, h, d, :], vt[:, g, h, d, :],
                                                       start=True, stop=True)
                                pe_.did(mm, f"{q}num")
                                for h in range(2):
                                    x = slice(64 * h, 64 * h + 64)
                                    for d in range(2):
                                        mm = pe.matmul(ps[:, g, h, d * V1:d * V1 + V1], kq[x, q, d, 1, :], state[x, q, d, :],
                                                       start=True, stop=True)
                                pe_.did(mm, f"{q}inter")
                            for q in (a, a + 1):
                                g = q - a
                                ac.wait(pe, f"{q}I", it)
                                for h in range(2):
                                    x = slice(64 * h, 64 * h + 64)
                                    for d in range(2):
                                        mm = pe.matmul(ps[x, g, 0, d * V1:d * V1 + V1], kt[:, g, h, d, :], vt[:, g, h, d, :],
                                                       start=True, stop=True)
                                pe_.did(mm, f"{q}c")
                    scan_iterations(pe, steps, body)

                @block.scalar
                def _(act):
                    act.wait_ge(s["ones_set"], 1)

                    def body(it, c0, c1):
                        for a in (0, 2):
                            for q in (a, a + 1):
                                g = q - a
                                dv.wait(act, f"{q}w0", it)
                                ac.did(act.activation(four(Wt[:, g]), four(Wt[:, g]), ACT.Exp), f"{q}W")
                                pe_.wait(act, f"{q}tok", it)
                                ac.did(act.activation(vt[:, g, :, :, 0:P].rearrange("p h d v -> p (h d) v"),
                                                      ps[:, g, 2, :].rearrange("p (l v) -> p l v", v=P), ACT.Copy), f"{q}v")
                            for q in (a, a + 1):
                                g = q - a
                                pe_.wait(act, f"{q}inter", it)
                                for h, d in lanes:
                                    ins = act.activation(NI[:, g, h, d, :], ps[:, g, h, d * V1:d * V1 + V1], ACT.Copy,
                                                         scale=cs[:, 1, d, 2 * q + h:2 * q + h + 1])
                                ac.did(ins, f"{q}I")
                            for q in (a, a + 1):
                                dv.wait(act, f"{q}h", it)
                                for d, c in enumerate((c0, c1)):
                                    act.dma_start(hscan[d, c][:, q * 256:q * 256 + 256],
                                                  Ht[:, q, d].rearrange("p h v -> p (h v)")).then_inc(stored[q], 16)
                    scan_iterations(act, steps, body)
                    for q in range(4):
                        act.wait_ge(stored[q], steps * 32)

                @block.vector
                def _(dve):
                    dve.memset(vt[:], 1.0).then_inc(s["ones_set"], 1)

                    def body(it, c0, c1):
                        dv.wait_before(dve, it)
                        ac.wait_before(dve, it)
                        pe_.wait_before(dve, it)
                        for d, c in enumerate((c0, c1)):
                            dv.did(dve.tensor_copy(cs[:, :, d, :], MC[:, bass.ds(c, 1), :, d, :].rearrange("p o w h -> p (o w) h")),
                                   f"cs{d}")
                        for d, c in enumerate((c0, c1)):
                            dv.did(dve.tensor_copy(mn[:, d, :], MN[:, d, bass.ds(c * P, P)]), f"mn{d}")
                        for d, c in enumerate((c0, c1)):
                            dv.did(dve.tensor_copy(we[:, d, :], WE[:, :, d, bass.ds(c, 1)].rearrange("p q o -> p (q o)")), f"we{d}")
                        dv.wait(dve, "we1", it)
                        for a in (0, 2):
                            for q in (a, a + 1):
                                g = q - a
                                pe_.wait(dve, f"{q}mb", it)
                                for i, (h, d) in enumerate(lanes):
                                    ins = dve.tensor_scalar(Wt[:, g, h, d, :], ps[:, g, 0, i * P:i * P + P],
                                                            cs[:, 0, d, 2 * q + h:2 * q + h + 1], 0.0, ALU.add, ALU.min)
                                dv.did(ins, f"{q}w0")
                                po.wait(dve, f"{q}wm", it)
                                pe_.wait(dve, f"{q}a", it)
                                for h, d in lanes:
                                    e = 0 if d else P - 1
                                    ins = dve.tensor_scalar(kt[:, g, h, d, :], ps[:, g, 1, d * P + 64 * h:d * P + 64 * h + 64],
                                                            Wm[:, g, h, d, e:e + 1], DK_C ** -0.5, ALU.mult, ALU.mult)
                                dv.did(ins, f"{q}k")
                                for h, o in ((0, ps[:, g, 1, 256:512]), (1, ps[:, g, 3, 0:256])):
                                    ins = dve.scalar_tensor_tensor(out=St[:, g, h].rearrange("p d t -> p (d t)"), in0=o,
                                                                   scalar=DK_C ** -0.5,
                                                                   in1=Wm[:, g, h].rearrange("p d t -> p (d t)"),
                                                                   op0=ALU.mult, op1=ALU.mult)
                                dv.did(ins, f"{q}s")
                            for q in (a, a + 1):
                                g = q - a
                                ac.wait(dve, f"{q}I", it)
                                pe_.wait(dve, f"{q}num", it)
                                for h in range(2):
                                    v = NI[:, g, h].rearrange("p d v -> p (d v)")
                                    ins = dve.tensor_tensor(v, v, ps[:, g, 2 + h, 0:2 * V1], ALU.add)
                                dv.did(ins, f"{q}tot")
                                dv.wait(dve, f"{q}tot", it)
                                dv.did(dve.scalar_tensor_tensor(out=den[:, g], in0=NI[:, g, :, :, P], scalar=-1.0,
                                                                in1=NI[:, g, :, :, P], op0=ALU.mult, op1=ALU.max), f"{q}abs")
                                dv.wait(dve, f"{q}abs", it)
                                dv.did(dve.tensor_tensor(den[:, g], den[:, g], cs[:, 2, :, 2 * q:2 * q + 2].rearrange("p d h -> p h d"),
                                                         ALU.max), f"{q}max")
                                dv.wait(dve, f"{q}max", it)
                                dv.did(dve.reciprocal(den[:, g], den[:, g]), f"{q}rec")
                                dv.wait(dve, f"{q}rec", it)
                                dve.wait_ge(stored[q], it * 32)
                                dv.did(dve.tensor_tensor(Ht[:, q].rearrange("p d h v -> p h d v"), NI[:, g, :, :, 0:P],
                                                         den[:, g, :, :, None].to_broadcast([P, 2, 2, P]), ALU.mult), f"{q}h")
                            for q in (a, a + 1):
                                pe_.wait(dve, f"{q}c", it)
                                for d in range(2):
                                    ins = dve.scalar_tensor_tensor(out=state[:, q, d, :], in0=state[:, q, d, :],
                                                                   scalar=we[:, d, q:q + 1], in1=ps[:, q - a, 0, d * V1:d * V1 + V1],
                                                                   op0=ALU.mult, op1=ALU.add)
                                dv.did(ins, f"{q}C")
                    scan_iterations(dve, steps, body)

                @block.gpsimd
                def _(pool):
                    def body(it, c0, c1):
                        for q in range(4):
                            g = q % 2
                            ac.wait(pool, f"{q}W", it)
                            if q >= 2:
                                dv.wait(pool, f"{q - 2}s", it)
                            else:
                                dv.wait_before(pool, it)
                            po.did(pool.tensor_tensor(Wm[:, g], Wt[:, g], K["order"][:, None, :, 1, :].to_broadcast([P, 2, 2, P]),
                                                      ALU.mult), f"{q}wm")
                    scan_iterations(pool, steps, body)


def mlstm_post_phase(nc, K, zc, hscan):
    HT, PT = K["HT"], K["PT"]
    with ExitStack() as ctx:
        h2 = sbuf(ctx, nc, "h_fwd_bwd", [P, 2, 2, D])
        og = sbuf(ctx, nc, "o_gate", [P, 2, H_C, P])
        sq = sbuf(ctx, nc, "h_sq", [P, D])
        ss = sbuf(ctx, nc, "h_sum", [P, H_C])
        eps = sbuf(ctx, nc, "h_eps", [P, 1])
        ps = psum(ctx, nc, "hpost_ps", [P, 2, D])
        with phase(nc, "in0", "in1", "dve", "act", "pe", "eps_set") as s:
            dv = Steps(s["dve"], ["h", "ss", "hn", "out"])
            ac = Steps(s["act"], ["sig", "sq", "ln", "rs"])
            pe_ = Steps(s["pe"], ["t"])
            loaded = [s["in0"], s["in1"]]
            o_src = zc[16:24].rearrange("m p (c t) -> c p m t", t=P)

            def all_chunks(eng, tile):
                with eng.Fori(0, NCH // 2) as j:
                    for k in range(2):
                        tile(2 * j + k, j, k)
                tile(NCH - 1, NCH // 2, 0)
            with nc.Block() as block:
                @block.sync
                def _(sp):
                    def tile(c, k):
                        sp.dma_start(h2[:, k, 0, :], hscan[0, c]).then_inc(loaded[k], 16)
                        sp.dma_start(h2[:, k, 1, :], hscan[1, c]).then_inc(loaded[k], 16)
                        sp.dma_start(og[:, k], o_src[c]).then_inc(loaded[k], 16)
                    tile(0, 0)
                    tile(1, 1)
                    with sp.Fori(1, NCH // 2) as j:
                        early(sp, hscan[0, 2 * j], hscan[1, 2 * j], o_src[2 * j], hscan[0, 2 * j + 1], hscan[1, 2 * j + 1],
                              o_src[2 * j + 1])
                        for k in range(2):
                            dv.wait(sp, "out", 2 * j - 2 + k)
                            tile(2 * j + k, k)
                    dv.wait(sp, "out", NCH - 3)
                    tile(NCH - 1, 0)

                @block.tensor
                def _(pe):
                    def tile(it, j, k):
                        dv.wait(pe, "hn", it)
                        for h in range(H_C):
                            mm = pe.transpose(ps[:, k, h * P:h * P + P], h2[:, k, 0, h * P:h * P + P], K["ident"][:])
                        pe_.did(mm, "t")
                    all_chunks(pe, tile)

                @block.scalar
                def _(act):
                    act.wait_ge(s["eps_set"], 1)

                    def tile(it, j, k):
                        act.wait_ge(loaded[k], j * 48 + 48)
                        ac.did(act.activation(og[:, k], og[:, k], ACT.Sigmoid), "sig")
                        dv.wait(act, "h", it)
                        ac.did(act.activation(sq[:], h2[:, k, 0, :], ACT.Square), "sq")
                        dv.wait(act, "ss", it)
                        ac.did(act.activation(ss[:], ss[:], ACT.Ln, scale=1.0 / DV_C, bias=eps[:]), "ln")
                        ac.wait(act, "ln", it)
                        ac.did(act.activation(ss[:], ss[:], ACT.Exp, scale=-0.5), "rs")
                    all_chunks(act, tile)

                @block.vector
                def _(dve):
                    dve.memset(eps[:], RMS_EPS).then_inc(s["eps_set"], 1)

                    def tile(it, j, k):
                        h, hb = h2[:, k, 0, :], h2[:, k, 1, :]
                        dve.wait_ge(loaded[k], j * 48 + 48)
                        dv.did(dve.tensor_tensor(h, h, hb, ALU.add), "h")
                        ac.wait(dve, "sq", it)
                        dv.did(dve.tensor_reduce(ss[:], sq[:].rearrange("p (h v) -> p h v", h=H_C), AX_X, ALU.add), "ss")
                        ac.wait(dve, "rs", it)
                        dv.did(dve.tensor_tensor(h.rearrange("p (h v) -> p h v", h=H_C), h.rearrange("p (h v) -> p h v", h=H_C),
                                                 ss[:, :, None].to_broadcast([P, H_C, P]), ALU.mult), "hn")
                        pe_.wait(dve, "t", it)
                        x = slice(it * P, it * P + P) if isinstance(it, int) else bass.ds(it * P, P)
                        dv.did(dve.scalar_tensor_tensor(out=HT[:, :, x], in0=ps[:, k, :].rearrange("p (h t) -> p h t", h=H_C),
                                                        scalar=PT[:, C_MLN:C_MLN + 1], in1=og[:, k], op0=ALU.mult,
                                                        op1=ALU.mult), "out")
                    all_chunks(dve, tile)


def trunk_kernel(nc, A, y_prompt, y_sample, rk_out, gd_out, mc_out, mn_out, mm_out):
    def scratch(name, *shape):
        return nc.dram_tensor(name, list(shape), F32).ap()

    zc = scratch("z_even", AB_T, P, T)
    ztail = scratch("z_even_gates", 16, T)
    units = scratch("rwkv_units", 4, 2, P, NCH, 4, P)
    bonus = scratch("rwkv_bonus", 4, P, T)
    yscan = scratch("rwkv_y", 2, 4, P, T)
    qkv = scratch("gdn_units", 4, P, NCH, 3, P)
    oscan = scratch("gdn_o", 2, 4, P, T)
    zc2 = scratch("z_odd", ML_T, P, T)
    ztail2 = scratch("z_odd_gates", 32, T)
    hscan = scratch("mlstm_h", 2, NCH, P, D)

    with ExitStack() as ctx:
        def keep(name, *shape):
            return sbuf(ctx, nc, name, list(shape))
        K = {
            "ident": keep("ident", P, P), "ones": keep("ones", P, P), "ones64": keep("ones64", P, P),
            "order": keep("order", P, 2, 2, P),
            "sel": keep("sel", 8, 8, P), "selpair": keep("selpair", 8, 4, P),
            "PT": keep("PT", P, PT_COLS), "taps": keep("taps", P, AB_T, 3), "cond": keep("cond", P, KD, 2),
            "mod": keep("mod", P, 2, 6, KD, 2), "gain": keep("gain", P, 2, 2, KD, 2),
            "XT": keep("XT", P, KD, T),
        }
        even = ctx.enter_context(ExitStack())
        K["pairs"] = sbuf(even, nc, "pairs", [P, NL, 2, P])
        setup_phase(nc, A, K)
        adaln_phase(nc, A, K)

        def shift(layer, w):
            return K["mod"][:, layer, 3 * w]

        def gate(layer, w):
            return K["mod"][:, layer, 3 * w + 2]

        with ExitStack() as mixer:
            K["HT"] = sbuf(mixer, nc, "HT", [P, KD, T])
            norm_phase(nc, K, K["HT"], K["gain"][:, 0, 0], shift(0, 0))
            mixer_in_phase(nc, K, A["ab_w_in"][0], AB_T, 16, zc, ztail, K["taps"][:])
            with ExitStack() as c:
                K["EM"] = sbuf(c, nc, "EM", [P, 2, NCH, 4])
                K["GR"] = sbuf(c, nc, "GR", [H_B, 2, T])
                K["GC"] = sbuf(c, nc, "GC", [P, NCH, 3, 2, H_B])
                rk_state = sbuf(c, nc, "rk_state", [P, 4, 2, 64])
                gd_state = sbuf(c, nc, "gd_state", [P, 2, 2, 2, P])
                rwkv_prep_phase(nc, A, K, zc, units, bonus)
                gdn_prep_phase(nc, A, K, zc, ztail, qkv)
                zero_states_phase(nc, [rk_state[:], gd_state[:]])
                rwkv_scan_phase(nc, K, units, zc, yscan, 1, rk_state)
                gdn_scan_phase(nc, K, qkv, oscan, 1, gd_state)
                with ExitStack() as t:
                    outs, ins = even_states(nc, t, A, rk_out, gd_out, rk_state, gd_state)
                    turn_states_phase(nc, K, outs, ins)
                rwkv_scan_phase(nc, K, units, zc, yscan, NCH - 1, rk_state)
                gdn_scan_phase(nc, K, qkv, oscan, NCH - 1, gd_state)
            rwkv_post_phase(nc, A, K, zc, yscan, bonus)
            gdn_post_phase(nc, K, zc, oscan)
            add_out_phase(nc, K, A["ab_w_out"][0], K["HT"][:], KD, gate(0, 0))
        even.close()
        for layer in range(2):
            if layer == 1:
                with ExitStack() as mixer:
                    K["HT"] = sbuf(mixer, nc, "HT", [P, KD, T])
                    norm_phase(nc, K, K["HT"], K["gain"][:, 1, 0], shift(1, 0))
                    mixer_in_phase(nc, K, A["ml_w_in"][0], ML_T, 32, zc2, ztail2, None)
                    with ExitStack() as c:
                        K["MN"] = sbuf(c, nc, "MN", [H_C, 2, T])
                        K["MC"] = sbuf(c, nc, "MC", [P, NCH, 3, 2, H_C])
                        K["WE"] = sbuf(c, nc, "WE", [P, 4, 2, NCH])
                        ml_state = sbuf(c, nc, "ml_state", [P, 4, 2, V1])
                        mlstm_prep_phase(nc, A, K, ztail2, mm_out)
                        zero_states_phase(nc, [ml_state[:]])
                        mlstm_scan_phase(nc, K, zc2, hscan, 1, ml_state)
                        with ExitStack() as t:
                            outs, ins = odd_states(nc, t, A, mc_out, mn_out, ml_state)
                            turn_states_phase(nc, K, outs, ins)
                        mlstm_scan_phase(nc, K, zc2, hscan, NCH - 1, ml_state)
                    mlstm_post_phase(nc, K, zc2, hscan)
                    add_out_phase(nc, K, A["ml_w_out"][0], K["HT"][:], KD, gate(1, 0))
            with ExitStack() as ffn:
                K["G"] = sbuf(ffn, nc, "G", [P, FT, T])
                with ExitStack() as c:
                    K["HT"] = sbuf(c, nc, "HT", [P, KD, T])
                    norm_phase(nc, K, K["HT"], K["gain"][:, layer, 1], shift(layer, 1))
                    ffn_in_phase(nc, A, K, layer)
                add_out_phase(nc, K, A["ffn_w_out"][layer], K["G"][:], FT, gate(layer, 1))
        K["HT"] = keep("HT", P, KD, T)
        fin = K["PT"][:, C_FIN:C_FIN + KD, None].to_broadcast([P, KD, 2])
        norm_phase(nc, K, K["HT"], fin, None)
        store_out_phase(nc, K, y_prompt, y_sample)


_INS = ["x_prompt", "x_sample", "state_rwkv", "state_gdn", "state_mlstm_c", "state_mlstm_n", "state_mlstm_m", "c", "c_ctx",
        "ada_w", "ada_b", "norm1_g", "norm2_g", "ab_w_in", "ab_w_out", "rk_mu", "rk_w0", "rk_w_up", "rk_a0", "rk_a_up",
        "rk_g_up", "rk_k_k", "rk_k_a", "rk_r_k", "rk_ln_g", "rk_ln_b", "gd_conv_w", "gd_a_log", "gd_dt_bias", "gd_norm_g",
        "ml_w_in", "ml_gate_b", "ml_norm_g", "ml_w_out", "ffn_w_in", "ffn_conv_w", "ffn_conv_b", "ffn_w_out", "final_g"]
_OUTS = [(1, CTX, D), (1, LAT, D), (1, 1, 2, H_A, HD_A, HD_A), (1, 1, 2, H_B, HD_B, HD_B), (1, 1, 2, H_C, DV_C, DK_C),
         (1, 1, 2, H_C, DK_C), (1, 1, 2, H_C)]


def kernel(**inputs):
    import numpy as _np
    import concourse.bacc as _bacc
    from concourse.bass_utils import run_bass_kernel_spmd as _run

    nc = _bacc.Bacc("TRN2", target_bir_lowering=False, num_devices=1)
    arrays, A = {}, {}
    for name in _INS:
        a = _np.ascontiguousarray(inputs[name])
        arrays[f"in_{name}_dram"] = a
        A[name] = nc.dram_tensor(f"in_{name}_dram", a.shape, F32, kind="ExternalInput").ap()
    outs = [nc.dram_tensor(f"out_{i}_dram", shape, F32, kind="ExternalOutput").ap() for i, shape in enumerate(_OUTS)]
    trunk_kernel(nc, A, *outs)
    r = _run(nc, [arrays], core_ids=[0])
    return tuple(r.results[0][f"out_{i}_dram"] for i in range(len(_OUTS)))
```

```python
from contextlib import ExitStack, contextmanager

import numpy as np
import concourse.bass as bass
import concourse.mybir as mybir

F32 = mybir.dt.float32
ACT = mybir.ActivationFunctionType
ALU = mybir.AluOpType
AX_X = mybir.AxisListType.X

P = 128
D = 1024
KD = D // P
CTX = 128
LAT = 1024
T = CTX + LAT
NCH = T // P
GRID = 64
ROWS = LAT // GRID
HD_A, H_A = 64, 8
HD_B, H_B = 128, 4
DK_C, DV_C, H_C = 64, 128, 8
PA_T = 15
PB_T = 16
QKV_T = 12
AB_T = PA_T + PB_T
ML_T = 24
DFF = 2816
FT = DFF // P
RMS_EPS = 1e-6
RWKV_LN_EPS = 64e-5
GATE_CAP = 15.0
LEVELS = [1, 2, 4, 8, 16, 32, 64]
EXP_HALF = float(np.exp(-0.5))

C_ADAB, C_N1, C_N2 = 0, 96, 112
C_FIN, C_MU, C_W0, C_A0, C_KK, C_KA, C_RK, C_LNG, C_LNB, C_CONV, C_GDN, C_MLN = (
    128, 136, 151, 159, 167, 171, 175, 179, 183, 187, 223, 224)
C_FFW, C_FFB = 256, 256 + 2 * 9 * FT
PT_COLS = 6 * P


@contextmanager
def phase(nc, *names):
    sems = {n: nc.alloc_semaphore(f"{n}_{nc.next_id()}") for n in names}
    yield sems
    nc.clear_and_free_semaphores(list(sems.values()))
    nc.all_engine_barrier()


def early(eng, *aps):
    for ap in aps:
        if not isinstance(ap.offset, int):
            eng.lower_val(ap.offset * 4)


def chain(eng, sem):
    n = [0]

    def link(ins):
        n[0] += 1
        ins.then_inc(sem, 1)
        eng.wait_ge(sem, n[0])
    return link


def sbuf(ctx, nc, name, shape):
    return ctx.enter_context(nc.sbuf_tensor(f"{name}_{nc.next_id()}", shape, F32))


def psum(ctx, nc, name, shape):
    return ctx.enter_context(nc.psum_tensor(f"{name}_{nc.next_id()}", shape, F32))


F32R = mybir.dt.float32r


def upper(eng, out, x):
    return eng.tensor_copy(out.bitcast(F32R), x)


def lower(eng, out, x, up):
    return eng.tensor_tensor(out.bitcast(F32R), x, up, ALU.subtract)


def matmul_split(pe, out, w, x, first, last):
    for n, (a, b) in enumerate(((0, 0), (0, 1), (1, 0))):
        for o, r in zip(out, x(b)):
            mm = pe.matmul(o, w(a).bitcast(F32R), r.bitcast(F32R), start=(first and n == 0), stop=(last and n == 2))
    return mm


ADA_U = 256
ADA_HEAD = 2 * D
ADA_ITS, ADA_N = 4, 10
assert ADA_HEAD + ADA_ITS * ADA_N * ADA_U == 12 * D


def setup_phase(nc, A, K):
    with ExitStack() as ctx:
        rows = sbuf(ctx, nc, "param_rows", [P, 6, P])
        crow = sbuf(ctx, nc, "cond_rows", [16, P])
        xt = sbuf(ctx, nc, "x_tokens", [P, 3, D])
        pp = psum(ctx, nc, "params_ps", [P, 2, 512])
        pc = psum(ctx, nc, "cond_ps", [P, 512])
        px = psum(ctx, nc, "x_ps", [P, 2, D])
        rowsum = [
            (0, 0, A["ada_b"].rearrange("l (n c) -> (l n) c", c=P)),
            (0, C_N1, A["norm1_g"].rearrange("l (n c) -> (l n) c", c=P)),
            (0, C_N2, A["norm2_g"].rearrange("l (n c) -> (l n) c", c=P)),
            (1, C_FIN, A["final_g"].rearrange("(n c) -> n c", c=P)),
            (1, C_MU, A["rk_mu"].rearrange("l (n c) -> (l n) c", c=P)),
            (1, C_W0, A["rk_w0"].rearrange("l d (n c) -> (l d n) c", c=P)),
            (1, C_A0, A["rk_a0"].rearrange("l d (n c) -> (l d n) c", c=P)),
            (1, C_KK, A["rk_k_k"].rearrange("l (n c) -> (l n) c", c=P)),
            (1, C_KA, A["rk_k_a"].rearrange("l (n c) -> (l n) c", c=P)),
            (1, C_RK, A["rk_r_k"].rearrange("l (n a) c -> (l n) (a c)", a=2)),
            (1, C_LNG, A["rk_ln_g"].rearrange("l (n c) -> (l n) c", c=P)),
            (1, C_LNB, A["rk_ln_b"].rearrange("l (n c) -> (l n) c", c=P)),
            (1, C_CONV, A["gd_conv_w"].rearrange("l t (n c) -> (l t n) c", c=P)),
            (1, C_GDN, A["gd_norm_g"]),
            (1, C_MLN, A["ml_norm_g"]),
        ]
        ffw = A["ffn_conv_w"].rearrange("l a b (n c) -> (l a b n) c", c=P)
        ffb = A["ffn_conv_b"].rearrange("l (n c) -> (l n) c", c=P)
        nw = ffw.shape[0]
        for g in range(4):
            a, b = g * P, min(g * P + P, nw)
            rowsum.append((2 + g, C_FFW + a, ffw[a:b, :]))
        rowsum.append((5, C_FFB, ffb))
        xs = A["x_sample"].rearrange("b (n p) c -> (b n) p c", p=P)
        xp = A["x_prompt"].rearrange("b p c -> (b p) c")
        with phase(nc, "rows_in", "cond_in", "x_in0", "x_in1", "x_in2", "consts", "pool_chain", "turned",
                   "table", "cond_turned", "cond_silu", "x_turned0", "x_turned1", "x_out0", "x_out1",
                   "dve_chain", "zeroed", "ada_in") as s:
            x_in = [s["x_in0"], s["x_in1"], s["x_in2"]]
            x_turned = [s["x_turned0"], s["x_turned1"]]
            x_out = [s["x_out0"], s["x_out1"]]
            with nc.Block() as block:
                @block.sync
                def _(sp):
                    sp.wait_ge(s["zeroed"], 1)
                    for g, col, src in rowsum:
                        r = col - g * P
                        sp.dma_start(rows[r:r + src.shape[0], g, :], src).then_inc(s["rows_in"], 16)
                    sp.dma_start(crow[0:8, :], A["c_ctx"].rearrange("(k c) -> k c", c=P)).then_inc(s["cond_in"], 16)
                    sp.dma_start(crow[8:16, :], A["c"].rearrange("b (k c) -> (b k) c", c=P)).then_inc(s["cond_in"], 16)
                    sp.dma_start(xt[:, 2, :], xp).then_inc(x_in[2], 16)
                    with sp.Fori(0, 4) as j:
                        early(sp, xs[2 * j], xs[2 * j + 1])
                        for k in range(2):
                            sp.wait_ge(x_turned[k], j)
                            sp.dma_start(xt[:, k, :], xs[2 * j + k]).then_inc(x_in[k], 16)

                @block.gpsimd
                def _(pool):
                    link = chain(pool, s["pool_chain"])
                    link(pool.memset(K["ident"][:], 0.0))
                    link(pool.affine_select(out=K["ident"][:], in_=K["ident"][:], compare_op=ALU.not_equal, fill=1.0,
                                            base=0, pattern=[[-1, P]], channel_multiplier=1))
                    pool.nop().then_inc(s["consts"], 1)
                    link(pool.memset(K["ones"][:], 1.0))
                    link(pool.memset(K["ones64"][:], 1.0))
                    for lo, hi, cm, step, base in ((0, 64, -1, 0, 63), (64, 128, 1, 0, -64)):
                        link(pool.affine_select(out=K["ones64"][:, lo:hi], in_=K["ones64"][:, lo:hi],
                                                compare_op=ALU.is_ge, fill=0.0, base=base, pattern=[[0, 64]],
                                                channel_multiplier=cm))
                    link(pool.memset(K["order"][:], 1.0))
                    for d in range(2):
                        sg = 1 - 2 * d
                        for q, op in ((0, ALU.is_gt), (1, ALU.is_ge)):
                            v = K["order"][:, d, q, :]
                            link(pool.affine_select(out=v, in_=v, compare_op=op, fill=0.0, base=0,
                                                    pattern=[[sg, P]], channel_multiplier=-sg))
                    link(pool.memset(K["pairs"][:], 1.0))
                    for n, b in enumerate(LEVELS):
                        nb = P // (2 * b)
                        for d in range(2):
                            v = K["pairs"][:, n, d, :].rearrange("p (x y) -> p x y", x=nb)
                            lo, hi = (0, b - 1) if d == 0 else (b, 2 * b - 1)
                            for base, pat, cm in ((-lo, [[-2 * b, nb], [0, 2 * b]], 1),
                                                  (hi, [[2 * b, nb], [0, 2 * b]], -1),
                                                  (-b, [[0, nb], [1, 2 * b]], 0) if d == 0 else
                                                  (b - 1, [[0, nb], [-1, 2 * b]], 0)):
                                link(pool.affine_select(out=v, in_=v, compare_op=ALU.is_ge, fill=0.0, base=base,
                                                        pattern=pat, channel_multiplier=cm))
                    link(pool.memset(K["sel"][:], 0.0))
                    link(pool.affine_select(out=K["sel"][:], in_=K["sel"][:], compare_op=ALU.not_equal, fill=1.0,
                                            base=0, pattern=[[-1, 8], [0, P]], channel_multiplier=1))
                    link(pool.memset(K["selpair"][:], 0.0))
                    v = K["selpair"][:].rearrange("p a (b c) -> p a b c", b=2)
                    link(pool.affine_select(out=v, in_=v, compare_op=ALU.not_equal, fill=1.0, base=0,
                                            pattern=[[-2, 4], [-1, 2], [0, 64]], channel_multiplier=1))

                @block.tensor
                def _(pe):
                    pe.wait_ge(s["consts"], 1)
                    pe.wait_ge(s["cond_in"], 32)
                    pe.transpose(pc[:, 0:16], crow[:, :], K["ident"][0:16, 0:16]).then_inc(s["cond_turned"], 1)
                    pe.wait_ge(s["rows_in"], 16 * len(rowsum))
                    for g in range(6):
                        pe.transpose(pp[:, g // 4, g % 4 * P:g % 4 * P + P], rows[:, g, :],
                                     K["ident"][:]).then_inc(s["turned"], 1)

                    def tile(k, slot, bank, first):
                        if not first:
                            pe.wait_ge(x_out[bank], k)
                        for c in range(KD):
                            mm = pe.transpose(px[:, bank, c * P:c * P + P], xt[:, slot, c * P:c * P + P], K["ident"][:])
                        mm.then_inc(x_turned[bank], 1)
                    with pe.Fori(0, 4) as j:
                        for k in range(2):
                            pe.wait_ge(x_in[k], j * 16 + 16)
                            tile(j, k, k, False)
                    pe.wait_ge(x_in[2], 16)
                    tile(4, 2, 0, False)

                @block.scalar
                def _(act):
                    for c in range(KD):
                        act.dma_start(K["AH"][:, c, :], A["ada_w"][0, c * P:c * P + P, 0:ADA_HEAD]).then_inc(s["ada_in"], 16)
                    act.wait_ge(s["cond_turned"], 1)
                    act.activation(K["cond"][:].rearrange("p k n -> p n k"),
                                   pc[:, 0:16].rearrange("p (n k) -> p n k", n=2), ACT.Silu).then_inc(s["cond_silu"], 1)
                    with act.Fori(0, 4) as j:
                        for k in range(2):
                            act.wait_ge(x_turned[k], j + 1)
                            act.activation(K["XT"][:, :, bass.ds((2 * j + (k + 1)) * P, P)],
                                           px[:, k, :].rearrange("p (c t) -> p c t", c=KD),
                                           ACT.Copy).then_inc(x_out[k], 1)
                    act.wait_ge(s["ada_in"], 16 * KD)
                    act.wait_ge(x_turned[0], 5)
                    act.activation(K["XT"][:, :, 0:P], px[:, 0, :].rearrange("p (c t) -> p c t", c=KD),
                                   ACT.Copy).then_inc(x_out[0], 1)

                @block.vector
                def _(dve):
                    link = chain(dve, s["dve_chain"])
                    dve.memset(rows[:], 0.0).then_inc(s["zeroed"], 1)
                    dve.wait_ge(s["turned"], 6)
                    PT = K["PT"]
                    link(dve.tensor_copy(PT[:, 0:512], pp[:, 0, :]))
                    link(dve.tensor_copy(PT[:, 512:768], pp[:, 1, 0:256]))
                    taps = K["taps"]
                    mu = PT[:, C_MU:C_MU + PA_T]
                    for t in (0, 2):
                        link(dve.tensor_scalar(taps[:, 0:PA_T, t], mu, 0.5, None, ALU.mult))
                    link(dve.tensor_scalar(taps[:, 0:PA_T, 1], mu, -1.0, 1.0, ALU.mult, ALU.add))
                    link(dve.tensor_copy(taps[:, PA_T:PA_T + QKV_T, :],
                                         PT[:, C_CONV:C_CONV + 36].rearrange("p (t n) -> p n t", t=3)))
                    link(dve.memset(taps[:, PA_T + QKV_T:AB_T, :], 0.0))
                    link(dve.memset(taps[:, PA_T + QKV_T:AB_T, 1:2], 1.0))


class AdaUnits:

    def __init__(self, K, s, prod, cols, rows):
        self.K, self.prod, self.cols, self.rows = K, prod, cols, rows
        self.made, self.out = [s["made0"], s["made1"]], [s["rows0"], s["rows1"]]
        self.turned = [s["turned0"], s["turned1"]]

    def part(self, k):
        return slice(64 * k, 64 * k + 2)

    def product(self, pe, k, w, n):
        pe.wait_ge(self.out[k], n)
        for c in range(KD):
            mm = pe.matmul(self.prod[self.part(k), 0:ADA_U], self.K["cond"][:, c, :], w(c), start=(c == 0), stop=(c == KD - 1))
        mm.then_inc(self.made[k], 1)

    def copy(self, act, k, n):
        act.wait_ge(self.made[k], n + 1)
        act.wait_ge(self.turned[k], n)
        act.activation(self.rows[0:2, k, :], self.prod[self.part(k), 0:ADA_U], ACT.Copy).then_inc(self.out[k], 1)

    def turn(self, pe, k, n, i):
        pe.wait_ge(self.out[k], n + 1)
        for m in range(ADA_U // P):
            c = 2 * (i * (ADA_U // P) + m)
            mm = pe.matmul(self.cols[:, c:c + 2], self.rows[0:2, k, m * P:m * P + P], self.K["ident"][0:2, 0:2],
                           start=True, stop=True)
        mm.then_inc(self.turned[k], 1)


ADA_SEMS = ["made0", "made1", "rows0", "rows1", "turned0", "turned1"]


def adaln_finish(link, dve, K, tiles, gains):
    mod = K["mod"]
    a, b = tiles
    for n in range(2):
        v = mod[:, :, :, :, n].rearrange("p l g k -> p (l g k)")[:, a:b]
        link(dve.tensor_tensor(v, v, K["PT"][:, C_ADAB + a:C_ADAB + b], ALU.add))
    for l, w in gains:
        g, col = ((1, C_N1), (4, C_N2))[w]
        for n in range(2):
            gain = K["gain"][:, l, w, :, n]
            link(dve.tensor_scalar(gain, mod[:, l, g, :, n], 1.0, None, ALU.add))
            link(dve.tensor_tensor(gain, gain, K["PT"][:, col + 8 * l:col + 8 * l + 8], ALU.mult))


def adaln_phase(nc, A, K):
    flat = K["mod"][:].rearrange("p l g k n -> p (l g k n)")
    units = ADA_HEAD // ADA_U
    with ExitStack() as ctx:
        rows = sbuf(ctx, nc, "ada_rows", [2, 2, ADA_U])
        prod = psum(ctx, nc, "ada_prod", [P, 512])
        cols = psum(ctx, nc, "ada_cols", [P, 512])
        with phase(nc, *ADA_SEMS, "dve_chain") as s:
            ada = AdaUnits(K, s, prod, cols, rows)
            with nc.Block() as block:
                @block.tensor
                def _(pe):
                    for i in range(units + 1):
                        if i < units:
                            ada.product(pe, i % 2, lambda c: K["AH"][:, c, i * ADA_U:(i + 1) * ADA_U], i // 2)
                        if i:
                            ada.turn(pe, (i - 1) % 2, (i - 1) // 2, i - 1)

                @block.scalar
                def _(act):
                    for i in range(units):
                        ada.copy(act, i % 2, i // 2)

                @block.vector
                def _(dve):
                    link = chain(dve, s["dve_chain"])
                    for k in range(2):
                        dve.wait_ge(ada.turned[k], units // 2)
                    link(dve.tensor_copy(flat[:, 0:2 * ADA_HEAD // P], cols[:, 0:2 * ADA_HEAD // P]))
                    adaln_finish(link, dve, K, (0, ADA_HEAD // P), [(0, 0)])


NORM_SEMS = ["squared", "summed", "log", "inv", "scaled", "eps_set", "shifted", "n_upper", "n_lower"]
HALVES = ((0, CTX), (CTX, T))


class Norm:

    def __init__(self, K, s, dst, gain, shift, tmp, rstd, eps, ps):
        self.XT, self.ones, self.s, self.dst, self.gain, self.shift = K["XT"], K["ones"], s, dst, gain, shift
        self.tmp, self.rstd, self.eps, self.ps = tmp, rstd, eps, ps

    def scalar(self, act):
        s, rstd = self.s, self.rstd
        for k in range(KD):
            if k >= 2:
                act.wait_ge(s["summed"], k - 1)
            act.activation(self.tmp[k % 2], self.XT[:, k, :], ACT.Square).then_inc(s["squared"], 1)
        act.wait_ge(s["summed"], KD)
        act.wait_ge(s["eps_set"], 1)
        act.activation(rstd[:, 0:CTX], self.ps[:, 0, 0:CTX], ACT.Ln, bias=self.eps[:], scale=1.0 / D).then_inc(s["log"], 1)
        act.activation(rstd[:, CTX:T], lat(self.ps), ACT.Ln, bias=self.eps[:], scale=1.0 / D).then_inc(s["log"], 1)
        act.wait_ge(s["log"], 2)
        act.activation(rstd[:], rstd[:], ACT.Exp, scale=-0.5).then_inc(s["inv"], 1)
        if self.shift is None:
            return
        for k in range(KD):
            x = self.tmp[k % 2]
            for n, (a, b) in enumerate(HALVES):
                act.wait_ge(s["scaled"], 2 * k + n + 1)
                act.activation(x[:, a:b], x[:, a:b], ACT.Identity,
                               bias=self.shift[:, k, n:n + 1]).then_inc(s["shifted"], 1)

    def tensor(self, pe):
        for k in range(KD):
            pe.wait_ge(self.s["squared"], k + 1)
            for b, i, j in BANKS:
                mm = pe.matmul(self.ps[:, b, 0:j - i], self.ones[:], self.tmp[k % 2][:, i:j],
                               start=(k == 0), stop=(k == KD - 1))
            mm.then_inc(self.s["summed"], 1)

    def vector(self, dve):
        s = self.s
        dve.memset(self.eps[:], RMS_EPS).then_inc(s["eps_set"], 1)
        dve.wait_ge(s["inv"], 1)

        def scale(k, out):
            for n, (a, b) in enumerate(HALVES):
                dve.scalar_tensor_tensor(out=out[:, a:b], in0=self.XT[:, k, a:b], scalar=self.gain[:, k, n:n + 1],
                                         in1=self.rstd[:, a:b], op0=ALU.mult, op1=ALU.mult).then_inc(s["scaled"], 1)
        if self.shift is None:
            for k in range(KD):
                scale(k, self.dst[0][:, k])
            return

        def cut(k):
            dve.wait_ge(s["shifted"], 2 * k + 2)
            upper(dve, self.dst[0][:, k], self.tmp[k % 2]).then_inc(s["n_upper"], 1)
        for k in range(KD):
            if k >= 2:
                cut(k - 2)
                dve.wait_ge(s["n_lower"], k - 1)
            scale(k, self.tmp[k % 2])
        cut(KD - 2)
        cut(KD - 1)

    def gpsimd(self, pool):
        for k in range(KD):
            pool.wait_ge(self.s["n_upper"], k + 1)
            lower(pool, self.dst[1][:, k], self.tmp[k % 2], self.dst[0][:, k]).then_inc(self.s["n_lower"], 1)


def final_norm_phase(nc, K, dst, gain):
    with ExitStack() as ctx:
        tmp = sbuf(ctx, nc, "squares", [P, 2, T])
        rstd = sbuf(ctx, nc, "rstd", [P, T])
        eps = sbuf(ctx, nc, "norm_eps", [P, 1])
        ps = psum(ctx, nc, "sum_ps", [P, 3, 512])
        with phase(nc, *NORM_SEMS) as s:
            norm = Norm(K, s, (dst, None), gain, None, [tmp[:, 0], tmp[:, 1]], rstd, eps, ps)
            with nc.Block() as block:
                block.scalar(norm.scalar)
                block.tensor(norm.tensor)
                block.vector(norm.vector)


BANKS = ((0, 0, CTX), (1, CTX, CTX + 512), (2, CTX + 512, T))


def matmul_tile(pe, ps, W, X, kt, ready=None):
    for k in range(kt):
        if ready is not None:
            pe.wait_ge(ready, k + 1)
        mm = matmul_split(pe, [ps[:, b, 0:j - i] for b, i, j in BANKS], lambda a: W[a][:, k, :],
                          lambda a: [X[a][:, k, i:j] for _, i, j in BANKS], k == 0, k == kt - 1)
    return mm


def lat(ps):
    return ps[:, 1:3, :].rearrange("p a b -> p (a b)")


def mixer_in_phase(nc, K, gain, shift, w, tiles, tail, zc, ztail, taps):
    X = (K["HU"], K["HL"])
    with ExitStack() as ctx:
        W = sbuf(ctx, nc, "in_w", [P, 2, KD, P])
        WU, WL = [sbuf(ctx, nc, n, [P, 2, KD, P]) for n in ("in_w_upper", "in_w_lower")]
        Wt, WtU, WtL = [sbuf(ctx, nc, n, [P, KD, tail]) for n in ("tail_w", "tail_w_upper", "tail_w_lower")]
        z = sbuf(ctx, nc, "z_tile", [P, 2, T])
        tp = sbuf(ctx, nc, "tile_taps", [P, 2, 3])
        rstd = sbuf(ctx, nc, "rstd", [P, T])
        eps = sbuf(ctx, nc, "norm_eps", [P, 1])
        tmp = sbuf(ctx, nc, "norm_tmp", [P, 2, T])
        ps = psum(ctx, nc, "in_ps", [P, 2, 3, 512])
        w_src = w[:, 0:tiles * P].rearrange("(k p) (m c) -> m p k c", p=P, c=P)
        with phase(nc, "w_in0", "w_in1", "upper0", "upper1", "lower0", "lower1", "tail_in", "tail_upper", "tail_lower",
                   "mm0", "mm1", "taps0", "taps1", "mid0", "mid1", "mid_ctx0", "mid_ctx1",
                   "part0", "part1", "z0", "z1", "stored0", "stored1", "tail_out", "tail_st", *NORM_SEMS) as s:
            norm = Norm(K, s, X, gain, shift, [tmp[:, 0], tmp[:, 1]], rstd, eps, ps[:, 1])
            w_in, up, low, mm_done, taps_ok, mid, part, z_ok, stored = [
                [s[n + "0"], s[n + "1"]] for n in ("w_in", "upper", "lower", "mm", "taps", "mid", "part", "z", "stored")]
            pairs, odd = tiles // 2, tiles % 2
            with nc.Block() as block:
                @block.sync
                def _(sp):
                    def load(j, k):
                        sp.wait_ge(low[k], j)
                        sp.dma_start(W[:, k], w_src[2 * j + k]).then_inc(w_in[k], 16)
                    with sp.Fori(0, pairs) as j:
                        early(sp, w_src[2 * j], w_src[2 * j + 1])
                        for k in range(2):
                            load(j, k)
                    if odd:
                        load(pairs, 0)
                    sp.dma_start(Wt[:], w[:, tiles * P:tiles * P + tail].rearrange("(k p) c -> p k c", p=P)).then_inc(s["tail_in"], 16)

                @block.tensor
                def _(pe):
                    def tile(j, k):
                        pe.wait_ge(low[k], j + 1)
                        pe.wait_ge(z_ok[k], j)
                        matmul_tile(pe, ps[:, k], (WU[:, k], WL[:, k]), X, KD).then_inc(mm_done[k], 1)
                    norm.tensor(pe)
                    pe.wait_ge(low[0], 1)
                    matmul_tile(pe, ps[:, 0], (WU[:, 0], WL[:, 0]), X, KD, s["n_lower"]).then_inc(mm_done[0], 1)
                    tile(0, 1)
                    with pe.Fori(0, pairs - 1) as j:
                        for k in range(2):
                            tile(j + 1, k)
                    if odd:
                        tile(pairs, 0)
                    pe.wait_ge(s["tail_lower"], 1)
                    pe.wait_ge(z_ok[odd], pairs)
                    matmul_tile(pe, ps[0:tail, odd], (WtU[:], WtL[:]), X, KD).then_inc(mm_done[odd], 1)

                @block.scalar
                def _(act):
                    norm.scalar(act)

                    def tile(j, k):
                        act.wait_ge(mm_done[k], j + 1)
                        act.wait_ge(stored[k], j * 16)
                        if taps is not None:
                            act.wait_ge(taps_ok[k], j + 1)
                            act.activation(z[:, k, 0:CTX], ps[:, k, 0, 0:CTX], ACT.Copy,
                                           scale=tp[:, k, 1:2]).then_inc(s["mid_ctx%d" % k], 1)
                            act.activation(z[:, k, CTX:T], lat(ps[:, k]), ACT.Copy,
                                           scale=tp[:, k, 1:2]).then_inc(mid[k], 1)
                        else:
                            act.activation(z[:, k, 0:CTX], ps[:, k, 0, 0:CTX], ACT.Copy).then_inc(mid[k], 1)
                            act.activation(z[:, k, CTX:T], lat(ps[:, k]), ACT.Copy).then_inc(z_ok[k], 1)
                    with act.Fori(0, pairs) as j:
                        for k in range(2):
                            tile(j, k)
                    if odd:
                        tile(pairs, 0)
                    act.wait_ge(mm_done[odd], pairs + 1)
                    act.wait_ge(stored[odd], pairs * 16)
                    act.activation(z[0:tail, odd, 0:CTX], ps[0:tail, odd, 0, 0:CTX], ACT.Copy).then_inc(s["tail_out"], 1)
                    act.activation(z[0:tail, odd, CTX:T], lat(ps[0:tail, odd]), ACT.Copy).then_inc(s["tail_out"], 1)

                @block.vector
                def _(dve):
                    def cut(j, k):
                        dve.wait_ge(w_in[k], j * 16 + 16)
                        dve.wait_ge(mm_done[k], j)
                        upper(dve, WU[:, k], W[:, k]).then_inc(up[k], 1)

                    def filter_taps(j, k):
                        dve.wait_ge(z_ok[k], j)
                        dve.tensor_copy(tp[:, k, :], taps[:, 2 * j + k, :]).then_inc(taps_ok[k], 1)

                    def tile(j, k):
                        c, l = ps[:, k, 0, 0:CTX], lat(ps[:, k])
                        dve.wait_ge(taps_ok[k], j + 1)
                        dve.wait_ge(s["mid_ctx%d" % k], j + 1)
                        dve.wait_ge(mid[k], j + 1)

                        def add(o, i, t):
                            return dve.scalar_tensor_tensor(out=o, in0=i, scalar=tp[:, k, t:t + 1], in1=o,
                                                            op0=ALU.mult, op1=ALU.add)
                        add(z[:, k, 1:CTX], c[:, 0:CTX - 1], 0).then_inc(part[k], 1)
                        add(z[:, k, CTX + 1:T], l[:, 0:LAT - 1], 0).then_inc(part[k], 1)
                        dve.wait_ge(part[k], j * 3 + 1)
                        add(z[:, k, 0:CTX - 1], c[:, 1:CTX], 2).then_inc(part[k], 1)
                        dve.wait_ge(part[k], j * 3 + 3)
                        add(z[:, k, CTX:T - 1], l[:, 1:LAT], 2).then_inc(z_ok[k], 1)
                    cut(0, 0)
                    cut(0, 1)
                    norm.vector(dve)

                    def step(j, k, more):
                        if taps is not None:
                            filter_taps(j, k)
                        if more:
                            cut(j + 1, k)
                        if taps is not None:
                            tile(j, k)
                    with dve.Fori(0, pairs - 1) as j:
                        for k in range(2):
                            step(j, k, True)
                    step(pairs - 1, 0, odd)
                    step(pairs - 1, 1, False)
                    if odd:
                        step(pairs, 0, False)
                    dve.wait_ge(s["tail_in"], 16)
                    upper(dve, WtU[:], Wt[:]).then_inc(s["tail_upper"], 1)

                @block.gpsimd
                def _(pool):
                    def rest(j, k):
                        pool.wait_ge(up[k], j + 1)
                        pool.wait_ge(mm_done[k], j)
                        lower(pool, WL[:, k], W[:, k], WU[:, k]).then_inc(low[k], 1)

                    def store(j, k):
                        pool.wait_ge(z_ok[k], j + 1)
                        if taps is None:
                            pool.wait_ge(mid[k], j + 1)
                        pool.dma_start(zc[2 * j + k], z[:, k, :]).then_inc(stored[k], 16)
                    rest(0, 0)
                    rest(0, 1)
                    norm.gpsimd(pool)
                    with pool.Fori(0, pairs - 1) as j:
                        for k in range(2):
                            rest(j + 1, k)
                            store(j, k)
                    if odd:
                        rest(pairs, 0)
                    store(pairs - 1, 0)
                    store(pairs - 1, 1)
                    if odd:
                        store(pairs, 0)
                    pool.wait_ge(s["tail_upper"], 1)
                    lower(pool, WtL[:], Wt[:], WtU[:]).then_inc(s["tail_lower"], 1)
                    pool.wait_ge(s["tail_out"], 2)
                    pool.dma_start(ztail, z[0:tail, odd, :]).then_inc(s["tail_st"], 16)
                    pool.wait_ge(s["tail_st"], 16)
                    pool.wait_ge(stored[0], (pairs + odd) * 16)
                    pool.wait_ge(stored[1], pairs * 16)


def add_out_phase(nc, K, w, gate):
    XT, HT = K["XT"], K["HT"]
    with ExitStack() as ctx:
        W = sbuf(ctx, nc, "out_w", [P, 2, KD, P])
        WU, WL = [sbuf(ctx, nc, n, [P, 2, KD, P]) for n in ("out_w_upper", "out_w_lower")]
        HU, HL = [sbuf(ctx, nc, n, [P, KD, T]) for n in ("h_upper", "h_lower")]
        g = sbuf(ctx, nc, "tile_gate", [P, 2, 2])
        ps = psum(ctx, nc, "out_ps", [P, 2, 3, 512])
        w_src = w.rearrange("(k p) (m c) -> m p k c", p=P, c=P)
        with phase(nc, "w_in0", "w_in1", "upper0", "upper1", "lower0", "lower1", "mm0", "mm1", "gate0", "gate1",
                   "added0", "added1", "h_upper", "h_lower", "h_lower_pool") as s:
            w_in, up, low, mm_done, gate_ok, added = [
                [s[n + "0"], s[n + "1"]] for n in ("w_in", "upper", "lower", "mm", "gate", "added")]
            with nc.Block() as block:
                @block.sync
                def _(sp):
                    with sp.Fori(0, KD // 2) as j:
                        early(sp, w_src[2 * j], w_src[2 * j + 1])
                        for k in range(2):
                            sp.wait_ge(low[k], j)
                            sp.dma_start(W[:, k], w_src[2 * j + k]).then_inc(w_in[k], 16)

                @block.tensor
                def _(pe):
                    with pe.Fori(0, KD // 2) as j:
                        for k in range(2):
                            pe.wait_ge(s["h_lower"], KD // 2)
                            pe.wait_ge(s["h_lower_pool"], KD // 2)
                            pe.wait_ge(low[k], j + 1)
                            pe.wait_ge(added[k], j * 2)
                            matmul_tile(pe, ps[:, k], (WU[:, k], WL[:, k]), (HU, HL), KD).then_inc(mm_done[k], 1)

                @block.vector
                def _(dve):
                    def cut(j, k):
                        dve.wait_ge(w_in[k], j * 16 + 16)
                        dve.wait_ge(mm_done[k], j)
                        upper(dve, WU[:, k], W[:, k]).then_inc(up[k], 1)

                    for c in (1, 0, 3, 2, 5, 4, 7, 6):
                        upper(dve, HU[:, c], HT[:, c]).then_inc(s["h_upper"], 1)
                        if c == 1:
                            cut(0, 0)
                            cut(0, 1)
                        if c % 2 == 0:
                            dve.wait_ge(s["h_upper"], c + 2)
                            lower(dve, HL[:, c], HT[:, c], HU[:, c]).then_inc(s["h_lower"], 1)

                    def take(j, k, more):
                        dve.wait_ge(added[k], j * 2)
                        dve.tensor_copy(g[:, k, :], gate[:, 2 * j + k, :]).then_inc(gate_ok[k], 1)
                        if more:
                            cut(j + 1, k)
                        dve.wait_ge(gate_ok[k], j + 1)
                        dve.wait_ge(mm_done[k], j + 1)
                        for n, (a, b, p) in enumerate(((0, CTX, ps[:, k, 0, 0:CTX]), (CTX, T, lat(ps[:, k])))):
                            x = XT[:, 2 * j + k, a:b]
                            dve.scalar_tensor_tensor(out=x, in0=p, scalar=g[:, k, n:n + 1], in1=x,
                                                     op0=ALU.mult, op1=ALU.add).then_inc(added[k], 1)
                    with dve.Fori(0, KD // 2 - 1) as j:
                        for k in range(2):
                            take(j, k, True)
                    for k in range(2):
                        take(KD // 2 - 1, k, False)

                @block.gpsimd
                def _(pool):
                    def rest(j, k):
                        pool.wait_ge(up[k], j + 1)
                        pool.wait_ge(mm_done[k], j)
                        lower(pool, WL[:, k], W[:, k], WU[:, k]).then_inc(low[k], 1)
                    for n, c in enumerate((1, 3, 5, 7)):
                        pool.wait_ge(s["h_upper"], 2 * n + 1)
                        lower(pool, HL[:, c], HT[:, c], HU[:, c]).then_inc(s["h_lower_pool"], 1)
                        if n < 2:
                            rest(0, n)
                    with pool.Fori(0, KD // 2 - 1) as j:
                        for k in range(2):
                            rest(j + 1, k)


FFN_CHUNKS = [(0, 5), (5, 10), (10, 14), (14, 18), (18, 22)]
GS = max(b - a for a, b in FFN_CHUNKS)
THIRD = T // 3
TAKEN = (0, 0, 2, 1, 3, 3)


def ffn_phase(nc, A, K, layer, gain, shift, gate):
    XT, X, PT = K["XT"], (K["HU"], K["HL"]), K["PT"]
    ffw = PT[:, C_FFW + layer * 9 * FT:C_FFW + (layer + 1) * 9 * FT].rearrange("p (t m) -> p t m", t=9)
    ffb = PT[:, C_FFB + layer * FT:C_FFB + (layer + 1) * FT]
    in_src = A["ffn_w_in"][layer].rearrange("(k p) (h m c) -> h m p k c", p=P, h=2, c=P)
    out_src = A["ffn_w_out"][layer].rearrange("(k p) (m c) -> m p k c", p=P, c=P)
    NM = KD // 2
    plan = []
    pair = 0
    for c, (t0, t1) in enumerate(FFN_CHUNKS):
        a, b = (t0 + 1 if c else 0), min(t1 + 1, FT)
        plan.append((a, b, pair, c, t0, t1, pair + b - a))
        pair += b - a + NM
    with ExitStack() as ctx:
        W = sbuf(ctx, nc, "ffn_w", [P, 2, KD, P])
        WU, WL = [sbuf(ctx, nc, n, [P, 2, KD, P]) for n in ("ffn_w_upper", "ffn_w_lower")]
        GU, GL = [sbuf(ctx, nc, n, [P, GS, T]) for n in ("g_upper", "g_lower")]
        u = sbuf(ctx, nc, "u_tile", [P, T])
        acc = sbuf(ctx, nc, "conv_acc", [P, T])
        tp = sbuf(ctx, nc, "ffn_taps", [P, 10])
        gt = sbuf(ctx, nc, "tile_gate", [P, 2, 2])
        eps = sbuf(ctx, nc, "norm_eps", [P, 1])
        tmp = sbuf(ctx, nc, "norm_tmp", [P, T])
        ps = psum(ctx, nc, "ffn_ps", [P, 2, 3, 512])
        po = psum(ctx, nc, "ffn_out_ps", [P, 2, 512])
        with phase(nc, "w_in0", "w_in1", "upper0", "upper1", "lower0", "lower1", "mm0", "mm1", "taps_ok", "u_ok",
                   "centre", "conv", "conv_sum", "silu", "product", "g_upper", "g_ready", "out0", "out1", "gate0",
                   "gate1", "taken0", "taken1", *NORM_SEMS) as s:
            norm = Norm(K, s, X, gain, shift, [tmp[:], u[:]], acc, eps, ps[:, 1])
            w_in, up, low, mm_done, out_mm, gate_ok, taken = [
                [s[n + "0"], s[n + "1"]] for n in ("w_in", "upper", "lower", "mm", "out", "gate", "taken")]
            SH = [(dy, dx) for dy in (-1, 0, 1) for dx in (-1, 0, 1) if (dy, dx) != (0, 0)]
            NCONV = len(SH) + 2
            with nc.Block() as block:
                @block.sync
                def _(sp):
                    for a, b, p0, c, t0, t1, p1 in plan:
                        with sp.Fori(0, b - a) as m:
                            early(sp, in_src[0, m + a], in_src[1, m + a])
                            sp.lower_val(m + p0)
                            for h in range(2):
                                sp.wait_ge(low[h], m + p0)
                                sp.dma_start(W[:, h], in_src[h, m + a]).then_inc(w_in[h], 16)
                        with sp.Fori(0, NM) as j:
                            early(sp, out_src[2 * j, :, t0:t1], out_src[2 * j + 1, :, t0:t1])
                            sp.lower_val(j + p1)
                            for h in range(2):
                                sp.wait_ge(low[h], j + p1)
                                sp.dma_start(W[:, h, 0:t1 - t0], out_src[2 * j + h, :, t0:t1]).then_inc(w_in[h], 16)

                @block.tensor
                def _(pe):
                    def u_tile(m, p, ready=None):
                        pe.wait_ge(low[0], p + 1)
                        pe.wait_ge(s["u_ok"], 2 * m)
                        matmul_tile(pe, ps[:, 0], (WU[:, 0], WL[:, 0]), X, KD, ready).then_inc(mm_done[0], 1)

                    def g_tile(m, p):
                        pe.wait_ge(low[1], p + 1)
                        pe.wait_ge(s["product"], 2 * m)
                        matmul_tile(pe, ps[:, 1], (WU[:, 1], WL[:, 1]), X, KD).then_inc(mm_done[1], 1)
                    norm.tensor(pe)
                    u_tile(0, 0, s["n_lower"])
                    g_tile(0, 0)
                    for a, b, p0, c, t0, t1, p1 in plan:
                        first = 1 if c == 0 else 0
                        with pe.Fori(0, b - a - first) as m:
                            u_tile(m + (a + first), m + (p0 + first))
                            g_tile(m + (a + first), m + (p0 + first))
                        with pe.Fori(0, NM) as j:
                            pe.wait_ge(s["g_ready"], t1)
                            for h in range(2):
                                pe.wait_ge(low[h], j + (p1 + 1))
                                for third in range(3):
                                    n = 3 * h + third
                                    x = slice(third * THIRD, third * THIRD + THIRD)
                                    pe.wait_ge(taken[n % 2], 4 * j + (4 * NM * c + TAKEN[n]))
                                    for k in range(t1 - t0):
                                        mm = matmul_split(pe, [po[:, n % 2, 0:THIRD]],
                                                          lambda q: (WU, WL)[q][:, h, k],
                                                          lambda q: [(GU, GL)[q][:, k, x]], k == 0, k == t1 - t0 - 1)
                                    mm.then_inc(out_mm[n % 2] if third < 2 else mm_done[h], 1)

                @block.scalar
                def _(act):
                    norm.scalar(act)

                    def tile(m, p):
                        act.wait_ge(mm_done[0], p + 1)
                        act.wait_ge(s["conv_sum"], m)
                        act.activation(u[:, 0:CTX], ps[:, 0, 0, 0:CTX], ACT.Copy).then_inc(s["u_ok"], 1)
                        act.activation(u[:, CTX:T], lat(ps[:, 0]), ACT.Copy).then_inc(s["u_ok"], 1)
                        act.wait_ge(s["u_ok"], 2 * m + 2)
                        act.wait_ge(s["taps_ok"], 2 * m + 2)
                        act.wait_ge(s["g_ready"], m)
                        act.activation(acc[:], u[:], ACT.Identity, bias=tp[:, 9:10],
                                       scale=tp[:, 4:5]).then_inc(s["centre"], 1)
                        act.wait_ge(s["conv_sum"], m + 1)
                        act.activation(acc[:], acc[:], ACT.Silu).then_inc(s["silu"], 1)
                    for a, b, p0, c, t0, t1, p1 in plan:
                        with act.Fori(0, b - a) as m:
                            tile(m + a, m + p0)

                @block.vector
                def _(dve):
                    def cut(h, p):
                        dve.wait_ge(w_in[h], 16 * p + 16)
                        dve.wait_ge(mm_done[h], p)
                        upper(dve, WU[:, h], W[:, h]).then_inc(up[h], 1)

                    def convolve(m, p, more):
                        dve.wait_ge(mm_done[0], p + 1)
                        dve.wait_ge(s["conv_sum"], m)
                        dve.tensor_copy(tp[:, 0:9], ffw[:, :, bass.ds(m, 1)].rearrange("p t m -> p (t m)")).then_inc(s["taps_ok"], 1)
                        dve.tensor_copy(tp[:, 9:10], ffb[:, bass.ds(m, 1)]).then_inc(s["taps_ok"], 1)
                        if more:
                            cut(0, p + 1)
                        dve.wait_ge(s["taps_ok"], 2 * m + 2)
                        dve.wait_ge(s["centre"], m + 1)
                        ug = u[:, CTX:T].rearrange("p (r c) -> p r c", c=GRID)
                        ag = acc[:, CTX:T].rearrange("p (r c) -> p r c", c=GRID)
                        n = 0
                        for dy, dx in SH:
                            r0, r1 = max(0, -dy), ROWS - max(0, dy)
                            c0, c1 = max(0, -dx), GRID - max(0, dx)
                            t = 3 * (dy + 1) + dx + 1
                            steps = [(ag[:, r0:r1, c0:c1], ug[:, r0 + dy:r1 + dy, c0 + dx:c1 + dx])]
                            if dy == 0:
                                i, j = max(0, -dx), CTX - max(0, dx)
                                steps.append((acc[:, i:j], u[:, i + dx:j + dx]))
                            for o, i in steps:
                                if n:
                                    dve.wait_ge(s["conv"], m * (NCONV - 1) + n)
                                n += 1
                                dve.scalar_tensor_tensor(out=o, in0=i, scalar=tp[:, t:t + 1], in1=o,
                                                         op0=ALU.mult, op1=ALU.add).then_inc(
                                    s["conv"] if n < NCONV else s["conv_sum"], 1)
                        if more:
                            cut(1, p + 1)

                    def product(m, slot, p):
                        dve.wait_ge(s["silu"], m + 1)
                        dve.wait_ge(mm_done[1], p + 1)
                        dve.tensor_tensor(acc[:, 0:CTX], acc[:, 0:CTX], ps[:, 1, 0, 0:CTX], ALU.mult).then_inc(s["product"], 1)
                        dve.tensor_tensor(acc[:, CTX:T], acc[:, CTX:T], lat(ps[:, 1]), ALU.mult).then_inc(s["product"], 1)
                        dve.wait_ge(s["product"], 2 * m + 2)
                        upper(dve, GU[:, slot], acc[:]).then_inc(s["g_upper"], 1)
                        dve.wait_ge(s["g_upper"], m + 1)
                        lower(dve, GL[:, slot], acc[:], GU[:, slot]).then_inc(s["g_ready"], 1)

                    def take(c, p1, j, more):
                        for h in range(2):
                            dve.wait_ge(taken[0], 4 * j + 4 * NM * c)
                            dve.wait_ge(taken[1], 4 * j + 4 * NM * c)
                            m = 2 * j + h
                            dve.tensor_copy(gt[:, h, :], gate[:, m, :]).then_inc(gate_ok[h], 1)
                            dve.wait_ge(gate_ok[h], j + (NM * c + 1))
                            for third in range(3):
                                n = 3 * h + third
                                x0 = third * THIRD
                                if third < 2:
                                    dve.wait_ge(out_mm[n % 2], 2 * j + (2 * NM * c + h + 1))
                                else:
                                    dve.wait_ge(mm_done[h], j + (p1 + 1))
                                parts = [(x0, x0 + THIRD, 1)] if third else [(0, CTX, 0), (CTX, THIRD, 1)]
                                for x, y, cond in parts:
                                    o = XT[:, m, x:y]
                                    dve.scalar_tensor_tensor(out=o, in0=po[:, n % 2, x - x0:y - x0],
                                                             scalar=gt[:, h, cond:cond + 1], in1=o,
                                                             op0=ALU.mult, op1=ALU.add).then_inc(taken[n % 2], 1)
                            if more:
                                cut(h, j + (p1 + 1))

                    cut(0, 0)
                    cut(1, 0)
                    norm.vector(dve)
                    for a, b, p0, c, t0, t1, p1 in plan:
                        with dve.Fori(0, t1 - a) as m:
                            convolve(m + a, m + p0, True)
                            product(m + a, m + (a - t0), m + p0)
                        if b > t1:
                            convolve(t1, p1 - 1, True)
                        if b > t1:
                            with dve.Fori(0, NM) as j:
                                take(c, p1, j, True)
                            product(t1, 0, p1 - 1)
                        else:
                            with dve.Fori(0, NM - 1) as j:
                                take(c, p1, j, True)
                            take(c, p1, NM - 1, False)

                @block.gpsimd
                def _(pool):
                    def rest(h, p):
                        pool.wait_ge(up[h], p + 1)
                        lower(pool, WL[:, h], W[:, h], WU[:, h]).then_inc(low[h], 1)
                    rest(0, 0)
                    rest(1, 0)
                    norm.gpsimd(pool)
                    with pool.Fori(0, pair - 1) as p:
                        for h in range(2):
                            rest(h, p + 1)


def store_out_phase(nc, K, y_prompt, y_sample):
    HT = K["HT"]
    yp = y_prompt.rearrange("b p c -> (b p) c")
    ys = y_sample.rearrange("b (n p) c -> (b n) p c", p=P)
    with ExitStack() as ctx:
        y = sbuf(ctx, nc, "y_tokens", [P, 2, D])
        col = sbuf(ctx, nc, "h_cols", [P, 2, KD, P])
        ps = psum(ctx, nc, "y_ps", [P, 2, D])
        with phase(nc, "cols0", "cols1", "turned0", "turned1", "y0", "y1", "stored0", "stored1") as s:
            cols, turned, y_ok, stored = [[s[n + "0"], s[n + "1"]] for n in ("cols", "turned", "y", "stored")]
            with nc.Block() as block:
                @block.vector
                def _(dve):
                    def take(j, k, t):
                        dve.wait_ge(turned[k], j)
                        dve.tensor_copy(col[:, k], HT[:, :, bass.ds(t * P, P)]).then_inc(cols[k], 1)
                    with dve.Fori(0, 4) as j:
                        for k in range(2):
                            take(j, k, 2 * j + k)
                    take(4, 0, 8)

                @block.tensor
                def _(pe):
                    def turn(j, k):
                        pe.wait_ge(cols[k], j + 1)
                        pe.wait_ge(y_ok[k], j)
                        for c in range(KD):
                            mm = pe.transpose(ps[:, k, c * P:c * P + P], col[:, k, c, :], K["ident"][:])
                        mm.then_inc(turned[k], 1)
                    with pe.Fori(0, 4) as j:
                        for k in range(2):
                            turn(j, k)
                    turn(4, 0)

                @block.scalar
                def _(act):
                    def out(j, k):
                        act.wait_ge(turned[k], j + 1)
                        act.wait_ge(stored[k], j * 16)
                        act.activation(y[:, k, :], ps[:, k, :], ACT.Copy).then_inc(y_ok[k], 1)
                    with act.Fori(0, 4) as j:
                        for k in range(2):
                            out(j, k)
                    out(4, 0)

                @block.gpsimd
                def _(pool):
                    pool.wait_ge(y_ok[0], 1)
                    pool.dma_start(yp, y[:, 0, :]).then_inc(stored[0], 16)
                    with pool.Fori(0, 4) as j:
                        for k in (1, 0):
                            pool.wait_ge(y_ok[k], j + (2 - k))
                            pool.dma_start(ys[2 * j + (1 - k)], y[:, k, :]).then_inc(stored[k], 16)
                    pool.wait_ge(stored[0], 5 * 16)
                    pool.wait_ge(stored[1], 4 * 16)


class Steps:

    def __init__(self, sem, names):
        self.sem, self.names, self.n = sem, names, 0

    def did(self, ins, name):
        assert self.names[self.n % len(self.names)] == name, (self.names[self.n % len(self.names)], name)
        self.n += 1
        ins.then_inc(self.sem, 1)

    def value(self, name, it):
        return it * len(self.names) + (self.names.index(name) + 1)

    def wait(self, eng, name, it=0):
        eng.wait_ge(self.sem, self.value(name, it))

    def wait_before(self, eng, it):
        eng.wait_ge(self.sem, it * len(self.names))


def chunked(ap):
    return ap.rearrange("p (c t) -> p c t", t=P)


def banks(T0=((0, 128), (128, 640), (640, 1152))):
    return list(enumerate(T0))


RW_DVE = (["pv", "ka1", "kkraw", "kk"]
          + [f"{n}{d}" for d in range(2) for n in ("kd_a", "kd", "ks", "b", "G", "M", "Gm", "Gex", "kkd", "rd", "kt", "bt")]
          + ["rk", "bonus_c", "bonus_l"])
RW_ACT = (["sq", "log_c", "log_l", "rinv"]
          + [f"{n}{d}" for d in range(2) for n in ("sg_c", "sg_l", "a_c", "a_l", "em", "e_in", "e_ex", "e_inv")])
RW_PE = ["norm"] + [f"{n}{d}" for d in range(2) for n in ("w", "a")] + ["bonus"]


def rwkv_prep_phase(nc, A, K, zc, units, bonus):
    HT = K["HT"]
    kkt, at, kdt, bt, sgt, gt, gx, ks = [HT[:, i, :] for i in range(8)]
    with ExitStack() as ctx:
        wd = sbuf(ctx, nc, "wd", [P, T])
        ad = sbuf(ctx, nc, "ad", [P, T])
        rkv = sbuf(ctx, nc, "rkv", [P, 2, 3, T])
        up = sbuf(ctx, nc, "w_a_up", [P, 2, 2, P])
        un = sbuf(ctx, nc, "unit_rows", [P, 2, NCH, 4, P])
        reset = sbuf(ctx, nc, "resets", [P, 2, T])
        pv = sbuf(ctx, nc, "pair_params", [P, 8])
        m9 = sbuf(ctx, nc, "half_end", [P, 2, NCH])
        tiny = sbuf(ctx, nc, "kk_eps", [P, 1])
        aw = sbuf(ctx, nc, "ada_w", [P, 2, KD, ADA_U])
        arows = sbuf(ctx, nc, "ada_rows", [2, 2, ADA_U])
        prod = psum(ctx, nc, "ada_prod", [P, 512])
        cols = psum(ctx, nc, "ada_cols", [P, 512])
        flat = K["mod"][:].rearrange("p l g k n -> p (l g k n)")
        half = ADA_N // 2
        per_layer = 6 * D // ADA_U
        a_src = A["ada_w"].rearrange("l (k p) (n c) -> l n p k c", p=P, c=ADA_U)
        ps = psum(ctx, nc, "prep_ps", [P, 2, 3, 512])
        w_up = A["rk_w_up"][0].rearrange("d r (q c) -> q (d r) c", c=P)
        a_up = A["rk_a_up"][0].rearrange("d r (q c) -> q (d r) c", c=P)
        par = K["PT"][:, C_W0:C_W0 + 28].rearrange("p (g q) -> p g q", q=4)
        with phase(nc, "loras_in", "in0", "in1", "dve", "act", "pe", "tanh", "ready", "st_un0", "st_un1", "st_bonus",
                   "ada_in0", "ada_in1", "ada_cols", "dve_chain", *ADA_SEMS) as s:
            ada = AdaUnits(K, s, prod, cols, arows)
            dv, ac, pe_ = Steps(s["dve"], RW_DVE), Steps(s["act"], RW_ACT), Steps(s["pe"], RW_PE)
            loaded = [s["in0"], s["in1"]]
            st_un = [s["st_un0"], s["st_un1"]]
            with nc.Block() as block:
                @block.sync
                def _(sp):
                    sp.dma_start(wd[:], zc[12]).then_inc(s["loras_in"], 16)
                    sp.dma_start(ad[:], zc[13]).then_inc(s["loras_in"], 16)

                    def load(q, k):
                        for i in range(3):
                            sp.dma_start(rkv[:, k, i, :], zc[4 * i + q]).then_inc(loaded[k], 16)
                        sp.dma_start(up[:, k, 0, :], w_up[q]).then_inc(loaded[k], 16)
                        sp.dma_start(up[:, k, 1, :], a_up[q]).then_inc(loaded[k], 16)
                    def ada_load(first, last):
                        for l in range(2):
                            a, b = max(first, l * per_layer), min(last, (l + 1) * per_layer)
                            if a < b:
                                n0 = (a - ADA_HEAD // ADA_U) // 2
                                with sp.Fori(0, (b - a) // 2) as n:
                                    src = [a_src[l, 2 * n + (a - l * per_layer + k)] for k in range(2)]
                                    early(sp, *src)
                                    sp.lower_val(n + n0)
                                    for k in range(2):
                                        sp.wait_ge(ada.made[k], n + n0)
                                        sp.dma_start(aw[:, k], src[k]).then_inc(s[f"ada_in{k}"], 16)
                    load(0, 0)
                    load(1, 1)
                    done = ADA_HEAD // ADA_U
                    for k in range(2):
                        ada_load(done, done + ADA_N + 2 * (k == 0))
                        done += ADA_N + 2 * (k == 0)
                        dv.wait(sp, "bonus_l", k)
                        load(2 + k, k)
                    ada_load(done, 2 * per_layer)

                @block.tensor
                def _(pe):
                    def ada_step(it, i):
                        if i < ADA_N:
                            n = half * it + i // 2
                            pe.wait_ge(s[f"ada_in{i % 2}"], 16 * n + 16)
                            ada.product(pe, i % 2, lambda c: aw[:, i % 2, c, :], n)
                        if i:
                            if i == 1:
                                pe.wait_ge(s["ada_cols"], it)
                            ada.turn(pe, (i - 1) % 2, half * it + (i - 1) // 2, i - 1)
                    with pe.Fori(0, 2) as j:
                        for k in range(2):
                            it = 2 * j + k
                            ada_step(it, 0)
                            ac.wait(pe, "sq", it)
                            dv.wait_before(pe, it)
                            for b, (x, y) in banks():
                                mm = pe.matmul(ps[:, 0, b, 0:y - x], K["ones64"][:], at[:, x:y], start=True, stop=True)
                            pe_.did(mm, "norm")
                            ada_step(it, 1)
                            ada_step(it, 2)
                            for d in range(2):
                                pe.wait_ge(s["tanh"], 1)
                                pe.wait_ge(loaded[k], j * 80 + 80)
                                ac.wait(pe, "log_l" if d == 0 else "sg_l0", it)
                                for b, (x, y) in banks():
                                    mm = pe.matmul(ps[:, 0, b, 0:y - x], up[64 * d:64 * d + 64, k, 0, :],
                                                   wd[64 * d:64 * d + 64, x:y], start=True, stop=True)
                                pe_.did(mm, f"w{d}")
                                if d == 1:
                                    ac.wait(pe, "a_l0", it)
                                for b, (x, y) in banks():
                                    mm = pe.matmul(ps[:, 1, b, 0:y - x], up[64 * d:64 * d + 64, k, 1, :],
                                                   ad[64 * d:64 * d + 64, x:y], start=True, stop=True)
                                pe_.did(mm, f"a{d}")
                            for i in range(3, ADA_N + 1):
                                ada_step(it, i)
                            dv.wait(pe, "rk", it)
                            ac.wait(pe, "sg_l1", it)
                            for b, (x, y) in banks():
                                mm = pe.matmul(ps[:, 0, b, 0:y - x], K["ones64"][:], ks[:, x:y], start=True, stop=True)
                            pe_.did(mm, "bonus")

                @block.scalar
                def _(act):
                    act.wait_ge(s["loras_in"], 32)
                    act.activation(wd[:], wd[:], ACT.Tanh).then_inc(s["tanh"], 1)
                    act.wait_ge(s["ready"], 3)
                    with act.Fori(0, 2) as j:
                        for k in range(2):
                            it = 2 * j + k
                            dv.wait(act, "kkraw", it)
                            ac.did(act.activation(at, kkt, ACT.Square), "sq")
                            ada.copy(act, 0, half * it)
                            pe_.wait(act, "norm", it)
                            for n, q, v in (("c", slice(0, CTX), ps[:, 0, 0, 0:CTX]), ("l", slice(CTX, T), lat(ps[:, 0]))):
                                ac.did(act.activation(kdt[:, q], v, ACT.Ln, bias=tiny[:]), f"log_{n}")
                            ac.wait(act, "log_l", it)
                            ac.did(act.activation(kdt, kdt, ACT.Exp, scale=-0.5), "rinv")
                            ada.copy(act, 1, half * it)
                            for d in range(2):
                                if d == 1:
                                    for i in range(2, 4):
                                        ada.copy(act, i % 2, half * it + i // 2)
                                for nm, sl, dst, off in (("sg", 0, sgt, d), ("a", 1, at, 2 + d)):
                                    pe_.wait(act, f"{'w' if sl == 0 else 'a'}{d}", it)
                                    if d == 1:
                                        dv.wait(act, "bt0", it)
                                    for n, q, v in (("c", slice(0, CTX), ps[:, sl, 0, 0:CTX]),
                                                    ("l", slice(CTX, T), lat(ps[:, sl]))):
                                        ac.did(act.activation(dst[:, q], v, ACT.Sigmoid, bias=pv[:, off:off + 1]),
                                               f"{nm}_{n}{d}")
                                if d == 1:
                                    for i in range(4, 6):
                                        ada.copy(act, i % 2, half * it + i // 2)
                                act.wait_ge(st_un[d], it * 16)
                                dv.wait(act, f"Gex{d}", it)
                                em = K["EM"][:, d, :, bass.ds(it, 1)].rearrange("p c o -> p (c o)")
                                ac.did(act.activation(em, m9[:, d, :], ACT.Exp, scale=-EXP_HALF), f"em{d}")
                                g, x = chunked(gt), chunked(gx)
                                ac.did(act.activation(un[:, d, :, 1, :], g, ACT.Exp, scale=-EXP_HALF), f"e_in{d}")
                                ac.did(act.activation(un[:, d, :, 0, :], x, ACT.Exp, scale=-EXP_HALF), f"e_ex{d}")
                                ac.did(act.activation(un[:, d, :, 2, :], g, ACT.Exp, scale=EXP_HALF), f"e_inv{d}")
                            for i in range(6, ADA_N):
                                ada.copy(act, i % 2, half * it + i // 2)

                @block.vector
                def _(dve):
                    dve.memset(reset[:], 1.0).then_inc(s["ready"], 1)
                    dve.memset(tiny[:], 1e-12).then_inc(s["ready"], 1)
                    dve.wait_ge(s["ready"], 2)
                    for d in range(2):
                        ins = dve.memset(chunked(reset[:, d, :])[:, :, d * (P - 1):d * (P - 1) + 1], 0.0)
                    ins.then_inc(s["ready"], 1)
                    dve.wait_ge(s["ready"], 3)
                    with dve.Fori(0, 2) as j:
                        for k in range(2):
                            it = 2 * j + k
                            r, kr, v = [rkv[:, k, i, :] for i in range(3)]
                            ac.wait_before(dve, it)
                            dve.wait_ge(s["st_bonus"], it * 16)
                            dv.did(dve.tensor_copy(pv[:, 0:7], par[:, :, bass.ds(it, 1)].rearrange("p g o -> p (g o)")), "pv")
                            dv.wait(dve, "pv", it)
                            dv.did(dve.tensor_scalar(pv[:, 7:8], pv[:, 5:6], -1.0, 1.0, ALU.mult, ALU.add), "ka1")
                            dve.wait_ge(loaded[k], j * 80 + 80)
                            dv.did(dve.tensor_scalar(kkt, kr, pv[:, 4:5], None, ALU.mult), "kkraw")
                            ac.wait(dve, "rinv", it)
                            dv.did(dve.tensor_tensor(kkt, kkt, kdt, ALU.mult), "kk")
                            for d in range(2):
                                ac.wait(dve, f"a_l{d}", it)
                                dv.wait(dve, "kk" if d == 0 else "bt0", it)
                                dv.did(dve.tensor_scalar(kdt, at, pv[:, 5:6], pv[:, 7:8], ALU.mult, ALU.add), f"kd_a{d}")
                                dv.wait(dve, f"kd_a{d}", it)
                                dv.did(dve.tensor_tensor(kdt, kdt, kr, ALU.mult), f"kd{d}")
                                dv.wait(dve, f"kd{d}", it)
                                if d == 0:
                                    dv.did(dve.tensor_copy(ks, kdt), "ks0")
                                else:
                                    dv.did(dve.tensor_tensor(ks, ks, kdt, ALU.add), "ks1")
                                dv.did(dve.tensor_tensor(bt, kkt, at, ALU.mult), f"b{d}")
                                sd = -1 if d else 1
                                if d == 1:
                                    ac.wait(dve, "e_inv0", it)
                                dv.did(dve.tensor_tensor_scan(gt[:, ::sd], reset[:, d, ::sd], sgt[:, ::sd], 0.0,
                                                              ALU.mult, ALU.add), f"G{d}")
                                dv.wait(dve, f"G{d}", it)
                                end = chunked(gt)[:, :, (0 if d else P - 1):(1 if d else P)]
                                dv.did(dve.tensor_scalar(m9[:, d, :], end.rearrange("p c o -> p (c o)"), 0.5, None,
                                                         ALU.mult), f"M{d}")
                                dv.wait(dve, f"M{d}", it)
                                dv.did(dve.tensor_tensor(chunked(gt), chunked(gt),
                                                         m9[:, d, :, None].to_broadcast([P, NCH, P]), ALU.subtract), f"Gm{d}")
                                dv.wait(dve, f"Gm{d}", it)
                                dv.did(dve.tensor_tensor(gx, gt, sgt, ALU.subtract), f"Gex{d}")
                                u = un[:, d]
                                ac.wait(dve, f"e_ex{d}", it)
                                dv.did(dve.tensor_tensor(u[:, :, 0, :], u[:, :, 0, :], chunked(kkt), ALU.mult), f"kkd{d}")
                                dv.did(dve.tensor_tensor(u[:, :, 1, :], u[:, :, 1, :], chunked(r), ALU.mult), f"rd{d}")
                                ac.wait(dve, f"e_inv{d}", it)
                                dv.did(dve.tensor_tensor(u[:, :, 3, :], u[:, :, 2, :], chunked(kdt), ALU.mult), f"kt{d}")
                                dv.wait(dve, f"kt{d}", it)
                                dv.did(dve.tensor_tensor(u[:, :, 2, :], u[:, :, 2, :], chunked(bt), ALU.mult), f"bt{d}")
                            dv.did(dve.scalar_tensor_tensor(out=ks, in0=ks, scalar=pv[:, 6:7], in1=r, op0=ALU.mult,
                                                            op1=ALU.mult), "rk")
                            pe_.wait(dve, "bonus", it)
                            dv.did(dve.tensor_tensor(ks[:, 0:CTX], v[:, 0:CTX], ps[:, 0, 0, 0:CTX], ALU.mult), "bonus_c")
                            dv.did(dve.tensor_tensor(ks[:, CTX:T], v[:, CTX:T], lat(ps[:, 0]), ALU.mult), "bonus_l")
                            for p in range(2):
                                dve.wait_ge(ada.turned[p], half * it + half)
                            nc_ = 2 * ADA_N * ADA_U // P
                            dve.tensor_copy(flat[:, bass.ds(nc_ * it + 2 * ADA_HEAD // P, nc_)],
                                            cols[:, 0:nc_]).then_inc(s["ada_cols"], 1)
                    dve.wait_ge(s["ada_cols"], ADA_ITS)
                    adaln_finish(chain(dve, s["dve_chain"]), dve, K, (ADA_HEAD // P, 96), [(0, 1), (1, 0), (1, 1)])

                @block.gpsimd
                def _(pool):
                    with pool.Fori(0, 4) as it:
                        for d in range(2):
                            dv.wait(pool, f"bt{d}", it)
                            pool.dma_start(units[it, d].rearrange("p c u t -> p (c u t)"),
                                           un[:, d].rearrange("p c u t -> p (c u t)")).then_inc(st_un[d], 16)
                        dv.wait(pool, "bonus_l", it)
                        pool.dma_start(bonus[it], ks).then_inc(s["st_bonus"], 16)
                    for n in ("st_un0", "st_un1", "st_bonus"):
                        pool.wait_ge(s[n], 64)


class ItSteps:

    def __init__(self, steps, it):
        self.steps, self.it = steps, it

    def did(self, ins, name):
        self.steps.did(ins, name)

    def wait(self, eng, name):
        self.steps.wait(eng, name, self.it)


NL = len(LEVELS)


def inverse_pe(pe, ps, st, K, B, q, g, level):
    dv, ac, po, pe_ = st
    X, Y, W, NM = B["X"][:, g], B["Y"][:, g], B["W"][:, g], B["NM"][:, g]
    lanes = [(h, d) for h in range(2) for d in range(2)]

    def bank(n, i):
        return ps[:, g, n, i * P:i * P + P]
    if level == 0:
        po.wait(pe, f"{q}m0")
        for i, (h, d) in enumerate(lanes):
            mm = pe.transpose(bank(0, i), NM[:, 0, h, d, :], K["ident"][:])
        pe_.did(mm, f"{q}y0")
        return
    po.wait(pe, f"{q}m{level}")
    dv.wait(pe, f"{q}Y{level - 1}")
    for i, (h, d) in enumerate(lanes):
        mm = pe.matmul(bank(1, i), NM[:, level, h, d, :], Y[:, h, d, :], start=True, stop=True)
    pe_.did(mm, f"{q}w{level}")
    if level > 1:
        for i, (h, d) in enumerate(lanes):
            mm = pe.transpose(bank(3, i), Y[:, h, d, :], K["ident"][:])
        pe_.did(mm, f"{q}x{level - 1}")


def inverse_pe2(pe, ps, st, K, B, q, g, level):
    dv, ac, po, pe_ = st
    X, Y, W = B["X"][:, g], B["Y"][:, g], B["W"][:, g]
    lanes = [(h, d) for h in range(2) for d in range(2)]
    ac.wait(pe, f"{q}W{level}")
    if level > 1:
        dv.wait(pe, f"{q}X{level - 1}")
    else:
        po.wait(pe, f"{q}X0")
    if level < NL - 1:
        for i, (h, d) in enumerate(lanes):
            mm = pe.matmul(ps[:, g, 2, i * P:i * P + P], X[:, h, d, :], W[:, h, d, :], start=True, stop=True)
        pe_.did(mm, f"{q}dy{level}")
        return
    for i, (h, d) in enumerate(lanes):
        mm = pe.matmul(ps[:, g, 3, i * P:i * P + P], W[:, h, d, :], X[:, h, d, :], start=True, stop=True)
    pe_.did(mm, f"{q}dx{level}")


def four(ap):
    return ap.rearrange("p h d t -> p (h d t)")


def inverse_dve(dve, ps, st, K, B, q, g, level):
    dv, ac, po, pe_ = st
    X, Y = four(B["X"][:, g]), four(B["Y"][:, g])
    if level == 0:
        pe_.wait(dve, f"{q}y0")
        dv.did(dve.tensor_tensor(Y.rearrange("p (l t) -> p l t", t=P), K["ident"][:, None, :].to_broadcast([P, 4, P]),
                                 ps[:, g, 0, :].rearrange("p (l t) -> p l t", t=P), ALU.subtract), f"{q}Y0")
        return
    if level < NL - 1:
        pe_.wait(dve, f"{q}dy{level}")
        dv.did(dve.tensor_tensor(Y, Y, ps[:, g, 2, :], ALU.subtract), f"{q}Y{level}")
    else:
        pe_.wait(dve, f"{q}dx{level}")
        dv.did(dve.tensor_tensor(X, X, ps[:, g, 3, :], ALU.subtract), f"{q}X{level}")


def inverse_dve2(dve, ps, st, K, B, q, g, level):
    dv, ac, po, pe_ = st
    pe_.wait(dve, f"{q}x{level}")
    dv.did(dve.tensor_copy(four(B["X"][:, g]), ps[:, g, 3, :]), f"{q}X{level}")


def inverse_pool_names(a):
    return ([f"{q}{n}" for q in (a, a + 1) for n in ("m0", "X0", "m1")]
            + [f"{q}m{l}" for l in range(2, NL) for q in (a, a + 1)])


def inverse_pool(pool, st, K, B, q, g, levels):
    dv, ac, po, pe_ = st
    N, NM, X = B["N"][:, g], B["NM"][:, g], B["X"][:, g]
    for level in levels:
        po.did(pool.tensor_tensor(NM[:, level], N[:, :, :, 0, :],
                                  K["pairs"][:, level, None, :, :].to_broadcast([P, 2, 2, P]), ALU.mult), f"{q}m{level}")
        if level == 0:
            po.wait(pool, f"{q}m0")
            po.did(pool.tensor_tensor(four(X).rearrange("p (l t) -> p l t", t=P),
                                      K["ident"][:, None, :].to_broadcast([P, 4, P]),
                                      four(NM[:, 0]).rearrange("p (l t) -> p l t", t=P), ALU.subtract), f"{q}X0")


def scan_steps(s, groups, pe_pre, pe_post, dve_pre, dve_post, act_pre, act_post, dve_head=(), inverse=True):
    pe, dve, act, pool = [], list(dve_head), [], []
    for a in range(0, groups, 2):
        prs = (a, a + 1)
        for lst, names in ((pe, pe_pre), (dve, dve_pre), (act, act_pre)):
            for q in prs:
                lst += [f"{q}{n}" for n in names]
        if inverse:
            pool += inverse_pool_names(a)
            for l in range(NL):
                for q in prs:
                    pe += [f"{q}y0"] if l == 0 else [f"{q}w{l}"] if l == 1 else [f"{q}w{l}", f"{q}x{l - 1}"]
                    if l:
                        act += [f"{q}W{l}"]
                if l:
                    for q in prs:
                        pe += [f"{q}dy{l}"] if l < NL - 1 else [f"{q}dx{l}"]
                for q in prs:
                    dve += [f"{q}Y{l}"] if l < NL - 1 else [f"{q}X{l}"]
                if 0 < l < NL - 1:
                    for q in prs:
                        dve += [f"{q}X{l}"]
        for names, lst in ((pe_post, pe), (dve_post, dve), (act_post, act)):
            for part in names:
                for q in prs:
                    lst += [f"{q}{n}" for n in part]
    return Steps(s["dve"], dve), Steps(s["act"], act), Steps(s["pool"], pool), Steps(s["pe"], pe)


def scan_iterations(eng, steps, body):
    if steps == 1:
        body(0, 0, 0)
    else:
        with eng.Fori(0, steps) as it:
            body(it, it + 1, steps - it)


def rwkv_scan_phase(nc, K, units, zc, yscan, steps, state):
    with ExitStack() as ctx:
        B = {n: sbuf(ctx, nc, n, [P, 2, 2, 2, P]) for n in ("X", "Y", "W")}
        B["N"] = sbuf(ctx, nc, "N", [P, 2, 2, 2, 2, P])
        B["NM"] = sbuf(ctx, nc, "NM", [P, 2, NL, 2, 2, P])
        AK = sbuf(ctx, nc, "AK", [P, 2, 2, 2, 2, P])
        un = sbuf(ctx, nc, "un", [P, 4, 2, 4, P])
        vv = sbuf(ctx, nc, "vv", [P, 4, 2, P])
        tok = sbuf(ctx, nc, "tok", [P, 2, 3, 2, P])
        em = sbuf(ctx, nc, "em", [P, 2, 4])
        S1 = sbuf(ctx, nc, "S_scaled", [P, 4, 2, 64])
        Rb = sbuf(ctx, nc, "Rb", [P, 2, 2, 2, 64])
        Ub = sbuf(ctx, nc, "Ub", [P, 2, 2, 2, 64])
        yt = sbuf(ctx, nc, "yt", [P, 4, 2, P])
        ps = psum(ctx, nc, "scan_ps", [P, 2, 4, 512])
        with phase(nc, "dve", "act", "pool", "pe", *[f"in{q}" for q in range(4)], *[f"out{q}" for q in range(4)]) as s:
            st = scan_steps(s, 4, ["tok", "a1", "a2"], [["r"], ["u"], ["y", "s"]],
                            ["S1", "n0", "n1", "k0", "k1"], [["s_tmp", "S"]],
                            ["tok_a", "tok_b"], [["R0", "R1"], ["U"], ["yt0", "yt1"]], dve_head=["em0", "em1"])
            dv, ac, po, pe_ = st
            loaded = [s[f"in{q}"] for q in range(4)]
            stored = [s[f"out{q}"] for q in range(4)]
            u_src = units.rearrange("q d p c u t -> q d c p (u t)")
            v_src = zc.rearrange("m p (c t) -> m c p t", t=P)
            y_dst = yscan.rearrange("d q p (c t) -> d q c p t", t=P)
            with nc.Block() as block:
                @block.sync
                def _(sp):
                    def load(q, d, c):
                        sp.dma_start(un[:, q, d], u_src[q, d, c].rearrange("p (u t) -> p u t", u=4)).then_inc(loaded[q], 16)
                        sp.dma_start(vv[:, q, d], v_src[8 + q, c]).then_inc(loaded[q], 16)

                    def body(it, cs, wait):
                        for q in range(4):
                            for d in range(2):
                                early(sp, u_src[q, d, cs[d]], v_src[8 + q, cs[d]])
                        for q in range(4):
                            if wait:
                                pe_.wait(sp, f"{q}s", it - 1)
                            for d in range(2):
                                load(q, d, cs[d])
                    if steps == 1:
                        body(0, (0, 0), False)
                    else:
                        body(0, (1, steps), False)
                        with sp.Fori(1, steps) as it:
                            body(it, (it + 1, steps - it), True)

                @block.tensor
                def _(pe):
                    def body(it, c0, c1):
                        for a in (0, 2):
                            for q in (a, a + 1):
                                g = q - a
                                pe.wait_ge(loaded[q], it * 64 + 64)
                                if a == 0:
                                    dv.wait_before(pe, it)
                                    ac.wait_before(pe, it)
                                else:
                                    dv.wait(pe, f"{g}S", it)
                                    ac.wait(pe, f"{g}yt1", it)
                                for i, (w, d) in enumerate(((2, 0), (2, 1), (3, 0), (3, 1))):
                                    pe.transpose(ps[:, g, 2, i * P:i * P + P], un[:, q, d, w, :], K["ident"][:])
                                for d in range(2):
                                    mm = pe.transpose(ps[:, g, 3, d * P:d * P + P], vv[:, q, d, :], K["ident"][:])
                                pe_.did(mm, f"{q}tok")
                                for w, nm in ((2, "a1"), (3, "a2")):
                                    if nm == "a2":
                                        ac.wait(pe, f"{q}tok_b", it)
                                    for d in range(2):
                                        for h in range(2):
                                            x = slice(64 * h, 64 * h + 64)
                                            mm = pe.matmul(ps[:, g, (w - 2) * 2 + h, d * 256:d * 256 + 256],
                                                           un[x, q, d, w, :], un[x, q, d, 0:2, :].rearrange("p u t -> p (u t)"),
                                                           start=True, stop=True)
                                    pe_.did(mm, f"{q}{nm}")
                            st_it = [ItSteps(x, it) for x in st]
                            for l in range(NL):
                                for q in (a, a + 1):
                                    if l == 0:
                                        dv.wait(pe, f"{q}n1", it)
                                    if l == 1:
                                        dv.wait(pe, f"{q}k1", it)
                                    inverse_pe(pe, ps, st_it, K, B, q, q - a, l)
                                if l:
                                    for q in (a, a + 1):
                                        inverse_pe2(pe, ps, st_it, K, B, q, q - a, l)
                            for q in (a, a + 1):
                                g = q - a
                                dv.wait(pe, f"{q}S1", it)
                                ac.wait(pe, f"{q}W{NL - 1}", it)
                                for h in range(2):
                                    x = slice(64 * h, 64 * h + 64)
                                    for d in range(2):
                                        o = ps[:, g, h, d * 64:d * 64 + 64]
                                        pe.matmul(o, un[x, q, d, 0, :], S1[x, q, d, :], start=True, stop=False)
                                        mm = pe.matmul(o, AK[:, g, h, d, 0, :], tok[:, g, 2, d, x], start=False, stop=True)
                                pe_.did(mm, f"{q}r")
                            for q in (a, a + 1):
                                g = q - a
                                dv.wait(pe, f"{q}X{NL - 1}", it)
                                ac.wait(pe, f"{q}R1", it)
                                for h in range(2):
                                    for d in range(2):
                                        i = 2 * h + d
                                        mm = pe.matmul(ps[:, g, 2, i * 64:i * 64 + 64], B["X"][:, g, h, d, :], Rb[:, g, h, d, :],
                                                       start=True, stop=True)
                                pe_.did(mm, f"{q}u")
                            for q in (a, a + 1):
                                g = q - a
                                ac.wait(pe, f"{q}U", it)
                                for h in range(2):
                                    x = slice(64 * h, 64 * h + 64)
                                    for d in range(2):
                                        o = ps[x, g, h, d * P:d * P + P]
                                        pe.matmul(o, Ub[:, g, h, d, :], B["N"][:, g, h, d, 1, :], start=True, stop=False)
                                        pe.matmul(o, tok[:, g, 2, d, x], AK[:, g, h, d, 1, :], start=False, stop=False)
                                        mm = pe.matmul(o, S1[x, q, d, :], un[x, q, d, 1, :], start=False, stop=True)
                                pe_.did(mm, f"{q}y")
                                for h in range(2):
                                    x = slice(64 * h, 64 * h + 64)
                                    for d in range(2):
                                        o = ps[x, g, 3, d * 64:d * 64 + 64]
                                        pe.matmul(o, tok[:, g, 0, d, x], Ub[:, g, h, d, :], start=True, stop=False)
                                        mm = pe.matmul(o, tok[:, g, 1, d, x], tok[:, g, 2, d, x], start=False, stop=True)
                                pe_.did(mm, f"{q}s")
                    scan_iterations(pe, steps, body)

                @block.scalar
                def _(act):
                    def body(it, c0, c1):
                        for a in (0, 2):
                            for q in (a, a + 1):
                                g = q - a
                                pe_.wait(act, f"{q}tok", it)
                                ac.did(act.activation(tok[:, g, 0:2].rearrange("p w d c -> p (w d c)"), ps[:, g, 2, :],
                                                      ACT.Copy), f"{q}tok_a")
                                ac.did(act.activation(tok[:, g, 2].rearrange("p d c -> p (d c)"), ps[:, g, 3, 0:256],
                                                      ACT.Copy), f"{q}tok_b")
                            for l in range(1, NL):
                                for q in (a, a + 1):
                                    pe_.wait(act, f"{q}w{l}", it)
                                    ac.did(act.activation(four(B["W"][:, q - a]), ps[:, q - a, 1, :], ACT.Copy), f"{q}W{l}")
                            for q in (a, a + 1):
                                pe_.wait(act, f"{q}r", it)
                                for h in range(2):
                                    ac.did(act.activation(Rb[:, q - a, h].rearrange("p d v -> p (d v)"),
                                                          ps[:, q - a, h, 0:P], ACT.Copy, scale=-1.0), f"{q}R{h}")
                            for q in (a, a + 1):
                                pe_.wait(act, f"{q}u", it)
                                ac.did(act.activation(Ub[:, q - a].rearrange("p h d v -> p (h d v)"),
                                                      ps[:, q - a, 2, 0:256], ACT.Copy), f"{q}U")
                            for q in (a, a + 1):
                                pe_.wait(act, f"{q}y", it)
                                act.wait_ge(stored[q], it * 32)
                                for h in range(2):
                                    x = slice(64 * h, 64 * h + 64)
                                    ac.did(act.activation(yt[x, q].rearrange("p d t -> p (d t)"), ps[x, q - a, h, 0:256],
                                                          ACT.Copy), f"{q}yt{h}")
                            for q in (a, a + 1):
                                ac.wait(act, f"{q}yt1", it)
                                for d in range(2):
                                    act.dma_start(y_dst[d, q, (c0, c1)[d]], yt[:, q, d, :]).then_inc(stored[q], 16)
                    scan_iterations(act, steps, body)
                    for q in range(4):
                        act.wait_ge(stored[q], steps * 32)

                @block.vector
                def _(dve):
                    def body(it, c0, c1):
                        dv.wait_before(dve, it)
                        for d, c in enumerate((c0, c1)):
                            dv.did(dve.tensor_copy(em[:, d, :], K["EM"][:, d, bass.ds(c, 1), :].rearrange("p o q -> p (o q)")),
                                   f"em{d}")
                        for a in (0, 2):
                            for q in (a, a + 1):
                                g = q - a
                                dv.wait(dve, "em1", it)
                                dv.did(dve.tensor_tensor(S1[:, q], state[:, q], em[:, :, q:q + 1].to_broadcast([P, 2, 64]),
                                                         ALU.mult), f"{q}S1")
                                for w, (nm, mt, dst) in enumerate((("n", "a1", B["N"]), ("k", "a2", AK))):
                                    pe_.wait(dve, f"{q}{mt}", it)
                                    for h in range(2):
                                        dv.did(dve.tensor_tensor(dst[:, g, h].rearrange("p d w t -> p (d w t)"), ps[:, g, 2 * w + h, :],
                                                                 K["order"][:].rearrange("p d w t -> p (d w t)"), ALU.mult),
                                               f"{q}{nm}{h}")
                            st_it = [ItSteps(x, it) for x in st]
                            for l in range(NL):
                                for q in (a, a + 1):
                                    inverse_dve(dve, ps, st_it, K, B, q, q - a, l)
                                if 0 < l < NL - 1:
                                    for q in (a, a + 1):
                                        inverse_dve2(dve, ps, st_it, K, B, q, q - a, l)
                            for q in (a, a + 1):
                                pe_.wait(dve, f"{q}s", it)
                                dv.did(dve.tensor_tensor(S1[:, q].rearrange("p d v -> p (d v)"), S1[:, q].rearrange("p d v -> p (d v)"),
                                                         ps[:, q - a, 3, 0:P], ALU.add), f"{q}s_tmp")
                                dv.wait(dve, f"{q}s_tmp", it)
                                dv.did(dve.tensor_tensor(state[:, q], S1[:, q], em[:, :, q:q + 1].to_broadcast([P, 2, 64]),
                                                         ALU.mult), f"{q}S")
                    scan_iterations(dve, steps, body)

                @block.gpsimd
                def _(pool):
                    def body(it, c0, c1):
                        for a in (0, 2):
                            st_it = [ItSteps(x, it) for x in st]
                            for q in (a, a + 1):
                                dv.wait(pool, f"{q}n1", it)
                                inverse_pool(pool, st_it, K, B, q, q - a, (0, 1))
                            for l in range(2, NL):
                                for q in (a, a + 1):
                                    inverse_pool(pool, st_it, K, B, q, q - a, (l,))
                    scan_iterations(pool, steps, body)


GD_PREP_DVE = ["rk", "rq"]


def gdn_prep_phase(nc, A, K, zc, ztail, qkv):
    GR, GC = K["GR"], K["GC"]
    with ExitStack() as ctx:
        z3 = sbuf(ctx, nc, "kqv", [P, 2, 3, T])
        un = sbuf(ctx, nc, "gdn_rows", [P, 2, NCH, 3, P])
        sq = sbuf(ctx, nc, "gdn_sq", [P, 2, T])
        rn = sbuf(ctx, nc, "gdn_rnorm", [P, 2, T])
        eps = sbuf(ctx, nc, "gdn_eps", [P, 1])
        al, be, t0, reset = [K["HT"][0:4, 2 * i:2 * i + 2, :] for i in range(4)]
        prm = sbuf(ctx, nc, "gate_params", [4, 2, 2])
        ps = psum(ctx, nc, "gdn_ps", [P, 2, 3, 512])
        pc = psum(ctx, nc, "gdn_cols", [P, 512])
        with phase(nc, "rows_in", "params_in", "d_chain", "a_chain", "gates", "cols", "in0", "in1", "dve", "act", "pe",
                   "eps_set", "st0", "st1", "x_ready", "abs_done", "reset_ok") as s:
            dv = Steps(s["dve"], ["k", "q"])
            ac = Steps(s["act"], ["sk", "sq", "sv", "qk", "qq", "lk0", "lk1", "lq0", "lq1", "ek", "eq"])
            pe_ = Steps(s["pe"], ["nk", "nq"])
            loaded, stored = [s["in0"], s["in1"]], [s["st0"], s["st1"]]
            with nc.Block() as block:
                @block.sync
                def _(sp):
                    sp.dma_start(al, ztail[0:8, :].rearrange("(d h) t -> h d t", d=2)).then_inc(s["rows_in"], 16)
                    sp.dma_start(be, ztail[8:16, :].rearrange("(d h) t -> h d t", d=2)).then_inc(s["rows_in"], 16)
                    for i, n in enumerate(("gd_a_log", "gd_dt_bias")):
                        sp.dma_start(prm[:, i, :], A[n].rearrange("l d h -> h (l d)"),
                                     allow_slow_non_contiguous=True).then_inc(s["params_in"], 16)

                    def load(h, k):
                        for i, base in enumerate((19, 15, 23)):
                            sp.dma_start(z3[:, k, i, :], zc[base + h]).then_inc(loaded[k], 16)
                    load(0, 0)
                    load(1, 1)
                    for k in range(2):
                        ac.wait(sp, "sv", k)
                        load(2 + k, k)

                @block.scalar
                def _(act):
                    link = chain(act, s["a_chain"])
                    act.wait_ge(s["rows_in"], 32)
                    act.wait_ge(s["params_in"], 32)
                    link(act.activation(prm[:, 0, :], prm[:, 0, :], ACT.Exp))
                    link(act.activation(be, be, ACT.Sigmoid))
                    act.wait_ge(s["x_ready"], 2)
                    link(act.activation(t0, al, ACT.Abs))
                    link(act.activation(t0, t0, ACT.Exp, scale=-1.0))
                    link(act.activation(t0, t0, ACT.Ln, bias=1.0))
                    act.nop().then_inc(s["abs_done"], 1)
                    act.wait_ge(s["cols"], 1)
                    cols = pc[:, 0:NCH * 16].rearrange("p (c w x) -> p c w x", c=NCH, w=2)
                    out = [GC[:, :, i].rearrange("p c d h -> p c (d h)") for i in range(3)]
                    link(act.activation(out[0], cols[:, :, 0, :], ACT.Copy))
                    link(act.activation(out[2], cols[:, :, 1, :], ACT.Copy))
                    link(act.activation(out[1], cols[:, :, 0, :], ACT.Exp))
                    link(act.activation(out[1], out[1], ACT.Copy, scale=-1.0))
                    act.wait_ge(s["eps_set"], 1)
                    with act.Fori(0, 2) as j:
                        for k in range(2):
                            it = 2 * j + k
                            act.wait_ge(loaded[k], j * 48 + 48)
                            act.wait_ge(stored[k], j * 16)
                            dv.wait_before(act, it)
                            for i, n in enumerate("kqv"):
                                ac.did(act.activation(un[:, k, :, i, :], chunked(z3[:, k, i, :]), ACT.Silu), f"s{n}")
                            for i, n in enumerate("kq"):
                                ac.wait(act, f"s{n}", it)
                                ac.did(act.activation(chunked(sq[:, i, :]), un[:, k, :, i, :], ACT.Square), f"q{n}")
                            for i, n in enumerate("kq"):
                                pe_.wait(act, f"n{n}", it)
                                ac.did(act.activation(rn[:, i, 0:CTX], ps[:, i, 0, 0:CTX], ACT.Ln, bias=eps[:]), f"l{n}0")
                                ac.did(act.activation(rn[:, i, CTX:T], lat(ps[:, i]), ACT.Ln, bias=eps[:]), f"l{n}1")
                            for i, n in enumerate("kq"):
                                ac.wait(act, f"l{n}1", it)
                                ac.did(act.activation(rn[:, i], rn[:, i], ACT.Exp, scale=-0.5), f"e{n}")

                @block.tensor
                def _(pe):
                    pe.wait_ge(s["gates"], 1)
                    for c in range(NCH):
                        for w, src in enumerate((GR, be)):
                            for d in range(2):
                                o = c * 16 + w * 8 + d * 4
                                mm = pe.transpose(pc[:, o:o + 4], src[:, d, c * P:c * P + P], K["ident"][0:4, 0:4])
                    mm.then_inc(s["cols"], 1)
                    with pe.Fori(0, 4) as it:
                        for i, n in enumerate("kq"):
                            ac.wait(pe, f"q{n}", it)
                            if i == 0:
                                ac.wait_before(pe, it)
                            for b, (x, y) in banks():
                                mm = pe.matmul(ps[:, i, b, 0:y - x], K["ones"][:], sq[:, i, x:y], start=True, stop=True)
                            pe_.did(mm, f"n{n}")

                @block.vector
                def _(dve):
                    link = chain(dve, s["d_chain"])
                    dve.memset(eps[:], 1e-6).then_inc(s["eps_set"], 1)
                    link(dve.memset(reset, 1.0))
                    for d in range(2):
                        link(dve.memset(chunked(reset[:, d, :])[:, :, d * (P - 1):d * (P - 1) + 1], 0.0))
                    dve.wait_ge(s["rows_in"], 32)
                    dve.wait_ge(s["params_in"], 32)
                    for d in range(2):
                        dve.tensor_scalar(al[:, d], al[:, d], prm[:, 1, d:d + 1], None, ALU.add).then_inc(s["x_ready"], 1)
                    dve.wait_ge(s["abs_done"], 1)
                    link(dve.tensor_scalar(prm[:, 0, :], prm[:, 0, :], -1.0, None, ALU.mult))
                    link(dve.scalar_tensor_tensor(out=al, in0=al, scalar=0.0, in1=t0, op0=ALU.max, op1=ALU.add))
                    for d in range(2):
                        link(dve.tensor_scalar(al[:, d], al[:, d], prm[:, 0, d:d + 1], None, ALU.mult))
                    for d in range(2):
                        sd = -1 if d else 1
                        link(dve.tensor_tensor_scan(GR[:, d, ::sd], reset[:, d, ::sd], al[:, d, ::sd], 0.0,
                                                    ALU.mult, ALU.add))
                    dve.nop().then_inc(s["gates"], 1)
                    with dve.Fori(0, 2) as j:
                        for k in range(2):
                            it = 2 * j + k
                            ac.wait(dve, "ek", it)
                            dv.did(dve.tensor_tensor(un[:, k, :, 0, :], un[:, k, :, 0, :], chunked(rn[:, 0]), ALU.mult), "k")
                            ac.wait(dve, "eq", it)
                            dv.did(dve.scalar_tensor_tensor(out=un[:, k, :, 1, :], in0=un[:, k, :, 1, :], scalar=HD_B ** -0.5,
                                                            in1=chunked(rn[:, 1]), op0=ALU.mult, op1=ALU.mult), "q")

                @block.gpsimd
                def _(pool):
                    with pool.Fori(0, 2) as j:
                        for k in range(2):
                            dv.wait(pool, "q", 2 * j + k)
                            pool.dma_start(qkv[2 * j + k].rearrange("p c u t -> p (c u t)"),
                                           un[:, k].rearrange("p c u t -> p (c u t)")).then_inc(stored[k], 16)
                    for k in range(2):
                        pool.wait_ge(stored[k], 32)


def gdn_scan_phase(nc, K, qkv, oscan, steps, state):
    GR, GC = K["GR"], K["GC"]
    with ExitStack() as ctx:
        B = {n: sbuf(ctx, nc, n, [P, 2, 2, 2, P]) for n in ("X", "Y", "W")}
        B["N"] = sbuf(ctx, nc, "N", [P, 2, 2, 2, 2, P])
        B["NM"] = sbuf(ctx, nc, "NM", [P, 2, NL, 2, 2, P])
        un = sbuf(ctx, nc, "gun", [P, 2, 2, 2, 3, P])
        idle = K["HT"][:].rearrange("p k t -> p (k t)")
        kt, vt, Dm, EG, QD, Rb, Ub, yt = [
            idle[:, n * 8 * P:(n + 1) * 8 * P].rearrange("p (g h d t) -> p g h d t", g=2, h=2, d=2) for n in range(8)]
        DM = sbuf(ctx, nc, "decay_masked", [P, 2, 2, 2, 2, P])
        cs = sbuf(ctx, nc, "chunk_cols", [P, 3, 2, 4])
        gr = sbuf(ctx, nc, "chunk_rows", [4, 2, P])
        ps = psum(ctx, nc, "gscan_ps", [P, 2, 4, 512])
        lanes = [(h, d) for h in range(2) for d in range(2)]
        with phase(nc, "dve", "act", "pool", "pe", "in0", "in1", "out0", "out1") as s:
            st = scan_steps(s, 2, ["gb", "tok", "a"], [["r"], ["u"], ["y", "s"]],
                            ["d0", "n", "qk"], [["R"], ["S"]],
                            ["D", "EG", "v", "k"], [["U"], ["yt"]], dve_head=["cs0", "cs1", "gr0", "gr1"])
            dv, ac, po, pe_ = st
            dv.names[4:10] = ["0d0", "1d0", "0n", "0qk", "1n", "1qk"]
            po.names[:] = (["0dm0", "0dm1", "1dm0", "1dm1"] + inverse_pool_names(0) + ["0qd", "1qd"])
            loaded, stored = [s["in0"], s["in1"]], [s["out0"], s["out1"]]
            u_src = qkv.rearrange("h p c u t -> h c p (u t)")
            o_dst = oscan.rearrange("d h p (c t) -> d h c p t", t=P)
            with nc.Block() as block:
                @block.sync
                def _(sp):
                    def body(it, cs_, wait):
                        for q in range(2):
                            for h, d in lanes:
                                early(sp, u_src[2 * q + h, cs_[d]])
                            if wait:
                                sp.lower_val(pe_.value(f"{q}s", it - 1))
                                sp.lower_val(po.value(f"{q}qd", it - 1))
                        for q in range(2):
                            if wait:
                                pe_.wait(sp, f"{q}s", it - 1)
                                po.wait(sp, f"{q}qd", it - 1)
                            for h, d in lanes:
                                sp.dma_start(un[:, q, h, d].rearrange("p u t -> p (u t)"),
                                             u_src[2 * q + h, cs_[d]]).then_inc(loaded[q], 16)
                    if steps == 1:
                        body(0, (0, 0), False)
                    else:
                        body(0, (1, steps), False)
                        with sp.Fori(1, steps) as it:
                            body(it, (it + 1, steps - it), True)

                @block.tensor
                def _(pe):
                    def body(it, c0, c1):
                        dv.wait(pe, "gr1", it)
                        dv.wait_before(pe, it)
                        ac.wait_before(pe, it)
                        st_it = [ItSteps(x, it) for x in st]
                        for q in range(2):
                            for i, (h, d) in enumerate(lanes):
                                mm = pe.matmul(ps[:, q, 0, i * P:i * P + P], K["sel"][0:4, 2 * q + h, :], gr[:, d, :],
                                               start=True, stop=True)
                            pe_.did(mm, f"{q}gb")
                            pe.wait_ge(loaded[q], it * 64 + 64)
                            for w, b in ((0, 2), (2, 3)):
                                for i, (h, d) in enumerate(lanes):
                                    mm = pe.transpose(ps[:, q, b, i * P:i * P + P], un[:, q, h, d, w, :], K["ident"][:])
                            pe_.did(mm, f"{q}tok")
                            ac.wait(pe, f"{q}EG", it)
                            dv.wait(pe, f"{q}d0", it)
                            for i, (h, d) in enumerate(lanes):
                                mm = pe.matmul(ps[:, q, h, d * 256:d * 256 + 256], un[:, q, h, d, 0, :],
                                               un[:, q, h, d, 0:2, :].rearrange("p u t -> p (u t)"), start=True, stop=True)
                            pe_.did(mm, f"{q}a")
                        for l in range(NL):
                            for q in range(2):
                                if l == 0:
                                    dv.wait(pe, f"{q}qk", it)
                                    ac.wait(pe, f"{q}k", it)
                                inverse_pe(pe, ps, st_it, K, B, q, q, l)
                            if l:
                                for q in range(2):
                                    inverse_pe2(pe, ps, st_it, K, B, q, q, l)
                        for q in range(2):
                            for i, (h, d) in enumerate(lanes):
                                mm = pe.matmul(ps[:, q, 0, i * P:i * P + P], un[:, q, h, d, 0, :], state[:, q, h, d, :],
                                               start=True, stop=True)
                            pe_.did(mm, f"{q}r")
                        for q in range(2):
                            dv.wait(pe, f"{q}X{NL - 1}", it)
                            dv.wait(pe, f"{q}R", it)
                            for i, (h, d) in enumerate(lanes):
                                mm = pe.matmul(ps[:, q, 2, i * P:i * P + P], B["X"][:, q, h, d, :], Rb[:, q, h, d, :],
                                               start=True, stop=True)
                            pe_.did(mm, f"{q}u")
                        for q in range(2):
                            ac.wait(pe, f"{q}U", it)
                            po.wait(pe, f"{q}qd", it)
                            for i, (h, d) in enumerate(lanes):
                                o = ps[:, q, 1, i * P:i * P + P]
                                pe.matmul(o, state[:, q, h, d, :], QD[:, q, h, d, :], start=True, stop=False)
                                mm = pe.matmul(o, Ub[:, q, h, d, :], B["N"][:, q, h, d, 1, :], start=False, stop=True)
                            pe_.did(mm, f"{q}y")
                            for i, (h, d) in enumerate(lanes):
                                mm = pe.matmul(ps[:, q, 3, i * P:i * P + P], kt[:, q, h, d, :], Ub[:, q, h, d, :],
                                               start=True, stop=True)
                            pe_.did(mm, f"{q}s")
                    scan_iterations(pe, steps, body)

                @block.scalar
                def _(act):
                    def body(it, c0, c1):
                        for q in range(2):
                            dv.wait(act, f"{q}d0", it)
                            ac.did(act.activation(four(Dm[:, q]), four(Dm[:, q]), ACT.Exp), f"{q}D")
                            ac.did(act.activation(four(EG[:, q]), ps[:, q, 0, :], ACT.Exp), f"{q}EG")
                            pe_.wait(act, f"{q}tok", it)
                            ac.did(act.activation(four(vt[:, q]), ps[:, q, 3, :], ACT.Copy), f"{q}v")
                            ac.wait(act, f"{q}D", it)
                            for i, (h, d) in enumerate(lanes):
                                e = 0 if d else P - 1
                                ins = act.activation(kt[:, q, h, d, :], ps[:, q, 2, i * P:i * P + P], ACT.Copy,
                                                     scale=Dm[:, q, h, d, e:e + 1])
                            ac.did(ins, f"{q}k")
                        for l in range(1, NL):
                            for q in range(2):
                                pe_.wait(act, f"{q}w{l}", it)
                                ac.did(act.activation(four(B["W"][:, q]), ps[:, q, 1, :], ACT.Copy), f"{q}W{l}")
                        for q in range(2):
                            pe_.wait(act, f"{q}u", it)
                            for i, (h, d) in enumerate(lanes):
                                ins = act.activation(Ub[:, q, h, d, :], ps[:, q, 2, i * P:i * P + P], ACT.Copy,
                                                     scale=cs[:, 2, d, 2 * q + h:2 * q + h + 1])
                            ac.did(ins, f"{q}U")
                        for q in range(2):
                            pe_.wait(act, f"{q}y", it)
                            act.wait_ge(stored[q], it * 64)
                            ac.did(act.activation(four(yt[:, q]), ps[:, q, 1, :], ACT.Copy), f"{q}yt")
                        for q in range(2):
                            ac.wait(act, f"{q}yt", it)
                            for h, d in lanes:
                                act.dma_start(o_dst[d, 2 * q + h, (c0, c1)[d]], yt[:, q, h, d, :]).then_inc(stored[q], 16)
                    scan_iterations(act, steps, body)
                    for q in range(2):
                        act.wait_ge(stored[q], steps * 64)

                @block.vector
                def _(dve):
                    def body(it, c0, c1):
                        dv.wait_before(dve, it)
                        ac.wait_before(dve, it)
                        pe_.wait_before(dve, it)
                        po.wait_before(dve, it)
                        for d, c in enumerate((c0, c1)):
                            dv.did(dve.tensor_copy(cs[:, :, d, :], GC[:, bass.ds(c, 1), :, d, :].rearrange("p o w h -> p (o w) h")),
                                   f"cs{d}")
                        for d, c in enumerate((c0, c1)):
                            dv.did(dve.tensor_copy(gr[:, d, :], GR[:, d, bass.ds(c * P, P)]), f"gr{d}")
                        dv.wait(dve, "cs1", it)
                        for q in range(2):
                            pe_.wait(dve, f"{q}gb", it)
                            for i, (h, d) in enumerate(lanes):
                                ins = dve.tensor_scalar(Dm[:, q, h, d, :], ps[:, q, 0, i * P:i * P + P],
                                                        cs[:, 0, d, 2 * q + h:2 * q + h + 1], 0.0, ALU.subtract, ALU.min)
                            dv.did(ins, f"{q}d0")
                        for q in range(2):
                            pe_.wait(dve, f"{q}a", it)
                            po.wait(dve, f"{q}dm1", it)
                            for i, (h, d) in enumerate(lanes):
                                ins = dve.scalar_tensor_tensor(out=B["N"][:, q, h, d, 0, :], in0=ps[:, q, h, d * 256:d * 256 + P],
                                                               scalar=cs[:, 2, d, 2 * q + h:2 * q + h + 1],
                                                               in1=DM[:, q, h, d, 0, :], op0=ALU.mult, op1=ALU.mult)
                            dv.did(ins, f"{q}n")
                            qk = ps[:, q, 0:2, :].rearrange("p h (d w t) -> p h d w t", d=2, w=2)[:, :, :, 1, :]
                            dv.did(dve.tensor_tensor(B["N"][:, q, :, :, 1, :], qk, DM[:, q, :, :, 1, :], ALU.mult), f"{q}qk")
                        st_it = [ItSteps(x, it) for x in st]
                        for l in range(NL):
                            for q in range(2):
                                inverse_dve(dve, ps, st_it, K, B, q, q, l)
                            if 0 < l < NL - 1:
                                for q in range(2):
                                    inverse_dve2(dve, ps, st_it, K, B, q, q, l)
                        for q in range(2):
                            pe_.wait(dve, f"{q}r", it)
                            ac.wait(dve, f"{q}v", it)
                            for i, (h, d) in enumerate(lanes):
                                ins = dve.scalar_tensor_tensor(out=Rb[:, q, h, d, :], in0=ps[:, q, 0, i * P:i * P + P],
                                                               scalar=cs[:, 1, d, 2 * q + h:2 * q + h + 1],
                                                               in1=vt[:, q, h, d, :], op0=ALU.mult, op1=ALU.add)
                            dv.did(ins, f"{q}R")
                        for q in range(2):
                            pe_.wait(dve, f"{q}s", it)
                            for i, (h, d) in enumerate(lanes):
                                e = 0 if d else P - 1
                                ins = dve.scalar_tensor_tensor(out=state[:, q, h, d, :], in0=state[:, q, h, d, :],
                                                               scalar=EG[:, q, h, d, e:e + 1], in1=ps[:, q, 3, i * P:i * P + P],
                                                               op0=ALU.mult, op1=ALU.add)
                            dv.did(ins, f"{q}S")
                    scan_iterations(dve, steps, body)

                @block.gpsimd
                def _(pool):
                    def body(it, c0, c1):
                        for q in range(2):
                            ac.wait(pool, f"{q}D", it)
                            for h in range(2):
                                po.did(pool.tensor_tensor(DM[:, q, h], Dm[:, q, h, :, None, :].to_broadcast([P, 2, 2, P]),
                                                          K["order"][:], ALU.mult), f"{q}dm{h}")
                        st_it = [ItSteps(x, it) for x in st]
                        for q in range(2):
                            dv.wait(pool, f"{q}n", it)
                            inverse_pool(pool, st_it, K, B, q, q, (0, 1))
                        for l in range(2, NL):
                            for q in range(2):
                                inverse_pool(pool, st_it, K, B, q, q, (l,))
                        for q in range(2):
                            ac.wait(pool, f"{q}EG", it)
                            pool.wait_ge(loaded[q], it * 64 + 64)
                            po.did(pool.tensor_tensor(QD[:, q], un[:, q, :, :, 1, :], EG[:, q], ALU.mult), f"{q}qd")
                    scan_iterations(pool, steps, body)


def zero_states_phase(nc, tiles):
    with phase(nc, "zeroed") as s:
        with nc.Block() as block:
            @block.vector
            def _(dve):
                for t in tiles:
                    dve.memset(t, 0.0).then_inc(s["zeroed"], 1)
                dve.wait_ge(s["zeroed"], len(tiles))


def turn_states_phase(nc, K, outs, ins):
    n_out, n_in = sum(len(x[2]) for x in outs), sum(len(x[2]) for x in ins)
    with ExitStack() as ctx:
        ps = psum(ctx, nc, "state_ps", [P, 8, 512])
        with phase(nc, "loaded", "out_t", "out_c", "in_t", "in_c", "stored") as s:
            jobs_out = [j for x in outs for j in x[2]]
            jobs_in = [j for x in ins for j in x[2]]
            with nc.Block() as block:
                @block.sync
                def _(sp):
                    n = 0
                    for dram, stage, _ in ins:
                        for d, t in zip(dram, stage):
                            sp.dma_start(t, d).then_inc(s["loaded"], 16)
                    sp.wait_ge(s["out_c"], n_out)
                    for dram, stage, _ in outs:
                        for d, t in zip(dram, stage):
                            sp.dma_start(d, t).then_inc(s["stored"], 16)
                            n += 16
                    sp.wait_ge(s["stored"], n)

                def out_ps(n, src):
                    return ps[0:src.shape[1], n % 8, 0:src.shape[0]]

                @block.tensor
                def _(pe):
                    for n, (state, stage) in enumerate(jobs_out):
                        if n >= 8:
                            pe.wait_ge(s["out_c"], n - 7)
                        pe.transpose(out_ps(n, state), state, K["ident"][:]).then_inc(s["out_t"], 1)
                    pe.wait_ge(s["loaded"], 16 * sum(len(x[0]) for x in ins))
                    pe.wait_ge(s["out_c"], n_out)
                    for n, (state, stage) in enumerate(jobs_in):
                        if n >= 8:
                            pe.wait_ge(s["in_c"], n - 7)
                        k = stage.shape[0]
                        pe.transpose(out_ps(n, stage), stage, K["ident"][0:k, 0:k]).then_inc(s["in_t"], 1)

                @block.vector
                def _(dve):
                    for n, (state, stage) in enumerate(jobs_out):
                        dve.wait_ge(s["out_t"], n + 1)
                        dve.tensor_copy(stage, out_ps(n, state)).then_inc(s["out_c"], 1)
                    for n, (state, stage) in enumerate(jobs_in):
                        dve.wait_ge(s["in_t"], n + 1)
                        dve.tensor_copy(state, out_ps(n, stage)).then_inc(s["in_c"], 1)


def even_states(nc, ctx, A, rk_out, gd_out, rk_state, gd_state):
    r_o = sbuf(ctx, nc, "rk_stage_out", [64, 2, 4, P])
    r_i = sbuf(ctx, nc, "rk_stage_in", [64, 2, 4, P])
    g_o = sbuf(ctx, nc, "gd_stage_out", [P, 2, 4, P])
    g_i = sbuf(ctx, nc, "gd_stage_in", [P, 2, 4, P])

    def entry(rk, gd, r, g, out):
        rd = [rk[0, 0, d].rearrange("h v k -> v h k") for d in range(2)]
        gdd = [gd[0, 0, d].rearrange("h v k -> v h k") for d in range(2)]
        return [
            (rd, [r[:, d].rearrange("v q (h k) -> v (q h) k", h=2) for d in range(2)],
             [(rk_state[:, q, d, :], r[:, d, q, :]) for d in range(2) for q in range(4)]),
            (gdd, [g[:, d] for d in range(2)],
             [(gd_state[:, h // 2, h % 2, d, :], g[:, d, h, :]) for d in range(2) for h in range(4)]),
        ]
    return entry(rk_out, gd_out, r_o, g_o, True), entry(A["state_rwkv"], A["state_gdn"], r_i, g_i, False)


def odd_states(nc, ctx, A, c_out, n_out, state):
    c_o = sbuf(ctx, nc, "c_stage_out", [P, 2, 4, P])
    c_i = sbuf(ctx, nc, "c_stage_in", [P, 2, 4, P])
    n_o = sbuf(ctx, nc, "n_stage_out", [4, 2, P])
    n_i = sbuf(ctx, nc, "n_stage_in", [4, 2, P])

    def entry(c, n, cs, ns):
        return [
            ([c[0, 0, d].rearrange("h v k -> v h k") for d in range(2)],
             [cs[:, d].rearrange("v q (h k) -> v (q h) k", h=2) for d in range(2)],
             [(state[:, q, d, 0:P], cs[:, d, q, :]) for d in range(2) for q in range(4)]),
            ([n[0, 0, d].rearrange("(q h) k -> q (h k)", h=2) for d in range(2)],
             [ns[:, d, :] for d in range(2)],
             [(state[:, :, d, P], ns[:, d, :]) for d in range(2)]),
        ]
    return entry(c_out, n_out, c_o, n_o), entry(A["state_mlstm_c"], A["state_mlstm_n"], c_i, n_i)


def rwkv_post_phase(nc, A, K, zc, yscan, bonus):
    HT, PT = K["HT"], K["PT"]
    with ExitStack() as ctx:
        gd = sbuf(ctx, nc, "gd", [P, T])
        y3 = sbuf(ctx, nc, "y_fwd_bwd_bonus", [P, 2, 3, T])
        gu = sbuf(ctx, nc, "g_up", [P, 2, P])
        sq = sbuf(ctx, nc, "y_sq", [P, T])
        rs = sbuf(ctx, nc, "y_rstd", [P, T])
        lnp = sbuf(ctx, nc, "ln_params", [P, 2])
        eps = sbuf(ctx, nc, "ln_eps", [P, 1])
        ps = psum(ctx, nc, "post_ps", [P, 2, 3, 512])
        par = PT[:, C_LNG:C_LNG + 8].rearrange("p (g q) -> p g q", q=4)
        with phase(nc, "gd_in", "gd_ok", "in0", "in1", "dve", "act", "pe", "eps_set") as s:
            dv = Steps(s["dve"], ["par", "y", "yc_c", "yc_l", "yn", "ya", "yb", "o_c", "o_l"])
            ac = Steps(s["act"], ["sq", "ln_c", "ln_l", "rs"])
            pe_ = Steps(s["pe"], ["sum", "var", "g"])
            loaded = [s["in0"], s["in1"]]
            g_src = A["rk_g_up"][0].rearrange("r (q c) -> q r c", c=P)
            with nc.Block() as block:
                @block.sync
                def _(sp):
                    sp.dma_start(gd[:], zc[14]).then_inc(s["gd_in"], 16)
                    for q in range(4):
                        if q >= 2:
                            dv.wait(sp, "o_l", q - 2)
                        for i, src in enumerate((yscan[0, q], yscan[1, q], bonus[q])):
                            sp.dma_start(y3[:, q % 2, i, :], src).then_inc(loaded[q % 2], 16)
                        sp.dma_start(gu[:, q % 2, :], g_src[q]).then_inc(loaded[q % 2], 16)

                @block.tensor
                def _(pe):
                    with pe.Fori(0, 2) as j:
                        for k in range(2):
                            it = 2 * j + k
                            dv.wait(pe, "y", it)
                            for b, (x, y) in banks():
                                mm = pe.matmul(ps[:, 0, b, 0:y - x], K["ones64"][:], y3[:, k, 0, x:y], start=True, stop=True)
                            pe_.did(mm, "sum")
                            ac.wait(pe, "sq", it)
                            for b, (x, y) in banks():
                                mm = pe.matmul(ps[:, 1, b, 0:y - x], K["ones64"][:], sq[:, x:y], start=True, stop=True)
                            pe_.did(mm, "var")
                            pe.wait_ge(s["gd_ok"], 1)
                            dv.wait(pe, "yc_l", it)
                            for b, (x, y) in banks():
                                mm = pe.matmul(ps[:, 0, b, 0:y - x], gu[:, k, :], gd[:, x:y], start=True, stop=True)
                            pe_.did(mm, "g")

                @block.scalar
                def _(act):
                    act.wait_ge(s["gd_in"], 16)
                    act.activation(gd[:], gd[:], ACT.Sigmoid).then_inc(s["gd_ok"], 1)
                    act.wait_ge(s["eps_set"], 1)
                    with act.Fori(0, 2) as j:
                        for k in range(2):
                            it = 2 * j + k
                            dv.wait(act, "yc_l", it)
                            ac.did(act.activation(sq[:], y3[:, k, 0, :], ACT.Square), "sq")
                            pe_.wait(act, "var", it)
                            ac.did(act.activation(rs[:, 0:CTX], ps[:, 1, 0, 0:CTX], ACT.Ln, scale=1.0 / HD_A, bias=eps[:]), "ln_c")
                            ac.did(act.activation(rs[:, CTX:T], lat(ps[:, 1]), ACT.Ln, scale=1.0 / HD_A, bias=eps[:]), "ln_l")
                            ac.wait(act, "ln_l", it)
                            ac.did(act.activation(rs[:], rs[:], ACT.Exp, scale=-0.5), "rs")

                @block.vector
                def _(dve):
                    dve.memset(eps[:], RWKV_LN_EPS).then_inc(s["eps_set"], 1)
                    with dve.Fori(0, 2) as j:
                        for k in range(2):
                            it = 2 * j + k
                            y, yb, bn = [y3[:, k, i, :] for i in range(3)]
                            dv.wait_before(dve, it)
                            dv.did(dve.tensor_copy(lnp[:], par[:, :, bass.ds(it, 1)].rearrange("p g o -> p (g o)")), "par")
                            dve.wait_ge(loaded[k], j * 64 + 64)
                            dv.did(dve.tensor_tensor(y, y, yb, ALU.add), "y")
                            pe_.wait(dve, "sum", it)
                            for n, (x, z), p in (("c", (0, CTX), ps[:, 0, 0, 0:CTX]), ("l", (CTX, T), lat(ps[:, 0]))):
                                dv.did(dve.scalar_tensor_tensor(out=y[:, x:z], in0=p, scalar=-1.0 / HD_A, in1=y[:, x:z],
                                                                op0=ALU.mult, op1=ALU.add), f"yc_{n}")
                            ac.wait(dve, "rs", it)
                            dv.did(dve.tensor_tensor(y, y, rs[:], ALU.mult), "yn")
                            dv.wait(dve, "yn", it)
                            dv.did(dve.tensor_scalar(y, y, lnp[:, 0:1], lnp[:, 1:2], ALU.mult, ALU.add), "ya")
                            dv.wait(dve, "ya", it)
                            dv.did(dve.tensor_tensor(y, y, bn, ALU.add), "yb")
                            dv.wait(dve, "yb", it)
                            pe_.wait(dve, "g", it)
                            for n, (x, z), p in (("c", (0, CTX), ps[:, 0, 0, 0:CTX]), ("l", (CTX, T), lat(ps[:, 0]))):
                                dv.did(dve.tensor_tensor(HT[:, it, x:z], y[:, x:z], p, ALU.mult), f"o_{n}")


def gdn_post_phase(nc, K, zc, oscan):
    HT, PT = K["HT"], K["PT"]
    with ExitStack() as ctx:
        o3 = sbuf(ctx, nc, "o_fwd_bwd_gate", [P, 2, 3, T])
        sq = sbuf(ctx, nc, "o_sq", [P, T])
        rs = sbuf(ctx, nc, "o_rstd", [P, T])
        eps = sbuf(ctx, nc, "o_eps", [P, 1])
        ps = psum(ctx, nc, "gpost_ps", [P, 3, 512])
        with phase(nc, "in0", "in1", "dve", "act", "pe", "eps_set") as s:
            dv = Steps(s["dve"], ["o", "on", "out"])
            ac = Steps(s["act"], ["silu", "sq", "ln_c", "ln_l", "rs"])
            pe_ = Steps(s["pe"], ["sum"])
            loaded = [s["in0"], s["in1"]]
            with nc.Block() as block:
                @block.sync
                def _(sp):
                    for h in range(4):
                        if h >= 2:
                            dv.wait(sp, "out", h - 2)
                        for i, src in enumerate((oscan[0, h], oscan[1, h], zc[27 + h])):
                            sp.dma_start(o3[:, h % 2, i, :], src).then_inc(loaded[h % 2], 16)

                @block.tensor
                def _(pe):
                    with pe.Fori(0, 4) as it:
                        ac.wait(pe, "sq", it)
                        for b, (x, y) in banks():
                            mm = pe.matmul(ps[:, b, 0:y - x], K["ones"][:], sq[:, x:y], start=True, stop=True)
                        pe_.did(mm, "sum")

                @block.scalar
                def _(act):
                    act.wait_ge(s["eps_set"], 1)
                    with act.Fori(0, 2) as j:
                        for k in range(2):
                            it = 2 * j + k
                            act.wait_ge(loaded[k], j * 48 + 48)
                            ac.did(act.activation(o3[:, k, 2, :], o3[:, k, 2, :], ACT.Silu), "silu")
                            dv.wait(act, "o", it)
                            ac.did(act.activation(sq[:], o3[:, k, 0, :], ACT.Square), "sq")
                            pe_.wait(act, "sum", it)
                            ac.did(act.activation(rs[:, 0:CTX], ps[:, 0, 0:CTX], ACT.Ln, scale=1.0 / HD_B, bias=eps[:]), "ln_c")
                            ac.did(act.activation(rs[:, CTX:T], lat(ps), ACT.Ln, scale=1.0 / HD_B, bias=eps[:]), "ln_l")
                            ac.wait(act, "ln_l", it)
                            ac.did(act.activation(rs[:], rs[:], ACT.Exp, scale=-0.5), "rs")

                @block.vector
                def _(dve):
                    dve.memset(eps[:], RMS_EPS).then_inc(s["eps_set"], 1)
                    with dve.Fori(0, 2) as j:
                        for k in range(2):
                            it = 2 * j + k
                            o, ob, gt = [o3[:, k, i, :] for i in range(3)]
                            dve.wait_ge(loaded[k], j * 48 + 48)
                            dv.did(dve.tensor_tensor(o, o, ob, ALU.add), "o")
                            ac.wait(dve, "rs", it)
                            dv.did(dve.tensor_tensor(o, o, rs[:], ALU.mult), "on")
                            dv.wait(dve, "on", it)
                            dv.did(dve.scalar_tensor_tensor(out=HT[:, 4 + it, :], in0=o, scalar=PT[:, C_GDN:C_GDN + 1], in1=gt,
                                                            op0=ALU.mult, op1=ALU.mult), "out")


def mlstm_prep_phase(nc, A, K, ztail, m_out):
    MN, MC, WE = K["MN"], K["MC"], K["WE"]
    with ExitStack() as ctx:
        g = sbuf(ctx, nc, "gates", [8, 4, T])
        t0 = sbuf(ctx, nc, "softplus", [8, 2, T])
        bs = sbuf(ctx, nc, "b_sum", [8, 2, T])
        en = sbuf(ctx, nc, "minus_m", [8, 2, T])
        wi = sbuf(ctx, nc, "m_minus_M", [8, 2, T])
        reset = sbuf(ctx, nc, "ml_reset", [8, 2, T])
        gb = sbuf(ctx, nc, "gate_bias", [8, 4])
        m0 = sbuf(ctx, nc, "m_latent", [8, 2])
        mp = sbuf(ctx, nc, "m_before", [8, 2, NCH + 1])
        me = sbuf(ctx, nc, "m_ctx_end", [8, 2])
        we = sbuf(ctx, nc, "w_end", [8, 2, NCH])
        pc = psum(ctx, nc, "ml_cols", [P, 512])
        pw = psum(ctx, nc, "ml_we", [P, 512])
        with phase(nc, "in", "bias_in", "bias_ok", "tanh", "abs_ready", "sp", "rows", "we_ok", "cols", "we_ps", "link_d",
                   "link_a", "m_stored", "ctx_m") as s:
            with nc.Block() as block:
                @block.sync
                def _(sp):
                    sp.dma_start(g[:], ztail.rearrange("(g h) t -> h g t", g=4)).then_inc(s["in"], 16)
                    sp.dma_start(gb[:], A["ml_gate_b"].rearrange("l (g h) -> h (l g)", g=4),
                                 allow_slow_non_contiguous=True).then_inc(s["bias_in"], 16)
                    sp.dma_start(m0[:], A["state_mlstm_m"].rearrange("a l d h -> h (a l d)"),
                                 allow_slow_non_contiguous=True).then_inc(s["bias_in"], 16)
                    sp.wait_ge(s["ctx_m"], 1)
                    sp.dma_start(m_out.rearrange("a l d h -> h (a l d)"), me[:],
                                 allow_slow_non_contiguous=True).then_inc(s["m_stored"], 16)
                    sp.wait_ge(s["m_stored"], 16)

                @block.scalar
                def _(act):
                    link = chain(act, s["link_a"])
                    act.wait_ge(s["bias_ok"], 1)
                    act.wait_ge(s["in"], 16)
                    for i in range(4):
                        act.activation(g[:, i], g[:, i], ACT.Tanh, scale=1.0 / GATE_CAP, bias=gb[:, i:i + 1]).then_inc(s["tanh"], 1)
                    act.wait_ge(s["abs_ready"], 1)
                    link(act.activation(t0[:], g[:, 2:4], ACT.Abs))
                    link(act.activation(t0[:], t0[:], ACT.Exp, scale=-1.0))
                    link(act.activation(t0[:], t0[:], ACT.Ln, bias=1.0))
                    act.nop().then_inc(s["sp"], 1)
                    act.wait_ge(s["rows"], 1)
                    link(act.activation(we[:], we[:], ACT.Exp))
                    act.nop().then_inc(s["we_ok"], 1)
                    act.wait_ge(s["cols"], 1)
                    cols = pc[:, 0:NCH * 48].rearrange("p (c w x) -> p c w x", c=NCH, w=3)
                    out = MC[:].rearrange("p c w d h -> p c w (d h)")
                    link(act.activation(out[:, :, 0, :], cols[:, :, 0, :], ACT.Copy))
                    link(act.activation(out[:, :, 1:3, :], cols[:, :, 1:3, :], ACT.Exp))
                    act.wait_ge(s["we_ps"], 1)
                    link(act.activation(WE[:].rearrange("p q d c -> p (q d c)"), pw[:, 0:8 * NCH], ACT.Copy))

                @block.vector
                def _(dve):
                    link = chain(dve, s["link_d"])
                    dve.wait_ge(s["bias_in"], 32)
                    link(dve.tensor_scalar(gb[:], gb[:], 1.0 / GATE_CAP, None, ALU.mult))
                    dve.nop().then_inc(s["bias_ok"], 1)
                    link(dve.memset(reset[:], 1.0))
                    for d in range(2):
                        link(dve.memset(chunked(reset[:, d, :])[:, :, d * (P - 1):d * (P - 1) + 1], 0.0))
                    link(dve.memset(mp[:], 0.0))
                    for d in range(2):
                        link(dve.tensor_copy(mp[:, d, 1:2], m0[:, d:d + 1]))
                    dve.wait_ge(s["tanh"], 4)
                    link(dve.tensor_scalar(g[:], g[:], GATE_CAP, None, ALU.mult))
                    dve.nop().then_inc(s["abs_ready"], 1)
                    dve.wait_ge(s["sp"], 1)
                    link(dve.scalar_tensor_tensor(out=g[:, 2:4], in0=g[:, 2:4], scalar=0.0, in1=t0[:], op0=ALU.min,
                                                  op1=ALU.subtract))
                    for d in range(2):
                        sd = -1 if d else 1
                        link(dve.tensor_tensor_scan(bs[:, d, ::sd], reset[:, d, ::sd], g[:, 2 + d, ::sd], 0.0,
                                                    ALU.mult, ALU.add))
                    link(dve.tensor_tensor(g[:, 0:2], g[:, 0:2], bs[:], ALU.subtract))
                    for n in range(NCH):
                        for d in range(2):
                            c = n if (n == 0 or d == 0) else NCH - n
                            x = slice(c * P, c * P + P)
                            sd = -1 if d else 1
                            e = c * P + (0 if d else P - 1)
                            a, M = g[:, d, x][:, ::sd], MN[:, d, x][:, ::sd]
                            link(dve.tensor_tensor_scan(M, a, a, mp[:, d, n:n + 1], ALU.max, ALU.max))
                            link(dve.tensor_scalar(wi[:, d, x], MN[:, d, x], -1.0, mp[:, d, n:n + 1], ALU.mult, ALU.add))
                            if n == 0:
                                link(dve.tensor_tensor(me[:, d:d + 1], bs[:, d, e:e + 1], MN[:, d, e:e + 1], ALU.add))
                            else:
                                link(dve.tensor_tensor(mp[:, d, n + 1:n + 2], bs[:, d, e:e + 1], MN[:, d, e:e + 1], ALU.add))\
                                    if n < NCH - 1 else None
                        if n == 0:
                            dve.nop().then_inc(s["ctx_m"], 1)
                    for d in range(2):
                        e = chunked(wi[:, d])[:, :, (0 if d else P - 1):(1 if d else P)]
                        link(dve.tensor_copy(we[:, d, :], e.rearrange("p c o -> p (c o)")))
                    link(dve.scalar_tensor_tensor(out=en[:], in0=MN[:], scalar=-1.0, in1=bs[:], op0=ALU.mult, op1=ALU.subtract))
                    link(dve.tensor_scalar(MN[:], MN[:], -1.0, None, ALU.mult))
                    dve.nop().then_inc(s["rows"], 1)

                @block.tensor
                def _(pe):
                    pe.wait_ge(s["rows"], 1)
                    for c in range(NCH):
                        for w, src in enumerate((g, wi, en)):
                            for d in range(2):
                                o = c * 48 + w * 16 + d * 8
                                mm = pe.transpose(pc[:, o:o + 8], src[:, d, c * P:c * P + P], K["ident"][0:8, 0:8])
                    mm.then_inc(s["cols"], 1)
                    pe.wait_ge(s["we_ok"], 1)
                    for q in range(4):
                        mm = pe.matmul(pw[:, q * 2 * NCH:(q + 1) * 2 * NCH], K["selpair"][:, q, :],
                                       we[:].rearrange("p d c -> p (d c)"), start=True, stop=True)
                    mm.then_inc(s["we_ps"], 1)


V1 = DV_C + 1


def mlstm_scan_phase(nc, K, zc, hscan, steps, state):
    MN, MC, WE = K["MN"], K["MC"], K["WE"]
    with ExitStack() as ctx:
        kq = sbuf(ctx, nc, "kq", [P, 4, 2, 2, P])
        vv = sbuf(ctx, nc, "mv", [P, 4, 2, 2, P])
        Wt, Wm, St = [sbuf(ctx, nc, n, [P, 2, 2, 2, P]) for n in ("w_raw", "w_intra", "s_intra")]
        Ht = sbuf(ctx, nc, "h_tok", [P, 4, 2, 2, P])
        kt = sbuf(ctx, nc, "mk_tok", [P, 2, 2, 2, 64])
        vt, NI = [sbuf(ctx, nc, n, [P, 2, 2, 2, V1]) for n in ("mv_tok", "num_inter")]
        den = sbuf(ctx, nc, "den", [P, 2, 2, 2])
        cs = sbuf(ctx, nc, "ml_cols", [P, 3, 2, 8])
        mn = sbuf(ctx, nc, "ml_rows", [8, 2, P])
        we = sbuf(ctx, nc, "ml_wend", [P, 2, 4])
        ps = psum(ctx, nc, "mscan_ps", [P, 2, 4, 512])
        lanes = [(h, d) for h in range(2) for d in range(2)]
        with phase(nc, "dve", "act", "pool", "pe", "ones_set", *[f"in{q}" for q in range(4)], *[f"out{q}" for q in range(4)]) as s:
            dv, ac, po, pe_ = scan_steps(s, 4, ["mb", "tok", "a"], [["num", "inter"], ["c"]],
                                         ["w0", "k", "s"], [["tot", "abs", "max", "rec", "h"], ["C"]],
                                         ["W", "v"], [["I"]],
                                         dve_head=["cs0", "cs1", "mn0", "mn1", "we0", "we1"], inverse=False)
            po.names[:] = [f"{q}wm" for q in range(4)]
            loaded = [s[f"in{q}"] for q in range(4)]
            stored = [s[f"out{q}"] for q in range(4)]
            z_src = zc.rearrange("m p (c t) -> m c p t", t=P)
            with nc.Block() as block:
                @block.sync
                def _(sp):
                    def body(it, cc, wait):
                        for q in range(4):
                            for d in range(2):
                                early(sp, z_src[4 + q, cc[d]], z_src[q, cc[d]], z_src[8 + 2 * q, cc[d]], z_src[9 + 2 * q, cc[d]])
                        for q in range(4):
                            if wait:
                                pe_.wait(sp, f"{q}inter", it - 1)
                            for d in range(2):
                                sp.dma_start(kq[:, q, d, 0, :], z_src[4 + q, cc[d]]).then_inc(loaded[q], 16)
                                sp.dma_start(kq[:, q, d, 1, :], z_src[q, cc[d]]).then_inc(loaded[q], 16)
                                for h in range(2):
                                    sp.dma_start(vv[:, q, h, d, :], z_src[8 + 2 * q + h, cc[d]]).then_inc(loaded[q], 16)
                    if steps == 1:
                        body(0, (0, 0), False)
                    else:
                        body(0, (1, steps), False)
                        with sp.Fori(1, steps) as it:
                            body(it, (it + 1, steps - it), True)

                @block.tensor
                def _(pe):
                    def body(it, c0, c1):
                        dv.wait(pe, "mn1", it)
                        for a in (0, 2):
                            for q in (a, a + 1):
                                g = q - a
                                if a == 0:
                                    dv.wait_before(pe, it)
                                    ac.wait_before(pe, it)
                                else:
                                    dv.wait(pe, f"{g}C", it)
                                for i, (h, d) in enumerate(lanes):
                                    mm = pe.matmul(ps[:, g, 0, i * P:i * P + P], K["sel"][:, 2 * q + h, :], mn[:, d, :],
                                                   start=True, stop=True)
                                pe_.did(mm, f"{q}mb")
                                pe.wait_ge(loaded[q], it * 128 + 128)
                                for d in range(2):
                                    pe.transpose(ps[:, g, 1, d * P:d * P + P], kq[:, q, d, 0, :], K["ident"][:])
                                for i, (h, d) in enumerate(lanes):
                                    mm = pe.transpose(ps[:, g, 2, i * P:i * P + P], vv[:, q, h, d, :], K["ident"][:])
                                pe_.did(mm, f"{q}tok")
                                for h, o in ((0, ps[:, g, 1, 256:512]), (1, ps[:, g, 3, 0:256])):
                                    x = slice(64 * h, 64 * h + 64)
                                    for d in range(2):
                                        mm = pe.matmul(o[:, d * P:d * P + P], kq[x, q, d, 0, :], kq[x, q, d, 1, :],
                                                       start=True, stop=True)
                                pe_.did(mm, f"{q}a")
                            for q in (a, a + 1):
                                g = q - a
                                dv.wait(pe, f"{q}s", it)
                                ac.wait(pe, f"{q}v", it)
                                for h in range(2):
                                    for d in range(2):
                                        mm = pe.matmul(ps[:, g, 2 + h, d * V1:d * V1 + V1], St[:, g, h, d, :], vt[:, g, h, d, :],
                                                       start=True, stop=True)
                                pe_.did(mm, f"{q}num")
                                for h in range(2):
                                    x = slice(64 * h, 64 * h + 64)
                                    for d in range(2):
                                        mm = pe.matmul(ps[:, g, h, d * V1:d * V1 + V1], kq[x, q, d, 1, :], state[x, q, d, :],
                                                       start=True, stop=True)
                                pe_.did(mm, f"{q}inter")
                            for q in (a, a + 1):
                                g = q - a
                                ac.wait(pe, f"{q}I", it)
                                for h in range(2):
                                    x = slice(64 * h, 64 * h + 64)
                                    for d in range(2):
                                        mm = pe.matmul(ps[x, g, 0, d * V1:d * V1 + V1], kt[:, g, h, d, :], vt[:, g, h, d, :],
                                                       start=True, stop=True)
                                pe_.did(mm, f"{q}c")
                    scan_iterations(pe, steps, body)

                @block.scalar
                def _(act):
                    act.wait_ge(s["ones_set"], 1)

                    def body(it, c0, c1):
                        for a in (0, 2):
                            for q in (a, a + 1):
                                g = q - a
                                dv.wait(act, f"{q}w0", it)
                                ac.did(act.activation(four(Wt[:, g]), four(Wt[:, g]), ACT.Exp), f"{q}W")
                                pe_.wait(act, f"{q}tok", it)
                                ac.did(act.activation(vt[:, g, :, :, 0:P].rearrange("p h d v -> p (h d) v"),
                                                      ps[:, g, 2, :].rearrange("p (l v) -> p l v", v=P), ACT.Copy), f"{q}v")
                            for q in (a, a + 1):
                                g = q - a
                                pe_.wait(act, f"{q}inter", it)
                                for h, d in lanes:
                                    ins = act.activation(NI[:, g, h, d, :], ps[:, g, h, d * V1:d * V1 + V1], ACT.Copy,
                                                         scale=cs[:, 1, d, 2 * q + h:2 * q + h + 1])
                                ac.did(ins, f"{q}I")
                            for q in (a, a + 1):
                                dv.wait(act, f"{q}h", it)
                                for d, c in enumerate((c0, c1)):
                                    act.dma_start(hscan[d, c][:, q * 256:q * 256 + 256],
                                                  Ht[:, q, d].rearrange("p h v -> p (h v)")).then_inc(stored[q], 16)
                    scan_iterations(act, steps, body)
                    for q in range(4):
                        act.wait_ge(stored[q], steps * 32)

                @block.vector
                def _(dve):
                    dve.memset(vt[:], 1.0).then_inc(s["ones_set"], 1)

                    def body(it, c0, c1):
                        dv.wait_before(dve, it)
                        ac.wait_before(dve, it)
                        pe_.wait_before(dve, it)
                        for d, c in enumerate((c0, c1)):
                            dv.did(dve.tensor_copy(cs[:, :, d, :], MC[:, bass.ds(c, 1), :, d, :].rearrange("p o w h -> p (o w) h")),
                                   f"cs{d}")
                        for d, c in enumerate((c0, c1)):
                            dv.did(dve.tensor_copy(mn[:, d, :], MN[:, d, bass.ds(c * P, P)]), f"mn{d}")
                        for d, c in enumerate((c0, c1)):
                            dv.did(dve.tensor_copy(we[:, d, :], WE[:, :, d, bass.ds(c, 1)].rearrange("p q o -> p (q o)")), f"we{d}")
                        dv.wait(dve, "we1", it)
                        for a in (0, 2):
                            for q in (a, a + 1):
                                g = q - a
                                pe_.wait(dve, f"{q}mb", it)
                                for i, (h, d) in enumerate(lanes):
                                    ins = dve.tensor_scalar(Wt[:, g, h, d, :], ps[:, g, 0, i * P:i * P + P],
                                                            cs[:, 0, d, 2 * q + h:2 * q + h + 1], 0.0, ALU.add, ALU.min)
                                dv.did(ins, f"{q}w0")
                                po.wait(dve, f"{q}wm", it)
                                pe_.wait(dve, f"{q}a", it)
                                for h, d in lanes:
                                    e = 0 if d else P - 1
                                    ins = dve.tensor_scalar(kt[:, g, h, d, :], ps[:, g, 1, d * P + 64 * h:d * P + 64 * h + 64],
                                                            Wm[:, g, h, d, e:e + 1], DK_C ** -0.5, ALU.mult, ALU.mult)
                                dv.did(ins, f"{q}k")
                                for h, o in ((0, ps[:, g, 1, 256:512]), (1, ps[:, g, 3, 0:256])):
                                    ins = dve.scalar_tensor_tensor(out=St[:, g, h].rearrange("p d t -> p (d t)"), in0=o,
                                                                   scalar=DK_C ** -0.5,
                                                                   in1=Wm[:, g, h].rearrange("p d t -> p (d t)"),
                                                                   op0=ALU.mult, op1=ALU.mult)
                                dv.did(ins, f"{q}s")
                            for q in (a, a + 1):
                                g = q - a
                                ac.wait(dve, f"{q}I", it)
                                pe_.wait(dve, f"{q}num", it)
                                for h in range(2):
                                    v = NI[:, g, h].rearrange("p d v -> p (d v)")
                                    ins = dve.tensor_tensor(v, v, ps[:, g, 2 + h, 0:2 * V1], ALU.add)
                                dv.did(ins, f"{q}tot")
                                dv.wait(dve, f"{q}tot", it)
                                dv.did(dve.scalar_tensor_tensor(out=den[:, g], in0=NI[:, g, :, :, P], scalar=-1.0,
                                                                in1=NI[:, g, :, :, P], op0=ALU.mult, op1=ALU.max), f"{q}abs")
                                dv.wait(dve, f"{q}abs", it)
                                dv.did(dve.tensor_tensor(den[:, g], den[:, g], cs[:, 2, :, 2 * q:2 * q + 2].rearrange("p d h -> p h d"),
                                                         ALU.max), f"{q}max")
                                dv.wait(dve, f"{q}max", it)
                                dv.did(dve.reciprocal(den[:, g], den[:, g]), f"{q}rec")
                                dv.wait(dve, f"{q}rec", it)
                                dve.wait_ge(stored[q], it * 32)
                                dv.did(dve.tensor_tensor(Ht[:, q].rearrange("p d h v -> p h d v"), NI[:, g, :, :, 0:P],
                                                         den[:, g, :, :, None].to_broadcast([P, 2, 2, P]), ALU.mult), f"{q}h")
                            for q in (a, a + 1):
                                pe_.wait(dve, f"{q}c", it)
                                for d in range(2):
                                    ins = dve.scalar_tensor_tensor(out=state[:, q, d, :], in0=state[:, q, d, :],
                                                                   scalar=we[:, d, q:q + 1], in1=ps[:, q - a, 0, d * V1:d * V1 + V1],
                                                                   op0=ALU.mult, op1=ALU.add)
                                dv.did(ins, f"{q}C")
                    scan_iterations(dve, steps, body)

                @block.gpsimd
                def _(pool):
                    def body(it, c0, c1):
                        for q in range(4):
                            g = q % 2
                            ac.wait(pool, f"{q}W", it)
                            if q >= 2:
                                dv.wait(pool, f"{q - 2}s", it)
                            else:
                                dv.wait_before(pool, it)
                            po.did(pool.tensor_tensor(Wm[:, g], Wt[:, g], K["order"][:, None, :, 1, :].to_broadcast([P, 2, 2, P]),
                                                      ALU.mult), f"{q}wm")
                    scan_iterations(pool, steps, body)


def mlstm_post_phase(nc, K, zc, hscan):
    HT, PT = K["HT"], K["PT"]
    with ExitStack() as ctx:
        h2 = sbuf(ctx, nc, "h_fwd_bwd", [P, 2, 2, D])
        og = sbuf(ctx, nc, "o_gate", [P, 2, H_C, P])
        sq = sbuf(ctx, nc, "h_sq", [P, D])
        ss = sbuf(ctx, nc, "h_sum", [P, H_C])
        eps = sbuf(ctx, nc, "h_eps", [P, 1])
        ps = psum(ctx, nc, "hpost_ps", [P, 2, D])
        with phase(nc, "in0", "in1", "dve", "act", "pe", "eps_set") as s:
            dv = Steps(s["dve"], ["h", "ss", "hn", "out"])
            ac = Steps(s["act"], ["sig", "sq", "ln", "rs"])
            pe_ = Steps(s["pe"], ["t"])
            loaded = [s["in0"], s["in1"]]
            o_src = zc[16:24].rearrange("m p (c t) -> c p m t", t=P)

            def all_chunks(eng, tile):
                with eng.Fori(0, NCH // 2) as j:
                    for k in range(2):
                        tile(2 * j + k, j, k)
                tile(NCH - 1, NCH // 2, 0)
            with nc.Block() as block:
                @block.sync
                def _(sp):
                    def tile(c, k):
                        sp.dma_start(h2[:, k, 0, :], hscan[0, c]).then_inc(loaded[k], 16)
                        sp.dma_start(h2[:, k, 1, :], hscan[1, c]).then_inc(loaded[k], 16)
                        sp.dma_start(og[:, k], o_src[c]).then_inc(loaded[k], 16)
                    tile(0, 0)
                    tile(1, 1)
                    with sp.Fori(1, NCH // 2) as j:
                        early(sp, hscan[0, 2 * j], hscan[1, 2 * j], o_src[2 * j], hscan[0, 2 * j + 1], hscan[1, 2 * j + 1],
                              o_src[2 * j + 1])
                        for k in range(2):
                            dv.wait(sp, "out", 2 * j - 2 + k)
                            tile(2 * j + k, k)
                    dv.wait(sp, "out", NCH - 3)
                    tile(NCH - 1, 0)

                @block.tensor
                def _(pe):
                    def tile(it, j, k):
                        dv.wait(pe, "hn", it)
                        for h in range(H_C):
                            mm = pe.transpose(ps[:, k, h * P:h * P + P], h2[:, k, 0, h * P:h * P + P], K["ident"][:])
                        pe_.did(mm, "t")
                    all_chunks(pe, tile)

                @block.scalar
                def _(act):
                    act.wait_ge(s["eps_set"], 1)

                    def tile(it, j, k):
                        act.wait_ge(loaded[k], j * 48 + 48)
                        ac.did(act.activation(og[:, k], og[:, k], ACT.Sigmoid), "sig")
                        dv.wait(act, "h", it)
                        ac.did(act.activation(sq[:], h2[:, k, 0, :], ACT.Square), "sq")
                        dv.wait(act, "ss", it)
                        ac.did(act.activation(ss[:], ss[:], ACT.Ln, scale=1.0 / DV_C, bias=eps[:]), "ln")
                        ac.wait(act, "ln", it)
                        ac.did(act.activation(ss[:], ss[:], ACT.Exp, scale=-0.5), "rs")
                    all_chunks(act, tile)

                @block.vector
                def _(dve):
                    dve.memset(eps[:], RMS_EPS).then_inc(s["eps_set"], 1)

                    def tile(it, j, k):
                        h, hb = h2[:, k, 0, :], h2[:, k, 1, :]
                        dve.wait_ge(loaded[k], j * 48 + 48)
                        dv.did(dve.tensor_tensor(h, h, hb, ALU.add), "h")
                        ac.wait(dve, "sq", it)
                        dv.did(dve.tensor_reduce(ss[:], sq[:].rearrange("p (h v) -> p h v", h=H_C), AX_X, ALU.add), "ss")
                        ac.wait(dve, "rs", it)
                        dv.did(dve.tensor_tensor(h.rearrange("p (h v) -> p h v", h=H_C), h.rearrange("p (h v) -> p h v", h=H_C),
                                                 ss[:, :, None].to_broadcast([P, H_C, P]), ALU.mult), "hn")
                        pe_.wait(dve, "t", it)
                        x = slice(it * P, it * P + P) if isinstance(it, int) else bass.ds(it * P, P)
                        dv.did(dve.scalar_tensor_tensor(out=HT[:, :, x], in0=ps[:, k, :].rearrange("p (h t) -> p h t", h=H_C),
                                                        scalar=PT[:, C_MLN:C_MLN + 1], in1=og[:, k], op0=ALU.mult,
                                                        op1=ALU.mult), "out")
                    all_chunks(dve, tile)


def trunk_kernel(nc, A, y_prompt, y_sample, rk_out, gd_out, mc_out, mn_out, mm_out):
    def scratch(name, *shape):
        return nc.dram_tensor(name, list(shape), F32).ap()

    zc = scratch("z_even", AB_T, P, T)
    ztail = scratch("z_even_gates", 16, T)
    units = scratch("rwkv_units", 4, 2, P, NCH, 4, P)
    bonus = scratch("rwkv_bonus", 4, P, T)
    yscan = scratch("rwkv_y", 2, 4, P, T)
    qkv = scratch("gdn_units", 4, P, NCH, 3, P)
    oscan = scratch("gdn_o", 2, 4, P, T)
    zc2 = scratch("z_odd", ML_T, P, T)
    ztail2 = scratch("z_odd_gates", 32, T)
    hscan = scratch("mlstm_h", 2, NCH, P, D)

    with ExitStack() as ctx:
        def keep(name, *shape):
            return sbuf(ctx, nc, name, list(shape))
        K = {
            "ident": keep("ident", P, P), "ones": keep("ones", P, P),
            "order": keep("order", P, 2, 2, P),
            "sel": keep("sel", 8, 8, P), "selpair": keep("selpair", 8, 4, P),
            "PT": keep("PT", P, PT_COLS), "taps": keep("taps", P, AB_T, 3), "cond": keep("cond", P, KD, 2),
            "mod": keep("mod", P, 2, 6, KD, 2), "gain": keep("gain", P, 2, 2, KD, 2),
            "XT": keep("XT", P, KD, T),
        }
        even = ctx.enter_context(ExitStack())
        K["pairs"] = sbuf(even, nc, "pairs", [P, NL, 2, P])
        K["ones64"] = sbuf(even, nc, "ones64", [P, P])
        with ExitStack() as c:
            K["AH"] = sbuf(c, nc, "ada_head_w", [P, KD, ADA_HEAD])
            setup_phase(nc, A, K)
            adaln_phase(nc, A, K)

        def shift(layer, w):
            return K["mod"][:, layer, 3 * w]

        def gate(layer, w):
            return K["mod"][:, layer, 3 * w + 2]

        with ExitStack() as c:
            K["HU"], K["HL"] = [sbuf(c, nc, n, [P, KD, T]) for n in ("HU", "HL")]
            mixer_in_phase(nc, K, K["gain"][:, 0, 0], shift(0, 0), A["ab_w_in"][0], AB_T, 16, zc, ztail, K["taps"][:])
        with ExitStack() as mixer:
            K["HT"] = sbuf(mixer, nc, "HT", [P, KD, T])
            with ExitStack() as c:
                K["EM"] = sbuf(c, nc, "EM", [P, 2, NCH, 4])
                K["GR"] = sbuf(c, nc, "GR", [H_B, 2, T])
                K["GC"] = sbuf(c, nc, "GC", [P, NCH, 3, 2, H_B])
                rwkv_prep_phase(nc, A, K, zc, units, bonus)
                gdn_prep_phase(nc, A, K, zc, ztail, qkv)
                rk_state = sbuf(c, nc, "rk_state", [P, 4, 2, 64])
                gd_state = sbuf(c, nc, "gd_state", [P, 2, 2, 2, P])
                zero_states_phase(nc, [rk_state[:], gd_state[:]])
                rwkv_scan_phase(nc, K, units, zc, yscan, 1, rk_state)
                gdn_scan_phase(nc, K, qkv, oscan, 1, gd_state)
                with ExitStack() as t:
                    outs, ins = even_states(nc, t, A, rk_out, gd_out, rk_state, gd_state)
                    turn_states_phase(nc, K, outs, ins)
                rwkv_scan_phase(nc, K, units, zc, yscan, NCH - 1, rk_state)
                gdn_scan_phase(nc, K, qkv, oscan, NCH - 1, gd_state)
            rwkv_post_phase(nc, A, K, zc, yscan, bonus)
            gdn_post_phase(nc, K, zc, oscan)
            add_out_phase(nc, K, A["ab_w_out"][0], gate(0, 0))
        even.close()
        for layer in range(2):
            if layer == 1:
                with ExitStack() as c:
                    K["HU"], K["HL"] = [sbuf(c, nc, n, [P, KD, T]) for n in ("HU", "HL")]
                    mixer_in_phase(nc, K, K["gain"][:, 1, 0], shift(1, 0), A["ml_w_in"][0], ML_T, 32, zc2, ztail2, None)
                with ExitStack() as mixer:
                    K["HT"] = sbuf(mixer, nc, "HT", [P, KD, T])
                    with ExitStack() as c:
                        K["MN"] = sbuf(c, nc, "MN", [H_C, 2, T])
                        K["MC"] = sbuf(c, nc, "MC", [P, NCH, 3, 2, H_C])
                        K["WE"] = sbuf(c, nc, "WE", [P, 4, 2, NCH])
                        ml_state = sbuf(c, nc, "ml_state", [P, 4, 2, V1])
                        mlstm_prep_phase(nc, A, K, ztail2, mm_out)
                        zero_states_phase(nc, [ml_state[:]])
                        mlstm_scan_phase(nc, K, zc2, hscan, 1, ml_state)
                        with ExitStack() as t:
                            outs, ins = odd_states(nc, t, A, mc_out, mn_out, ml_state)
                            turn_states_phase(nc, K, outs, ins)
                        mlstm_scan_phase(nc, K, zc2, hscan, NCH - 1, ml_state)
                    mlstm_post_phase(nc, K, zc2, hscan)
                    add_out_phase(nc, K, A["ml_w_out"][0], gate(1, 0))
            with ExitStack() as ffn:
                K["HU"], K["HL"] = [sbuf(ffn, nc, n, [P, KD, T]) for n in ("HU", "HL")]
                ffn_phase(nc, A, K, layer, K["gain"][:, layer, 1], shift(layer, 1), gate(layer, 1))
        K["HT"] = keep("HT", P, KD, T)
        fin = K["PT"][:, C_FIN:C_FIN + KD, None].to_broadcast([P, KD, 2])
        final_norm_phase(nc, K, K["HT"], fin)
        store_out_phase(nc, K, y_prompt, y_sample)


_INS = ["x_prompt", "x_sample", "state_rwkv", "state_gdn", "state_mlstm_c", "state_mlstm_n", "state_mlstm_m", "c", "c_ctx",
        "ada_w", "ada_b", "norm1_g", "norm2_g", "ab_w_in", "ab_w_out", "rk_mu", "rk_w0", "rk_w_up", "rk_a0", "rk_a_up",
        "rk_g_up", "rk_k_k", "rk_k_a", "rk_r_k", "rk_ln_g", "rk_ln_b", "gd_conv_w", "gd_a_log", "gd_dt_bias", "gd_norm_g",
        "ml_w_in", "ml_gate_b", "ml_norm_g", "ml_w_out", "ffn_w_in", "ffn_conv_w", "ffn_conv_b", "ffn_w_out", "final_g"]
_OUTS = [(1, CTX, D), (1, LAT, D), (1, 1, 2, H_A, HD_A, HD_A), (1, 1, 2, H_B, HD_B, HD_B), (1, 1, 2, H_C, DV_C, DK_C),
         (1, 1, 2, H_C, DK_C), (1, 1, 2, H_C)]


def kernel(**inputs):
    import numpy as _np
    import concourse.bacc as _bacc
    from concourse.bass_utils import run_bass_kernel_spmd as _run

    nc = _bacc.Bacc("TRN2", target_bir_lowering=False, num_devices=1)
    arrays, A = {}, {}
    for name in _INS:
        a = _np.ascontiguousarray(inputs[name])
        arrays[f"in_{name}_dram"] = a
        A[name] = nc.dram_tensor(f"in_{name}_dram", a.shape, F32, kind="ExternalInput").ap()
    outs = [nc.dram_tensor(f"out_{i}_dram", shape, F32, kind="ExternalOutput").ap() for i, shape in enumerate(_OUTS)]
    trunk_kernel(nc, A, *outs)
    r = _run(nc, [arrays], core_ids=[0])
    return tuple(r.results[0][f"out_{i}_dram"] for i in range(len(_OUTS)))
```
